# Optimizing a Trainium2 kernel written in Bass

```python
import math
import jax, jax.numpy as jnp
from jax import lax
import numpy as np
import jax
import jax.numpy as jnp

D_MODEL = 1024
BATCH = 1
SEQ = 256
DEPTH = 1

GLA_HEADS = 4
GLA_DK = D_MODEL // 8
GLA_DV = D_MODEL // 4
GLA_GATE_RANK = 16
GLA_GATE_TAU = 16.0
GLA_CHUNK = 64
GDN_HEADS = 8
GDN_DK = D_MODEL // 8
GDN_DV = D_MODEL // 8
GDN_CONV = 5
GDN_CHUNK = 64
N_GROUPS = 4
EXPERTS_PER_GROUP = 8
N_EXPERTS = N_GROUPS * EXPERTS_PER_GROUP
TOP_K = 2
D_EXPERT = D_MODEL // 4
MOE_BLOCK = 128
EPS = 1e-6

GLA_QK = GLA_HEADS * GLA_DK
GLA_V = GLA_HEADS * GLA_DV
GDN_QK = GDN_HEADS * GDN_DK
GDN_V = GDN_HEADS * GDN_DV
IN_SPLITS = (
    GLA_QK, GLA_QK, GLA_V, GLA_V,
    GLA_GATE_RANK, GLA_GATE_RANK,
    GDN_QK, GDN_QK, GDN_V, GDN_V,
    4 * GDN_HEADS,
    D_MODEL, D_MODEL,
)
D_IN = sum(IN_SPLITS)


def rms_norm(x, w):
    xf = x.astype(jnp.float32)
    y = xf * lax.rsqrt(jnp.mean(xf * xf, axis=-1, keepdims=True) + EPS)
    return (y * w.astype(jnp.float32)).astype(x.dtype)

def l2_norm(t):
    return t * lax.rsqrt(jnp.sum(t * t, axis=-1, keepdims=True) + EPS)

def to_heads(t, n_heads):
    b, l, _ = t.shape
    return t.reshape(b, l, n_heads, -1).transpose(0, 2, 1, 3)

def from_heads(t):
    b, h, l, d = t.shape
    return t.transpose(0, 2, 1, 3).reshape(b, l, h * d)

def rev(t):
    return jnp.flip(t, axis=2)

def gla_chunked(q, k, v, log_a):
    b_, h_, l_, dk = q.shape
    dv = v.shape[-1]
    c = GLA_CHUNK
    n = l_ // c
    q, k, log_a = (t.reshape(b_, h_, n, c, dk) for t in (q, k, log_a))
    v = v.reshape(b_, h_, n, c, dv)
    cum = jnp.cumsum(log_a, axis=3)
    cum_last = cum[:, :, :, -1:, :]
    q_dec = q * jnp.exp(cum)
    k_inv = k * jnp.exp(-cum)
    causal = jnp.tril(jnp.ones((c, c), dtype=bool))
    scores = jnp.where(causal, jnp.einsum('bhntd,bhnsd->bhnts', q_dec, k_inv), 0.0)
    o_intra = jnp.einsum('bhnts,bhnsv->bhntv', scores, v)
    k_tail = k * jnp.exp(cum_last - cum)
    chunk_kv = jnp.einsum('bhnsd,bhnsv->bhndv', k_tail, v)
    chunk_decay = jnp.exp(cum_last[:, :, :, 0, :])

    def step(state, inp):
        kv, dec = inp
        return dec[..., None] * state + kv, state

    _, states = lax.scan(step, jnp.zeros((b_, h_, dk, dv), q.dtype),
                         (jnp.moveaxis(chunk_kv, 2, 0), jnp.moveaxis(chunk_decay, 2, 0)))
    states = jnp.moveaxis(states, 0, 2)
    o_inter = jnp.einsum('bhntd,bhndv->bhntv', q_dec, states)
    return (o_intra + o_inter).reshape(b_, h_, l_, dv)

def gdn_chunked(q, k, v, g, beta):
    b_, h_, l_, dk = q.shape
    dv = v.shape[-1]
    c = GDN_CHUNK
    n = l_ // c
    q, k = (t.reshape(b_, h_, n, c, dk) for t in (q, k))
    v = v.reshape(b_, h_, n, c, dv)
    g = jnp.cumsum(g.reshape(b_, h_, n, c), axis=-1)
    beta = beta.reshape(b_, h_, n, c)
    tri = jnp.tril(jnp.ones((c, c), dtype=bool))
    strict = jnp.tril(jnp.ones((c, c), dtype=bool), -1)
    diff = g[..., :, None] - g[..., None, :]
    decay = jnp.where(tri, jnp.exp(jnp.where(tri, diff, 0.0)), 0.0)
    k_beta = k * beta[..., None]
    v_beta = v * beta[..., None]
    lower = jnp.where(strict, jnp.einsum('bhntd,bhnsd->bhnts', k_beta, k) * decay, 0.0)
    unit_lower = lower + jnp.eye(c, dtype=q.dtype)
    u = lax.linalg.triangular_solve(unit_lower, v_beta, left_side=True, lower=True,
                                    unit_diagonal=True)
    w = lax.linalg.triangular_solve(unit_lower, k_beta * jnp.exp(g)[..., None],
                                    left_side=True, lower=True, unit_diagonal=True)
    attn = jnp.where(tri, jnp.einsum('bhntd,bhnsd->bhnts', q, k) * decay, 0.0)
    g_last = g[..., -1]
    k_tail = k * jnp.exp(g_last[..., None] - g)[..., None]
    q_dec = q * jnp.exp(g)[..., None]
    chunk_decay = jnp.exp(g_last)

    def step(state, inp):
        q_c, k_c, u_c, w_c, a_c, dec_c = inp
        v_new = u_c - jnp.einsum('bhtd,bhdv->bhtv', w_c, state)
        o = (jnp.einsum('bhtd,bhdv->bhtv', q_c, state)
             + jnp.einsum('bhts,bhsv->bhtv', a_c, v_new))
        state = dec_c[..., None, None] * state + jnp.einsum('bhsd,bhsv->bhdv', k_c, v_new)
        return state, o

    xs = tuple(jnp.moveaxis(t, 2, 0) for t in (q_dec, k_tail, u, w, attn, chunk_decay))
    _, o = lax.scan(step, jnp.zeros((b_, h_, dk, dv), q.dtype), xs)
    return jnp.moveaxis(o, 0, 2).reshape(b_, h_, l_, dv)

def centred_depthwise_conv(x, w):
    kw, ch = w.shape
    pad = kw // 2
    return lax.conv_general_dilated(
        x, w[:, None, :].astype(x.dtype), window_strides=(1,), padding=[(pad, pad)],
        dimension_numbers=('NWC', 'WIO', 'NWC'), feature_group_count=ch)

def token_mixer(h, w_in, gla_w2_f, gla_b_f, gla_w2_b, gla_b_b, gla_norm_w, conv_w,
                a_log_f, dt_bias_f, a_log_b, dt_bias_b, gdn_norm_w, w_out):
    f32 = jnp.float32
    points = [int(p) for p in np.cumsum(IN_SPLITS)[:-1]]
    proj = h @ w_in
    (gq, gk, gv, gr, glr_f, glr_b, dq, dk, dv, dz, dab, m_a, m_b) = jnp.split(proj, points, axis=-1)

    q = to_heads(gq.astype(f32), GLA_HEADS) * (GLA_DK ** -0.5)
    k = to_heads(gk.astype(f32), GLA_HEADS)
    v = to_heads(gv.astype(f32), GLA_HEADS)
    la_f = to_heads(jax.nn.log_sigmoid((glr_f @ gla_w2_f + gla_b_f).astype(f32)) / GLA_GATE_TAU, GLA_HEADS)
    la_b = to_heads(jax.nn.log_sigmoid((glr_b @ gla_w2_b + gla_b_b).astype(f32)) / GLA_GATE_TAU, GLA_HEADS)
    o = gla_chunked(q, k, v, la_f) + rev(gla_chunked(rev(q), rev(k), rev(v), rev(la_b)))
    o_a = from_heads(rms_norm(o, gla_norm_w)) * jax.nn.silu(gr.astype(f32))

    qkv = jax.nn.silu(centred_depthwise_conv(jnp.concatenate([dq, dk, dv], axis=-1), conv_w))
    cq, ck, cv = jnp.split(qkv.astype(f32), [GDN_QK, 2 * GDN_QK], axis=-1)
    q = l2_norm(to_heads(cq, GDN_HEADS)) * (GDN_DK ** -0.5)
    k = l2_norm(to_heads(ck, GDN_HEADS))
    v = to_heads(cv, GDN_HEADS)
    a_f, a_b, b_f, b_b = (t.transpose(0, 2, 1) for t in jnp.split(dab.astype(f32), 4, axis=-1))
    g_f = -jnp.exp(a_log_f.astype(f32))[None, :, None] * jax.nn.softplus(a_f + dt_bias_f.astype(f32)[None, :, None])
    g_b = -jnp.exp(a_log_b.astype(f32))[None, :, None] * jax.nn.softplus(a_b + dt_bias_b.astype(f32)[None, :, None])
    beta_f = jax.nn.sigmoid(b_f)
    beta_b = jax.nn.sigmoid(b_b)
    o = (gdn_chunked(q, k, v, g_f, beta_f)
         + rev(gdn_chunked(rev(q), rev(k), rev(v), rev(g_b), rev(beta_b))))
    o_b = from_heads(rms_norm(o, gdn_norm_w)) * jax.nn.silu(dz.astype(f32))

    mixed = jax.nn.sigmoid(m_a.astype(f32)) * o_a + jax.nn.sigmoid(m_b.astype(f32)) * o_b
    return mixed.astype(h.dtype) @ w_out

def hierarchical_moe(h, w_group, w_router, w_gate, w_up, w_down):
    f32 = jnp.float32
    b_, l_, d = h.shape
    n_tok = b_ * l_
    t = h.reshape(n_tok, d)
    group_logits = (t @ w_group).astype(f32)
    group_prob = jax.nn.softmax(group_logits, axis=-1)
    group_idx = jnp.argmax(group_logits, axis=-1).astype(jnp.int32)
    group_w = jnp.take_along_axis(group_prob, group_idx[:, None], axis=-1)
    exp_logits = (t @ w_router).astype(f32).reshape(n_tok, N_GROUPS, EXPERTS_PER_GROUP)
    exp_logits = jnp.take_along_axis(exp_logits, group_idx[:, None, None], axis=1)[:, 0]
    top_p, top_i = lax.top_k(jax.nn.softmax(exp_logits, axis=-1), TOP_K)
    weights = group_w * top_p / jnp.sum(top_p, axis=-1, keepdims=True)
    expert_id = group_idx[:, None] * EXPERTS_PER_GROUP + top_i.astype(jnp.int32)

    n_assign = n_tok * TOP_K
    flat_e = expert_id.reshape(n_assign)
    flat_tok = jnp.repeat(jnp.arange(n_tok, dtype=jnp.int32), TOP_K)
    flat_w = weights.reshape(n_assign)
    order = jnp.argsort(flat_e)
    sorted_e = flat_e[order]
    counts = jnp.bincount(flat_e, length=N_EXPERTS)
    padded = (counts + MOE_BLOCK - 1) // MOE_BLOCK * MOE_BLOCK
    start = jnp.cumsum(counts) - counts
    ends = jnp.cumsum(padded)
    pstart = ends - padded
    dest = pstart[sorted_e] + jnp.arange(n_assign, dtype=jnp.int32) - start[sorted_e]
    n_blocks = -(-(n_assign + N_EXPERTS * (MOE_BLOCK - 1)) // MOE_BLOCK)
    n_rows = n_blocks * MOE_BLOCK
    row_tok = jnp.full((n_rows,), n_tok, jnp.int32).at[dest].set(flat_tok[order])
    row_w = jnp.zeros((n_rows,), f32).at[dest].set(flat_w[order])
    block_expert = jnp.minimum(
        jnp.searchsorted(ends, jnp.arange(n_blocks, dtype=jnp.int32) * MOE_BLOCK, side='right'),
        N_EXPERTS - 1)
    t_pad = jnp.concatenate([t, jnp.zeros((1, d), t.dtype)], axis=0)
    xb = t_pad[row_tok].reshape(n_blocks, MOE_BLOCK, d)

    def expert_block(args):
        xs, e = args
        hid = jax.nn.silu(xs @ w_gate[e]) * (xs @ w_up[e])
        return hid @ w_down[e]

    yb = lax.map(expert_block, (xb, block_expert)).reshape(n_rows, d)
    out = jnp.zeros((n_tok + 1, d), f32).at[row_tok].add(yb.astype(f32) * row_w[:, None])[:n_tok]
    return out.astype(h.dtype).reshape(b_, l_, d)

def first_inputs(seed: int = 0) -> dict:
    key = jax.random.key(seed)
    ks = jax.random.split(key, 24)
    f32 = jnp.float32
    nl = DEPTH

    def nrm(k, shape, fan_in):
        return jax.random.normal(k, shape, f32) * (fan_in ** -0.5)

    def gain(k, shape):
        return 1.0 + 0.02 * jax.random.normal(k, shape, f32)

    def dt_bias(k):
        dt = jnp.exp(jax.random.uniform(k, (nl, GDN_HEADS), f32, math.log(1e-3), math.log(1e-1)))
        return dt + jnp.log(-jnp.expm1(-dt))

    def a_log(k):
        return jnp.log(jax.random.uniform(k, (nl, GDN_HEADS), f32, 1.0, 16.0))

    return {
        'x': jax.random.normal(ks[0], (BATCH, SEQ, D_MODEL), f32),
        'norm1_w': gain(ks[1], (nl, D_MODEL)),
        'w_in': nrm(ks[2], (nl, D_MODEL, D_IN), D_MODEL),
        'gla_gate_w2_fwd': nrm(ks[3], (nl, GLA_GATE_RANK, GLA_QK), GLA_GATE_RANK),
        'gla_gate_b_fwd': 0.1 * jax.random.normal(ks[4], (nl, GLA_QK), f32),
        'gla_gate_w2_bwd': nrm(ks[5], (nl, GLA_GATE_RANK, GLA_QK), GLA_GATE_RANK),
        'gla_gate_b_bwd': 0.1 * jax.random.normal(ks[6], (nl, GLA_QK), f32),
        'gla_norm_w': gain(ks[7], (nl, GLA_DV)),
        'gdn_conv_w': nrm(ks[8], (nl, GDN_CONV, 2 * GDN_QK + GDN_V), GDN_CONV),
        'gdn_a_log_fwd': a_log(ks[9]),
        'gdn_dt_bias_fwd': dt_bias(ks[10]),
        'gdn_a_log_bwd': a_log(ks[11]),
        'gdn_dt_bias_bwd': dt_bias(ks[12]),
        'gdn_norm_w': gain(ks[13], (nl, GDN_DV)),
        'w_out': nrm(ks[14], (nl, D_MODEL, D_MODEL), D_MODEL),
        'norm2_w': gain(ks[15], (nl, D_MODEL)),
        'moe_w_group': nrm(ks[16], (nl, D_MODEL, N_GROUPS), D_MODEL),
        'moe_w_router': nrm(ks[17], (nl, D_MODEL, N_EXPERTS), D_MODEL),
        'moe_w_gate': nrm(ks[18], (nl, N_EXPERTS, D_MODEL, D_EXPERT), D_MODEL),
        'moe_w_up': nrm(ks[19], (nl, N_EXPERTS, D_MODEL, D_EXPERT), D_MODEL),
        'moe_w_down': nrm(ks[20], (nl, N_EXPERTS, D_EXPERT, D_MODEL), D_EXPERT),
        'norm_f_w': gain(ks[21], (D_MODEL,)),
    }

def first_block(x, norm1_w, w_in, gla_gate_w2_fwd, gla_gate_b_fwd, gla_gate_w2_bwd, gla_gate_b_bwd,
              gla_norm_w, gdn_conv_w, gdn_a_log_fwd, gdn_dt_bias_fwd, gdn_a_log_bwd, gdn_dt_bias_bwd,
              gdn_norm_w, w_out, norm2_w, moe_w_group, moe_w_router, moe_w_gate, moe_w_up,
              moe_w_down, norm_f_w):
    for i in range(DEPTH):
        h = rms_norm(x, norm1_w[i])
        x = x + token_mixer(h, w_in[i], gla_gate_w2_fwd[i], gla_gate_b_fwd[i], gla_gate_w2_bwd[i],
                            gla_gate_b_bwd[i], gla_norm_w[i], gdn_conv_w[i], gdn_a_log_fwd[i],
                            gdn_dt_bias_fwd[i], gdn_a_log_bwd[i], gdn_dt_bias_bwd[i], gdn_norm_w[i],
                            w_out[i])
        h = rms_norm(x, norm2_w[i])
        x = x + hierarchical_moe(h, moe_w_group[i], moe_w_router[i], moe_w_gate[i], moe_w_up[i],
                                 moe_w_down[i])
    return rms_norm(x, norm_f_w)


DEPTH_2 = 2

RET_HEADS = 4
RET_HEAD_DIM = D_MODEL // 2 // RET_HEADS
RET_VALUE_DIM = D_MODEL // 2 // RET_HEADS
RET_CHUNK = 128
RET_WIDTH = RET_HEADS * RET_VALUE_DIM
WIN_Q_HEADS = 8
WIN_KV_HEADS = 2
WIN_HEAD_DIM = D_MODEL // 2 // WIN_Q_HEADS
WINDOW = 128
WIN_BLOCK = WINDOW
WIN_WIDTH = WIN_Q_HEADS * WIN_HEAD_DIM
FOURIER_GROUPS = 4
ROPE_THETA = 10000.0
N_EXPERTS_2 = N_GROUPS * EXPERTS_PER_GROUP
EXPERT_HIDDEN = D_MODEL // 2
LN_EPS = 1e-5
GN_EPS = 1e-6
DEEPNORM_ALPHA = (2.0 * DEPTH_2) ** 0.25
DEEPNORM_BETA = (8.0 * DEPTH_2) ** -0.25
N_EVEN = (DEPTH_2 + 1) // 2
N_ODD = DEPTH_2 // 2
RET_QK = RET_HEADS * RET_HEAD_DIM
WIN_KV = WIN_KV_HEADS * WIN_HEAD_DIM
EVEN_SPLITS = tuple(np.cumsum([RET_QK, RET_QK, RET_WIDTH, RET_WIDTH, WIN_WIDTH, WIN_KV])[:].tolist())
IN_EVEN = 2 * RET_QK + 2 * RET_WIDTH + WIN_WIDTH + 2 * WIN_KV


def layer_norm(x, gain, bias):
    xf = x.astype(jnp.float32)
    mu = jnp.mean(xf, axis=-1, keepdims=True)
    var = jnp.mean(jnp.square(xf - mu), axis=-1, keepdims=True)
    y = (xf - mu) * lax.rsqrt(var + LN_EPS) * gain.astype(jnp.float32) + bias.astype(jnp.float32)
    return y.astype(x.dtype)

def rope(x, pos):
    d = x.shape[-1]
    half = d // 2
    inv = ROPE_THETA ** (-jnp.arange(half, dtype=jnp.float32) / half)
    ang = pos.astype(jnp.float32)[:, None] * inv[None, :]
    cos = jnp.cos(ang)[None, :, None, :]
    sin = jnp.sin(ang)[None, :, None, :]
    xf = x.astype(jnp.float32)
    x1, x2 = xf[..., :half], xf[..., half:]
    return jnp.concatenate([x1 * cos - x2 * sin, x1 * sin + x2 * cos], axis=-1).astype(x.dtype)

def retention_one_direction(q, k, v, log_gamma, include_diag):
    B, H, S, dk = q.shape
    dv = v.shape[-1]
    C = RET_CHUNK
    NC = S // C
    qc = q.reshape(B, H, NC, C, dk)
    kc = k.reshape(B, H, NC, C, dk)
    vc = v.reshape(B, H, NC, C, dv)
    pos = jnp.arange(C, dtype=jnp.float32)
    lg = log_gamma[:, None, None]
    diff = pos[:, None] - pos[None, :]
    mask = diff >= 0 if include_diag else diff > 0
    dmat = jnp.where(mask[None], jnp.exp(lg * jnp.maximum(diff, 0.0)[None]), 0.0)
    scores = jnp.einsum('bhncd,bhnmd->bhncm', qc, kc) * dmat[None, :, None]
    y_inner = jnp.einsum('bhncm,bhnmv->bhncv', scores, vc)
    zeta = jnp.exp(log_gamma[:, None] * (C - 1.0 - pos)[None])
    kv = jnp.einsum('bhnmd,bhnmv->nbhdv', kc * zeta[None, :, None, :, None], vc)
    chunk_decay = jnp.exp(log_gamma * C)[None, :, None, None]

    def step(state, kv_n):
        return state * chunk_decay + kv_n, state

    _, r_prev = lax.scan(step, jnp.zeros((B, H, dk, dv), jnp.float32), kv)
    xi = jnp.exp(log_gamma[:, None] * (pos + 1.0)[None])
    y_cross = jnp.einsum('bhncd,nbhdv->bhncv', qc * xi[None, :, None, :, None], r_prev)
    return (y_inner + y_cross).reshape(B, H, S, dv)

def bidirectional_retention(q, k, v, decay_logit):
    qf = jnp.transpose(q.astype(jnp.float32), (0, 2, 1, 3))
    kf = jnp.transpose(k.astype(jnp.float32), (0, 2, 1, 3))
    vf = jnp.transpose(v.astype(jnp.float32), (0, 2, 1, 3))
    log_gamma = jax.nn.log_sigmoid(decay_logit.astype(jnp.float32))
    fwd = retention_one_direction(qf, kf, vf, log_gamma[0], True)
    bwd = jnp.flip(retention_one_direction(jnp.flip(qf, 2), jnp.flip(kf, 2), jnp.flip(vf, 2),
                                           log_gamma[1], False), 2)
    return jnp.transpose(fwd + bwd, (0, 2, 1, 3))

def banded_keys(t):
    B, S, Hkv, d = t.shape
    NB = S // WIN_BLOCK
    tp = jnp.pad(t, ((0, 0), (WINDOW, WINDOW), (0, 0), (0, 0))).reshape(B, NB + 2, WIN_BLOCK, Hkv, d)
    return jnp.concatenate([tp[:, :-2], tp[:, 1:-1], tp[:, 2:]], axis=2)

def window_attention_with_sink(q, k, v, sink_logit):
    B, S, Hq, d = q.shape
    Hkv = k.shape[2]
    G = Hq // Hkv
    NB = S // WIN_BLOCK
    qb = q.reshape(B, NB, WIN_BLOCK, Hkv, G, d)
    kb = banded_keys(k)
    vb = banded_keys(v)
    s = jnp.einsum('bnqhgd,bnkhd->bnhgqk', qb, kb).astype(jnp.float32)
    i = jnp.arange(WIN_BLOCK)[:, None]
    j = jnp.arange(3 * WIN_BLOCK)[None, :]
    rel_ok = jnp.abs(i - j + WINDOW) <= WINDOW
    kpos = jnp.arange(NB)[:, None] * WIN_BLOCK + jnp.arange(3 * WIN_BLOCK)[None, :] - WINDOW
    in_ok = (kpos >= 0) & (kpos < S)
    mask = rel_ok[None] & in_ok[:, None, :]
    s = jnp.where(mask[None, :, None, None], s, -1e30)
    sink = jnp.broadcast_to(sink_logit.astype(jnp.float32).reshape(1, 1, Hkv, G, 1, 1), s.shape[:-1] + (1,))
    p = jax.nn.softmax(jnp.concatenate([s, sink], axis=-1), axis=-1)[..., :-1]
    o = jnp.einsum('bnhgqk,bnkhd->bnqhgd', p.astype(v.dtype), vb)
    return o.reshape(B, S, Hq * d)

def even_mixer(x, w_in, decay_logit, gn_gain, sink_logit, w_out, pos):
    B, S, _ = x.shape
    h = x @ w_in
    qa, ka, va, ga, qb, kb, vb = jnp.split(h, EVEN_SPLITS, axis=-1)
    qa = rope(qa.reshape(B, S, RET_HEADS, RET_HEAD_DIM), pos)
    ka = rope(ka.reshape(B, S, RET_HEADS, RET_HEAD_DIM), pos) * (RET_HEAD_DIM ** -0.5)
    va = va.reshape(B, S, RET_HEADS, RET_VALUE_DIM)
    ya = bidirectional_retention(qa, ka, va, decay_logit)
    mu = jnp.mean(ya, axis=-1, keepdims=True)
    var = jnp.mean(jnp.square(ya - mu), axis=-1, keepdims=True)
    ya = ((ya - mu) * lax.rsqrt(var + GN_EPS)).reshape(B, S, RET_WIDTH) * gn_gain.astype(jnp.float32)
    ya = jax.nn.silu(ga) * ya.astype(x.dtype)
    qb = rope(qb.reshape(B, S, WIN_Q_HEADS, WIN_HEAD_DIM), pos) * (WIN_HEAD_DIM ** -0.5)
    kb = rope(kb.reshape(B, S, WIN_KV_HEADS, WIN_HEAD_DIM), pos)
    vb = vb.reshape(B, S, WIN_KV_HEADS, WIN_HEAD_DIM)
    yb = window_attention_with_sink(qb, kb, vb, sink_logit)
    return jnp.concatenate([ya, yb], axis=-1) @ w_out

def fourier_mixer(x, w_out):
    B, S, D = x.shape
    xg = x.astype(jnp.float32).reshape(B, S, FOURIER_GROUPS, D // FOURIER_GROUPS)
    y = jnp.fft.fft2(xg, axes=(1, 3), norm='ortho').real.reshape(B, S, D)
    return y.astype(x.dtype) @ w_out

def hierarchical_moe_2(x, w_coarse, b_coarse, w_fine, b_fine, w_gate, w_up, w_down):
    B, S, D = x.shape
    xt = x.reshape(B * S, D)
    T = B * S
    coarse = (xt @ w_coarse + b_coarse).astype(jnp.float32)
    p_group, g_idx = lax.top_k(jax.nn.softmax(coarse, axis=-1), 1)
    fine = (xt @ w_fine + b_fine).astype(jnp.float32).reshape(T, N_GROUPS, EXPERTS_PER_GROUP)
    fine_g = jnp.take_along_axis(fine, g_idx[:, :, None], axis=1)[:, 0]
    top_val, top_idx = lax.top_k(fine_g, TOP_K)
    gate = jax.nn.softmax(top_val, axis=-1) * p_group
    expert_id = (g_idx * EXPERTS_PER_GROUP + top_idx).reshape(-1)
    order = jnp.argsort(expert_id)
    tok = order // TOP_K
    sizes = jnp.bincount(expert_id, length=N_EXPERTS_2).astype(jnp.int32)
    xs = xt[tok]
    hid = jax.nn.silu(lax.ragged_dot(xs, w_gate, sizes)) * lax.ragged_dot(xs, w_up, sizes)
    ys = lax.ragged_dot(hid, w_down, sizes) * gate.reshape(-1)[order][:, None].astype(x.dtype)
    out = jax.ops.segment_sum(ys, tok, num_segments=T)
    return out.reshape(B, S, D)

def second_inputs(seed: int = 0) -> dict:
    key = jax.random.key(seed)
    ks = jax.random.split(key, 20)
    f32 = jnp.float32
    nrm = lambda k, shape: jax.random.normal(k, shape, f32)
    base_logit = jnp.log(2.0 ** (5.0 + jnp.arange(RET_HEADS, dtype=f32)) - 1.0)
    return {
        "x": nrm(ks[0], (BATCH, SEQ, D_MODEL)),
        "w_in_even": nrm(ks[1], (N_EVEN, D_MODEL, IN_EVEN)) * D_MODEL ** -0.5,
        "ret_decay_logit": base_logit[None, None, :] + 0.1 * nrm(ks[2], (N_EVEN, 2, RET_HEADS)),
        "ret_gn_gain": 1.0 + 0.02 * nrm(ks[3], (N_EVEN, RET_WIDTH)),
        "sink_logit": 0.5 * nrm(ks[4], (N_EVEN, WIN_Q_HEADS)),
        "w_out_even": nrm(ks[5], (N_EVEN, D_MODEL, D_MODEL)) * D_MODEL ** -0.5 * DEEPNORM_BETA,
        "w_out_fourier": nrm(ks[6], (N_ODD, D_MODEL, D_MODEL)) * D_MODEL ** -0.5 * DEEPNORM_BETA,
        "ln1_gain": 1.0 + 0.02 * nrm(ks[7], (DEPTH_2, D_MODEL)),
        "ln1_bias": 0.02 * nrm(ks[8], (DEPTH_2, D_MODEL)),
        "ln2_gain": 1.0 + 0.02 * nrm(ks[9], (DEPTH_2, D_MODEL)),
        "ln2_bias": 0.02 * nrm(ks[10], (DEPTH_2, D_MODEL)),
        "router_coarse_w": nrm(ks[11], (DEPTH_2, D_MODEL, N_GROUPS)) * D_MODEL ** -0.5,
        "router_coarse_b": 0.01 * nrm(ks[12], (DEPTH_2, N_GROUPS)),
        "router_fine_w": nrm(ks[13], (DEPTH_2, D_MODEL, N_EXPERTS_2)) * D_MODEL ** -0.5,
        "router_fine_b": 0.01 * nrm(ks[14], (DEPTH_2, N_EXPERTS_2)),
        "expert_w_gate": nrm(ks[15], (DEPTH_2, N_EXPERTS_2, D_MODEL, EXPERT_HIDDEN)) * D_MODEL ** -0.5,
        "expert_w_up": nrm(ks[16], (DEPTH_2, N_EXPERTS_2, D_MODEL, EXPERT_HIDDEN)) * D_MODEL ** -0.5,
        "expert_w_down": nrm(ks[17], (DEPTH_2, N_EXPERTS_2, EXPERT_HIDDEN, D_MODEL)) * EXPERT_HIDDEN ** -0.5 * DEEPNORM_BETA,
    }

def second_block(x, w_in_even, ret_decay_logit, ret_gn_gain, sink_logit, w_out_even, w_out_fourier,
              ln1_gain, ln1_bias, ln2_gain, ln2_bias, router_coarse_w, router_coarse_b,
              router_fine_w, router_fine_b, expert_w_gate, expert_w_up, expert_w_down):
    pos = jnp.arange(x.shape[1], dtype=jnp.int32)
    for layer in range(DEPTH_2):
        if layer % 2 == 0:
            e = layer // 2
            mix = even_mixer(x, w_in_even[e], ret_decay_logit[e], ret_gn_gain[e], sink_logit[e],
                             w_out_even[e], pos)
        else:
            mix = fourier_mixer(x, w_out_fourier[layer // 2])
        x = layer_norm(DEEPNORM_ALPHA * x + mix, ln1_gain[layer], ln1_bias[layer])
        ffn = hierarchical_moe_2(x, router_coarse_w[layer], router_coarse_b[layer], router_fine_w[layer],
                               router_fine_b[layer], expert_w_gate[layer], expert_w_up[layer],
                               expert_w_down[layer])
        x = layer_norm(DEEPNORM_ALPHA * x + ffn, ln2_gain[layer], ln2_bias[layer])
    return x


def setup_inputs(seed=0):
    out = dict(first_inputs(seed))
    for name, value in second_inputs(seed + 1).items():
        if name != "x":
            out[name + "_2"] = value
    return out


def reference(
    x, norm1_w, w_in, gla_gate_w2_fwd, gla_gate_b_fwd, gla_gate_w2_bwd, gla_gate_b_bwd,
    gla_norm_w, gdn_conv_w, gdn_a_log_fwd, gdn_dt_bias_fwd, gdn_a_log_bwd, gdn_dt_bias_bwd,
    gdn_norm_w, w_out, norm2_w, moe_w_group, moe_w_router, moe_w_gate, moe_w_up, moe_w_down,
    norm_f_w, w_in_even_2, ret_decay_logit_2, ret_gn_gain_2, sink_logit_2, w_out_even_2,
    w_out_fourier_2, ln1_gain_2, ln1_bias_2, ln2_gain_2, ln2_bias_2, router_coarse_w_2,
    router_coarse_b_2, router_fine_w_2, router_fine_b_2, expert_w_gate_2, expert_w_up_2,
    expert_w_down_2,
):
    x = first_block(
        x, norm1_w, w_in, gla_gate_w2_fwd, gla_gate_b_fwd, gla_gate_w2_bwd, gla_gate_b_bwd,
        gla_norm_w, gdn_conv_w, gdn_a_log_fwd, gdn_dt_bias_fwd, gdn_a_log_bwd, gdn_dt_bias_bwd,
        gdn_norm_w, w_out, norm2_w, moe_w_group, moe_w_router, moe_w_gate, moe_w_up, moe_w_down,
        norm_f_w,
    )
    return second_block(
        x, w_in_even_2, ret_decay_logit_2, ret_gn_gain_2, sink_logit_2, w_out_even_2,
        w_out_fourier_2, ln1_gain_2, ln1_bias_2, ln2_gain_2, ln2_bias_2, router_coarse_w_2,
        router_coarse_b_2, router_fine_w_2, router_fine_b_2, expert_w_gate_2, expert_w_up_2,
        expert_w_down_2,
    )


_drawn_inputs = setup_inputs


def setup_inputs(seed=0):
    import zlib

    import numpy as np

    out = dict(_drawn_inputs(seed))
    spreads = {}
    factors = {'gdn_norm_w': 3.006,
     'ret_gn_gain_2': 23.306,
     'sink_logit_2': 34.142,
     'router_coarse_b_2': 26.691,
     'router_fine_b_2': 7.804}
    for name, (base, spread) in spreads.items():
        noise = np.random.default_rng([zlib.crc32(name.encode()), seed]).standard_normal(out[name].shape)
        drawn = base * np.exp(spread * noise) if base else spread * noise
        out[name] = jnp.asarray(drawn.astype(out[name].dtype))
    for name, factor in factors.items():
        out[name] = (out[name] * factor).astype(out[name].dtype)
    return out
```

```python
from contextlib import ExitStack

import numpy as np

import concourse.bass as bass
from concourse import mybir

ALU = mybir.AluOpType
ACT = mybir.ActivationFunctionType
AX = mybir.AxisListType
F32 = mybir.dt.float32
I32 = mybir.dt.int32

P = 128
T = 256
NJ = T // P
D = 1024
KC = D // P
W = 512
EPS = 1e-6
CH = 64

GLA_H, GLA_DK, GLA_DV, RANK, TAU = 4, 128, 256, 16, 16.0
GDN_H, GDN_D, TAPS = 8, 128, 5
NG, NE, EPG = 4, 32, 8
H1, H2 = 256, 512
RET_H, WIN_H, WIN_KV, WIN_D = 4, 8, 2, 64
ALPHA = 4.0 ** 0.25
LN_EPS, GN_EPS = 1e-5, 1e-6
NT_BLOCKS, NN_BLOCKS = 8, 10
BIG = 1e30
CAP = 64


class Order:

    def __init__(self, eng, sem):
        self.eng, self.sem, self.n = eng, sem, 0

    def __call__(self, ins):
        self.n += 1
        ins.then_inc(self.sem, 1)
        self.eng.wait_ge(self.sem, self.n)

    def restart(self):
        self.eng.sem_clear(self.sem)
        self.n = 0


LEVELS = 6
TABLE = dict(ident=P, ones=P, cum=2 * P, blk=P, half=2 * P, strictn=2 * P, incl=2 * P,
             lev=LEVELS * 2 * P, lev0=2 * P, rank=NG + NE,
             before=P, slot=CAP)
OFF = {}
_at = 0
for _k, _n in TABLE.items():
    OFF[_k] = _at
    _at += _n
TABLE_N = _at


def tables():
    p = np.arange(P)[:, None]
    x = np.arange(P)[None, :]
    same = (p // CH) == (x // CH)
    f = lambda m: m.astype(np.float32)
    out = dict(
        ident=f(p == x), ones=np.ones((P, P), np.float32),
        cum=np.concatenate([f(same & (p <= x)), f(same & (p >= x))], 1),
        blk=f(same),
        half=np.concatenate([f((p < CH) & (x >= 0)), f((p >= CH) & (x >= 0))], 1),
        strictn=np.concatenate([-f(same & (x < p)), -f(same & (x > p))], 1),
        incl=np.concatenate([f(same & (p <= x)), f(same & (p >= x))], 1),
    )
    lev = []
    for l in range(LEVELS):
        pair = (p >> (l + 1)) == (x >> (l + 1))
        lev.append(f(pair & (((p >> l) & 1) == 0) & (((x >> l) & 1) == 1)))
        lev.append(f(pair & (((p >> l) & 1) == 1) & (((x >> l) & 1) == 0)))
    out["lev"] = np.concatenate(lev, 1)
    out["lev0"] = np.concatenate([lev[1], lev[0]], 1)
    out["rank"] = np.tile(np.concatenate([np.arange(NG, 0, -1), np.arange(NE, 0, -1)]).astype(np.float32), (P, 1))
    out["before"] = f(p < x)
    out["slot"] = np.tile(np.arange(CAP, dtype=np.float32), (P, 1))
    return np.ascontiguousarray(np.concatenate([out[k] for k in TABLE], 1))


def dft_table():
    t = np.arange(T)
    ang = 2 * np.pi * ((t[:, None] * t[None, :]) % T) / T
    both = np.stack([np.cos(ang), np.sin(ang)], 1).astype(np.float32)
    return np.ascontiguousarray(both.reshape(NJ, P, 2, T).transpose(1, 0, 2, 3))


ROPE_N = 2 * (64 + 32) * NJ


def even_tables():
    pos = np.arange(T, dtype=np.float32)
    parts = []
    for half in (64, 32):
        inv = np.float32(10000.0) ** (-np.arange(half, dtype=np.float32) / np.float32(half))
        ang = pos[:, None] * inv[None, :]
        for f in (np.cos, np.sin):
            parts.append(f(ang).astype(np.float32).reshape(NJ, P, half).transpose(1, 0, 2).reshape(P, -1))
    s, t = pos[:, None], pos[None, :]
    rows = lambda m: m.astype(np.float32).reshape(NJ, P, T).transpose(1, 0, 2).reshape(P, -1)
    parts += [rows(np.maximum(t - s, 0)), rows(np.maximum(s - t, 0)),
              rows(np.where(np.abs(s - t) <= P, 0.0, -BIG))]
    return np.ascontiguousarray(np.concatenate(parts, 1))


class Core:

    def __init__(self, nc, ins, out, ctx):
        self.nc, self.i, self.out, self.ctx = nc, ins, out, ctx
        self.live = None
        self.order = {e: self.sem(f"{e}_order") for e in ("dve", "act", "pool", "pe")}
        self.scope = ctx

    def sem(self, name):
        s = self.nc.alloc_semaphore(name=name)
        if self.live is not None:
            self.live.append(s)
        return s

    def retire(self):
        self.nc.all_engine_barrier()
        self.nc.clear_and_free_semaphores(self.live)
        self.nc.all_engine_barrier()
        self.live = []

    def sb(self, name, shape, dt=F32):
        return self.scope.enter_context(self.nc.sbuf_tensor(name, shape, dt))

    def ps(self, name, shape):
        return self.scope.enter_context(self.nc.psum_tensor(name, shape, F32))

    def table(self, name, n=0):
        a = OFF[name] + n * P
        return self.tab[:, a:a + P]


def bc(ap, axis, n):
    shape = list(ap.shape)
    return ap.unsqueeze(axis).broadcast_to(shape[:axis] + [n] + shape[axis:])


def refine(nc, o, r, v, tmp):
    o(nc.vector.tensor_tensor(tmp, r, r, ALU.mult))
    o(nc.vector.tensor_tensor(tmp, tmp, v, ALU.mult))
    o(nc.vector.tensor_scalar(tmp, tmp, -0.5, 1.5, ALU.mult, ALU.add))
    o(nc.vector.tensor_tensor(r, r, tmp, ALU.mult))


def stage_load(k):
    nc, i = k.nc, k.i
    k.tab = k.sb("tables", [P, TABLE_N])
    k.x = k.sb("x", [P, NJ, D])
    k.hT = k.sb("hT", [P, KC, T])
    k.s_small = k.sem("small_loaded")
    with nc.Block() as block:
        @block.sync
        def _(sp):
            sp.dma_start(k.x[:], i["x"].rearrange("a (j p) d -> p (a j) d", p=P)).then_inc(k.s_small, 16)
            sp.dma_start(k.tab[:], i["tables"]).then_inc(k.s_small, 16)
            sp.wait_ge(k.s_small, 32)


def stage_norm_t(k, tag, src, weight, hn):
    nc = k.nc
    s_w, s_ss, s_inv, s_rs, s_h, s_t = (k.sem(f"{n}_{tag}") for n in (
        "norm_weight_loaded", "sumsq_done", "inv_done", "rstd_done", "h_done", "turned"))
    scope = ExitStack()
    k.scope = scope
    ss = k.sb(f"ss_{tag}", [P, NJ])
    inv = k.sb(f"inv_{tag}", [P, NJ])
    rstd = k.sb(f"rstd_{tag}", [P, NJ])
    turned = k.ps(f"turned_ps_{tag}", [P, 4, W])
    rows = hn if weight is not None else src
    wrow = k.sb(f"norm_row_{tag}", [P, D]) if weight is not None else None
    with scope, nc.Block() as block:
        @block.sync
        def _(sp):
            if weight is not None:
                sp.dma_start(wrow[:], weight.broadcast_to([P, D])).then_inc(s_w, 16)

        @block.scalar
        def _(act):
            if weight is None:
                if hn is not None:
                    nc.scalar.activation(hn[:], src[:], ACT.Copy)
                return
            for j in range(NJ):
                nc.scalar.activation(hn[:, j, :], src[:, j, :], ACT.Square,
                                     accum_out=ss[:, j:j + 1]).then_inc(s_ss, 1)
            act.wait_ge(s_inv, 1)
            nc.scalar.activation(rstd[:], inv[:], ACT.Sqrt).then_inc(s_rs, 1)

        @block.vector
        def _(dve):
            o = Order(dve, k.order["dve"])
            if weight is not None:
                dve.wait_ge(s_ss, NJ)
                o(nc.vector.tensor_scalar(ss[:], ss[:], 1.0 / D, EPS, ALU.mult, ALU.add))
                nc.vector.reciprocal(inv[:], ss[:]).then_inc(s_inv, 1)
                dve.wait_ge(s_rs, 1)
                refine(nc, o, rstd[:], ss[:], inv[:])
                dve.wait_ge(s_w, 16)
                for j in range(NJ):
                    nc.vector.scalar_tensor_tensor(out=hn[:, j, :], in0=src[:, j, :], scalar=rstd[:, j:j + 1],
                                                   in1=wrow[:], op0=ALU.mult, op1=ALU.mult).then_inc(s_h, 1)
            for b in range(4):
                j, c0 = b // 2, 4 * (b % 2)
                dve.wait_ge(s_t, b + 1)
                dst = k.hT[:, c0:c0 + 4, j * P:(j + 1) * P]
                got = turned[:, b, :].rearrange("p (c t) -> p c t", c=4)
                nc.vector.tensor_copy(dst, got)
            o.restart()

        @block.tensor
        def _(pe):
            for b in range(4):
                j, c0 = b // 2, 4 * (b % 2)
                if weight is not None:
                    pe.wait_ge(s_h, j + 1)
                for c in range(4):
                    last = nc.tensor.transpose(turned[:, b, c * P:(c + 1) * P],
                                               rows[:, j, c0 + c:D:KC], k.table("ident"))
                last.then_inc(s_t, 1)
    k.scope = k.ctx


def stage_project(k):
    nc, i = k.nc, k.i
    k.qkT = k.sb("gla_qkT", [P, 2, GLA_H, T])
    k.nat = k.sb("nat", [P, 5, NJ, 2 * W])
    k.glrT = k.sb("glrT", [RANK, 2, T])
    k.dab = k.sb("dab", [P, NJ, 4 * GDN_H])
    k.conv = k.sb("conv", [P, 3 * GDN_H, T])
    PAD = TAPS // 2
    s_wf = [k.sem(f"w_in_loaded{b}") for b in range(2)]
    s_ws, s_cw, s_pad = k.sem("w_small_loaded"), k.sem("conv_w_loaded"), k.sem("pad_zeroed")
    s_prod, s_out, s_sm = (k.sem(n) for n in ("block_product", "block_out", "small_product"))
    scope = ExitStack()
    k.scope = scope
    with scope:
        wbuf = [k.sb(f"w_in_buf{b}", [P, KC, W]) for b in range(2)]
        wsm = k.sb("w_small", [P, KC, 64])
        cin = k.sb("conv_in", [P, 3 * GDN_H, T + 2 * PAD])
        cw = k.sb("conv_w", [P, 3 * GDN_H, TAPS])
        pp = k.ps("proj_ps", [P, 2, 2 * W])
        sm = k.ps("small_ps", [P, 3, W])
        wsrc = i["w_in_blocks"].rearrange("b (p c) n -> b p c n", c=KC)
        nblk = NT_BLOCKS + NN_BLOCKS
        with nc.Block() as block:
            @block.sync
            def _(sp):
                for b in range(2):
                    sp.dma_start(wbuf[b][:], wsrc[b]).then_inc(s_wf[b], 16)
                sp.dma_start(wsm[:], i["w_in_small"].rearrange("(p c) n -> p c n", c=KC)).then_inc(s_ws, 16)
                sp.dma_start(cw[:], i["conv_w"].rearrange("p (g t) -> p g t", t=TAPS)).then_inc(s_cw, 16)
                with nc.sync.Fori(1, nblk // 2) as it:
                    for b in range(2):
                        sp.wait_ge(s_prod, it * 2 + (b - 1))
                        sp.dma_start(wbuf[b][:], wsrc[it * 2 + b]).then_inc(s_wf[b], 16)

            def turned_block(b):
                for m in range(4):
                    for c in range(KC):
                        last = nc.tensor.matmul(pp[:, b, m * T:(m + 1) * T],
                                                wbuf[b][:, c, m * P:(m + 1) * P], k.hT[:, c, :],
                                                start=(c == 0), stop=(c == KC - 1))
                return last

            def straight_block(b):
                for j in range(NJ):
                    for c in range(KC):
                        last = nc.tensor.matmul(pp[:, b, j * W:(j + 1) * W],
                                                k.hT[:, c, j * P:(j + 1) * P], wbuf[b][:, c, :],
                                                start=(c == 0), stop=(c == KC - 1))
                return last

            @block.tensor
            def _(pe):
                pe.wait_ge(s_ws, 16)
                for d in range(2):
                    for c in range(KC):
                        nc.tensor.matmul(sm[0:RANK, d, 0:T], wsm[:, c, d * RANK:(d + 1) * RANK],
                                         k.hT[:, c, :], start=(c == 0), stop=(c == KC - 1))
                for j in range(NJ):
                    for c in range(KC):
                        last = nc.tensor.matmul(sm[:, 2, j * 32:(j + 1) * 32],
                                                k.hT[:, c, j * P:(j + 1) * P], wsm[:, c, 32:64],
                                                start=(c == 0), stop=(c == KC - 1))
                last.then_inc(s_sm, 1)
                for b in range(2):
                    pe.wait_ge(s_wf[b], 16)
                    turned_block(b).then_inc(s_prod, 1)
                with nc.tensor.Fori(1, NT_BLOCKS // 2) as it:
                    for b in range(2):
                        pe.wait_ge(s_wf[b], it * 16 + 16)
                        pe.wait_ge(s_out, it * 2 + (b - 1))
                        turned_block(b).then_inc(s_prod, 1)
                with nc.tensor.Fori(NT_BLOCKS // 2, nblk // 2) as it:
                    for b in range(2):
                        pe.wait_ge(s_wf[b], it * 16 + 16)
                        pe.wait_ge(s_out, it * 2 + (b - 1))
                        straight_block(b).then_inc(s_prod, 1)

            @block.scalar
            def _(act):
                act.wait_ge(s_sm, 1)
                nc.scalar.activation(k.glrT[:], sm[0:RANK, 0:2, 0:T], ACT.Copy)
                nc.scalar.activation(k.dab[:], sm[:, 2, 0:64].rearrange("p (j n) -> p j n", j=NJ), ACT.Copy)
                for b in range(2):
                    act.wait_ge(s_prod, b + 1)
                    nc.scalar.activation(k.qkT[:, b], pp[:, b, :].rearrange("p (m t) -> p m t", m=4),
                                         ACT.Copy).then_inc(s_out, 1)
                act.wait_ge(s_pad, 2)
                with nc.scalar.Fori(1, NT_BLOCKS // 2) as it:
                    for b in range(2):
                        act.wait_ge(s_prod, it * 2 + (b + 1))
                        nc.scalar.activation(cin[:, bass.ds(it * 8 + (4 * b - 8), 4), PAD:PAD + T],
                                             pp[:, b, :].rearrange("p (m t) -> p m t", m=4),
                                             ACT.Copy).then_inc(s_out, 1)
                with nc.scalar.Fori(NT_BLOCKS // 2, nblk // 2) as it:
                    for b in range(2):
                        act.wait_ge(s_prod, it * 2 + (b + 1))
                        nc.scalar.activation(k.nat[:, bass.ds(it - NT_BLOCKS // 2, 1), :, b * W:(b + 1) * W],
                                             pp[:, b, :].rearrange("p (o j n) -> p o j n", o=1, j=NJ),
                                             ACT.Copy).then_inc(s_out, 1)

            @block.vector
            def _(dve):
                o = Order(dve, k.order["dve"])
                nc.vector.memset(cin[:, :, 0:PAD], 0.0).then_inc(s_pad, 1)
                nc.vector.memset(cin[:, :, PAD + T:], 0.0).then_inc(s_pad, 1)
                dve.wait_ge(s_pad, 2)
                dve.wait_ge(s_cw, 16)
                with nc.vector.Fori(1, NT_BLOCKS // 2) as it:
                    o.restart()
                    for b in range(2):
                        dve.wait_ge(s_out, it * 2 + (b + 1))
                        for t in range(TAPS):
                            for m in range(4):
                                g = it * 8 + (4 * b - 8 + m)
                                acc = k.conv[:, bass.ds(g, 1), :]
                                seen = cin[:, bass.ds(g, 1), t:t + T]
                                tap = cw[:, bass.ds(g, 1), t]
                                if t == 0:
                                    ins = nc.vector.tensor_scalar(acc, seen, tap, None, ALU.mult)
                                else:
                                    ins = nc.vector.scalar_tensor_tensor(
                                        out=acc, in0=seen, scalar=tap, in1=acc, op0=ALU.mult, op1=ALU.add)
                                o(ins)
                o.restart()
    k.scope = k.ctx


def stage_gates(k):
    nc, i = k.nc, k.i
    k.la = k.sb("log_a", [P, 2, NJ, W])
    k.g = k.sb("g", [P, 2, NJ, GDN_H])
    k.gcum = k.sb("g_cum", [P, 2, NJ, GDN_H])
    k.eg = k.sb("exp_g_cum", [P, 2, NJ, GDN_H])
    k.et = k.sb("exp_g_tail", [P, 2, NJ, GDN_H])
    k.beta = k.sb("beta", [P, 2, NJ, GDN_H])
    k.beg = k.sb("beta_exp_g", [P, 2, NJ, GDN_H])
    k.dec = k.sb("chunk_decay", [P, 2, 2, NJ, GDN_H])
    k.rn = k.sb("inv_norm", [P, 2 * GDN_H, T])
    names = ("gate_w_loaded", "z_product", "z_abs", "z_log", "log_a_done", "rate_done", "softplus_z",
             "softplus_log", "beta_exp", "beta_done", "g_done", "g_sums", "tail_diff", "g_exps",
             "silu_done", "squares_done", "norm_product", "norm_inv", "norm_exp", "log_a_min",
             "sp_abs", "ones_ready")
    (s_ld, s_z, s_abs, s_log, s_la, s_rate, s_spz, s_spl, s_be, s_bd, s_g, s_sum, s_td, s_ge,
     s_silu, s_sq, s_np, s_ni, s_ne, s_mn, s_sa, s_one) = (k.sem(n) for n in names)
    scope = ExitStack()
    k.scope = scope
    with scope:
        w2 = k.sb("gate_w2", [RANK, 2, W])
        gb = k.sb("gate_b", [1, 2, W])
        rows = k.sb("gdn_rows", [P, 2, 2 * GDN_H])
        zabs = k.sb("z_absexp", [P, 2, NJ, W])
        sp = k.sb("sp", [P, 4, 2, NJ, GDN_H])
        sq = k.sb("sq", [P, 2 * GDN_H, T])
        zp = k.ps("z_ps", [P, 2, NJ, W])
        sp_ps = k.ps("sums_ps", [P, W])
        npz = k.ps("norm_ps", [P, 2, W])
        with nc.Block() as block:
            @block.sync
            def _(sy):
                for d, n in enumerate(("fwd", "bwd")):
                    sy.dma_start(w2[:, d, :], i[f"gla_gate_w2_{n}"][0]).then_inc(s_ld, 16)
                    sy.dma_start(gb[:, d, :], i[f"gla_gate_b_{n}"]).then_inc(s_ld, 16)
                    h = slice(d * GDN_H, (d + 1) * GDN_H)
                    sy.dma_start(rows[:, 0, h], i[f"gdn_a_log_{n}"].broadcast_to([P, GDN_H])).then_inc(s_ld, 16)
                    sy.dma_start(rows[:, 1, h], i[f"gdn_dt_bias_{n}"].broadcast_to([P, GDN_H])).then_inc(s_ld, 16)

            @block.tensor
            def _(pe):
                pe.wait_ge(s_ld, 128)
                for d in range(2):
                    for j in range(NJ):
                        nc.tensor.matmul(zp[:, d, j, :], k.glrT[:, d, j * P:(j + 1) * P], w2[:, d, :],
                                         start=True, stop=False)
                        nc.tensor.matmul(zp[:, d, j, :], k.table("ones")[0:1, :], gb[:, d, :],
                                         start=False, stop=True).then_inc(s_z, 1)
                pe.wait_ge(s_g, 1)
                n = NJ * GDN_H
                for d in range(2):
                    nc.tensor.matmul(sp_ps[:, d * n:(d + 1) * n], k.table("cum", d),
                                     k.g[:, d], start=True, stop=True)
                nc.tensor.matmul(sp_ps[:, 2 * n:4 * n], k.table("blk"), k.g[:], start=True, stop=True)
                for c in range(2):
                    last = nc.tensor.matmul(sp_ps[:, (4 + 2 * c) * n:(6 + 2 * c) * n],
                                            k.table("half", c), k.g[:], start=True, stop=True)
                last.then_inc(s_sum, 1)
                pe.wait_ge(s_sq, 1)
                for b in range(GDN_H):
                    if b >= 2:
                        pe.wait_ge(s_ni, b - 1)
                    nc.tensor.matmul(npz[:, b % 2, :], k.table("ones"), sq[:, 2 * b:2 * b + 2, :],
                                     start=True, stop=True).then_inc(s_np, 1)

            @block.scalar
            def _(act):
                act.wait_ge(s_z, 4)
                nc.scalar.activation(zabs[:], zp[:], ACT.Abs).then_inc(s_abs, 1)
                act.wait_ge(s_abs, 1)
                nc.scalar.activation(zabs[:], zabs[:], ACT.Exp, scale=-1.0).then_inc(s_abs, 1)
                act.wait_ge(s_abs, 2)
                nc.scalar.activation(zabs[:], zabs[:], ACT.Ln, bias=1.0).then_inc(s_log, 1)
                act.wait_ge(s_spz, 2)
                nc.scalar.activation(sp[:, 1], sp[:, 1], ACT.Exp, scale=-1.0).then_inc(s_sa, 1)
                act.wait_ge(s_sa, 1)
                nc.scalar.activation(sp[:, 1], sp[:, 1], ACT.Ln, bias=1.0).then_inc(s_spl, 1)
                nc.scalar.activation(rows[:, 0, :], rows[:, 0, :], ACT.Exp).then_inc(s_rate, 1)
                nc.scalar.activation(k.beta[:],
                                     k.dab[:, :, 2 * GDN_H:].rearrange("p j (d h) -> p d j h", d=2),
                                     ACT.Exp, scale=-1.0).then_inc(s_be, 1)
                act.wait_ge(s_td, 1)
                nc.scalar.activation(k.eg[:], k.gcum[:], ACT.Exp).then_inc(s_ge, 1)
                nc.scalar.activation(k.et[:], k.et[:], ACT.Exp).then_inc(s_ge, 1)
                nc.scalar.activation(k.dec[:], k.dec[:], ACT.Exp).then_inc(s_ge, 1)
                nc.scalar.activation(k.conv[:], k.conv[:], ACT.Silu).then_inc(s_silu, 1)
                act.wait_ge(s_ni, GDN_H)
                nc.scalar.activation(k.rn[:, 0:GDN_H], k.rn[:, 0:GDN_H], ACT.Sqrt, scale=1.0 / GDN_D)
                nc.scalar.activation(k.rn[:, GDN_H:], k.rn[:, GDN_H:], ACT.Sqrt)

            @block.vector
            def _(dve):
                o = Order(dve, k.order["dve"])
                dve.wait_ge(s_ld, 128)
                z = k.dab[:, :, 0:2 * GDN_H].rearrange("p j (d h) -> p d j h", d=2)
                for d in range(2):
                    o(nc.vector.tensor_tensor(sp[:, 0, d], z[:, d],
                                              bc(rows[:, 1, d * GDN_H:(d + 1) * GDN_H], 1, NJ), ALU.add))
                o(nc.vector.tensor_scalar(sp[:, 1], sp[:, 0], -1.0, None, ALU.mult))
                nc.vector.tensor_tensor(sp[:, 1], sp[:, 1], sp[:, 0], ALU.max).then_inc(s_spz, 1)
                nc.vector.tensor_scalar(sp[:, 0], sp[:, 0], 0.0, None, ALU.max).then_inc(s_spz, 1)
                dve.wait_ge(s_abs, 1)
                nc.vector.tensor_scalar(k.la[:], zp[:], 0.0, None, ALU.min).then_inc(s_mn, 1)
                dve.wait_ge(s_log, 1)
                dve.wait_ge(s_mn, 1)
                o(nc.vector.tensor_tensor(k.la[:], k.la[:], zabs[:], ALU.subtract))
                dve.wait_ge(s_spl, 1)
                dve.wait_ge(s_spz, 2)
                o(nc.vector.tensor_tensor(sp[:, 0], sp[:, 0], sp[:, 1], ALU.add))
                dve.wait_ge(s_rate, 1)
                for d in range(2):
                    o(nc.vector.tensor_tensor(k.g[:, d], sp[:, 0, d],
                                              bc(rows[:, 0, d * GDN_H:(d + 1) * GDN_H], 1, NJ), ALU.mult))
                nc.vector.tensor_scalar(k.g[:], k.g[:], -1.0, None, ALU.mult).then_inc(s_g, 1)
                dve.wait_ge(s_be, 1)
                o(nc.vector.tensor_scalar(k.beta[:], k.beta[:], 1.0, None, ALU.add))
                o(nc.vector.reciprocal(k.beta[:], k.beta[:]))
                n = 2 * NJ * GDN_H
                dve.wait_ge(s_sum, 1)
                flat = "p d j h -> p (d j h)"
                o(nc.vector.tensor_copy(k.gcum[:].rearrange(flat), sp_ps[:, 0:n]))
                nc.vector.tensor_copy(k.dec[:].rearrange("p c d j h -> p (c d j h)"), sp_ps[:, 2 * n:4 * n])
                o(nc.vector.tensor_tensor(k.et[:].rearrange(flat), sp_ps[:, n:2 * n],
                                          k.gcum[:].rearrange(flat), ALU.subtract))
                dve.sem_inc(s_td, 1)
                dve.wait_ge(s_ge, 3)
                o(nc.vector.tensor_tensor(k.beg[:], k.beta[:], k.eg[:], ALU.mult))
                dve.wait_ge(s_silu, 1)
                nc.vector.tensor_tensor(sq[:], k.conv[:, 0:2 * GDN_H], k.conv[:, 0:2 * GDN_H],
                                        ALU.mult).then_inc(s_sq, 1)
                for b in range(GDN_H):
                    dve.wait_ge(s_np, b + 1)
                    dst = k.rn[:, 2 * b:2 * b + 2, :]
                    o(nc.vector.tensor_scalar(dst.rearrange("p a t -> p (a t)"), npz[:, b % 2, :],
                                              EPS, None, ALU.add))
                    nc.vector.reciprocal(dst, dst).then_inc(s_ni, 1)
                o.restart()
    k.scope = k.ctx


def stage_gla(k):
    nc = k.nc
    HP = 2
    NI = GLA_H // HP
    U = 4
    k.oa = k.sb("o_gla", [P, NJ, D])
    A = range(HP)
    mk = lambda n: [k.sem(f"gla_{n}{a}") for a in A]
    (s_stg, s_cum, s_tot, s_exp, s_te, s_dk, s_sc, s_kt, s_at, s_ktn, s_kv, s_st, s_o, s_hd, s_zero, s_v) = (
        mk(n) for n in ("staged", "cum_product", "total_out", "exps_done", "tail_exp", "decayed", "scores",
                        "tail_turned", "scores_masked", "tail_natural", "chunk_kv", "state_done",
                        "out_product", "head_done", "zeroed", "v_staged"))
    scope = ExitStack()
    k.scope = scope
    with scope:
        sb = lambda n, sh: [k.sb(f"gla_{n}{a}", sh) for a in A]
        q, kk = sb("q", [P, T]), sb("k", [P, T])
        la, v = sb("la", [P, U, P]), sb("v", [P, NJ, GLA_DV])
        tot, dec = sb("tot", [P, U, 2]), sb("dec", [P, U, 2])
        ep, en, et = sb("ep", [P, U, P]), sb("en", [P, U, P]), sb("et", [P, U, P])
        at, ktn = sb("at", [P, U, P]), sb("ktn", [P, U, P])
        st = sb("st", [P, 3, 2, GLA_DV])
        B0 = [k.ps(f"gla_cum_ps{a}", [P, U, P]) for a in A]
        B1 = [k.ps(f"gla_sc_ps{a}", [P, U, P]) for a in A]
        BO = [k.ps(f"gla_out_ps{a}", [P, NJ, W]) for a in A]

        def rows(d, n):
            m = n if d == 0 else 3 - n
            return m // 2, m % 2

        with nc.Block() as block:
            @block.scalar
            def _(act):
                with nc.scalar.Fori(0, NI) as it:
                    for a in A:
                        h = it * HP + a
                        nc.scalar.activation(la[a][:], k.la[:, :, :, bass.ds(h * P, P)].rearrange("p d j n -> p (d j) n"),
                                             ACT.Copy, scale=1.0 / TAU).then_inc(s_stg[a], 1)
                        nc.scalar.activation(q[a][:], k.qkT[:, 0, bass.ds(h, 1), :].rearrange("p o t -> p (o t)"), ACT.Copy,
                                             scale=float(GLA_DK) ** -0.5).then_inc(s_stg[a], 1)
                        nc.scalar.activation(kk[a][:], k.qkT[:, 1, bass.ds(h, 1), :].rearrange("p o t -> p (o t)"), ACT.Copy).then_inc(s_stg[a], 1)
                        nc.scalar.activation(v[a][:], k.nat[:, 0, :, bass.ds(h * GLA_DV, GLA_DV)],
                                             ACT.Copy).then_inc(s_v[a], 1)
                    for a in A:
                        act.wait_ge(s_cum[a], it + 1)
                        act.wait_ge(s_tot[a], it * 2 + 2)
                        nc.scalar.activation(ep[a][:], B0[a][:], ACT.Exp).then_inc(s_exp[a], 1)
                        nc.scalar.activation(en[a][:], B0[a][:], ACT.Exp, scale=-1.0).then_inc(s_exp[a], 1)
                        nc.scalar.activation(et[a][:], et[a][:], ACT.Exp).then_inc(s_exp[a], 1)
                        nc.scalar.activation(dec[a][:], tot[a][:], ACT.Exp).then_inc(s_exp[a], 1)
                    for a in A:
                        act.wait_ge(s_kt[a], it + 1)
                        nc.scalar.activation(ktn[a][:], B0[a][:], ACT.Copy).then_inc(s_ktn[a], 1)
                    for a in A:
                        act.wait_ge(s_hd[a], it + 1)

            @block.vector
            def _(dve):
                o = Order(dve, k.order["dve"])
                for a in A:
                    nc.vector.memset(at[a][:], 0.0).then_inc(s_zero[a], 1)
                with nc.vector.Fori(0, NI) as it:
                    o.restart()
                    for a in A:
                        dve.wait_ge(s_cum[a], it + 1)
                        o(nc.vector.tensor_copy(tot[a][:, 0:2], B0[a][:, 0:2, CH - 1::CH]))
                        o(nc.vector.tensor_copy(tot[a][:, 2:4], B0[a][:, 2:4, 0::CH]))
                        for d in range(2):
                            nc.vector.tensor_tensor(
                                et[a][:, 2 * d:2 * d + 2].rearrange("p j (c t) -> p (j c) t", c=2),
                                bc(tot[a][:, 2 * d:2 * d + 2].rearrange("p j c -> p (j c)"), 2, CH),
                                B0[a][:, 2 * d:2 * d + 2].rearrange("p j (c t) -> p (j c) t", c=2),
                                ALU.subtract).then_inc(s_tot[a], 1)
                    for a in A:
                        dve.wait_ge(s_exp[a], it * 4 + 4)
                        dve.wait_ge(s_stg[a], it * 3 + 3)
                        for e, x in ((ep, q), (en, kk), (et, kk)):
                            e4 = e[a][:].rearrange("p (d j) t -> p d (j t)", d=2)
                            nc.vector.tensor_tensor(e4, e4, bc(x[a][:], 1, 2), ALU.mult).then_inc(s_dk[a], 1)
                    for a in A:
                        dve.wait_ge(s_zero[a], 1)
                        dve.wait_ge(s_sc[a], it + 1)
                        for d in range(2):
                            nc.vector.copy_predicated(at[a][:, 2 * d:2 * d + 2], bc(k.table("incl", d).bitcast(I32), 1, NJ),
                                                      B1[a][:, 2 * d:2 * d + 2]).then_inc(s_at[a], 1)
                    for n in range(3):
                        for a in A:
                            dve.wait_ge(s_kv[a], it * 3 + (n + 1))
                            kv = B1[a][:].rearrange("p u t -> p (u t)")
                            for d in range(2):
                                j, c = rows(d, n)
                                got = kv[:, d * GLA_DV:(d + 1) * GLA_DV]
                                if n == 0:
                                    ins = nc.vector.tensor_copy(st[a][:, 0, d], got)
                                else:
                                    ins = nc.vector.scalar_tensor_tensor(
                                        out=st[a][:, n, d], in0=st[a][:, n - 1, d],
                                        scalar=dec[a][:, 2 * d + j, c:c + 1], in1=got, op0=ALU.mult, op1=ALU.add)
                                ins.then_inc(s_st[a], 1)
                            dve.wait_ge(s_st[a], it * 6 + (2 * n + 2))
                    for a in A:
                        dve.wait_ge(s_o[a], it + 1)
                        h = it * HP + a
                        nc.vector.tensor_copy(k.oa[:, :, bass.ds(h * GLA_DV, GLA_DV)],
                                              BO[a][:, :, 0:GLA_DV]).then_inc(s_hd[a], 1)
                    for a in A:
                        dve.wait_ge(s_hd[a], it + 1)
                o.restart()

            @block.tensor
            def _(pe):
                po = Order(pe, k.order["pe"])
                with nc.tensor.Fori(0, NI) as it:
                    po.restart()
                    for a in A:
                        pe.wait_ge(s_stg[a], it * 3 + 3)
                        for u in range(U):
                            last = nc.tensor.matmul(B0[a][:, u], la[a][:, u], k.table("cum", u // 2),
                                                    start=True, stop=True)
                        last.then_inc(s_cum[a], 1)
                    for a in A:
                        pe.wait_ge(s_dk[a], it * 3 + 3)
                        for u in range(U):
                            last = nc.tensor.matmul(B1[a][:, u], en[a][:, u], ep[a][:, u], start=True, stop=True)
                        last.then_inc(s_sc[a], 1)
                        for u in range(U):
                            last = nc.tensor.transpose(B0[a][:, u], et[a][:, u], k.table("ident"))
                        last.then_inc(s_kt[a], 1)
                    for a in A:
                        pe.wait_ge(s_v[a], it + 1)
                        pe.wait_ge(s_at[a], it * 2 + 2)
                        for j in range(NJ):
                            for d in range(2):
                                nc.tensor.matmul(BO[a][:, j, 0:GLA_DV], at[a][:, 2 * d + j], v[a][:, j],
                                                 start=(d == 0), stop=True, skip_group_check=True)
                    for n in range(4):
                        for a in A:
                            if n < 3:
                                pe.wait_ge(s_ktn[a], it + 1)
                                if n:
                                    pe.wait_ge(s_st[a], it * 6 + 2 * n)
                                kv = B1[a][:].rearrange("p u t -> p (u t)")
                                for d in range(2):
                                    j, c = rows(d, n)
                                    r = slice(c * CH, (c + 1) * CH)
                                    last = nc.tensor.matmul(kv[:, d * GLA_DV:(d + 1) * GLA_DV],
                                                            ktn[a][r, 2 * d + j], v[a][r, j],
                                                            start=True, stop=True)
                                    if d == 0:
                                        po(last)
                                last.then_inc(s_kv[a], 1)
                            if n:
                                pe.wait_ge(s_st[a], it * 6 + 2 * n)
                                for d in range(2):
                                    j, c = rows(d, n)
                                    r = slice(c * CH, (c + 1) * CH)
                                    last = nc.tensor.matmul(BO[a][r, j, 0:GLA_DV], ep[a][:, 2 * d + j, r],
                                                            st[a][:, n - 1, d], start=False, stop=True,
                                                            skip_group_check=True)
                                if n == 3:
                                    last.then_inc(s_o[a], 1)
                    for a in A:
                        pe.wait_ge(s_hd[a], it + 1)
    k.scope = k.ctx


def stage_gdn(k):
    nc = k.nc
    HP = 2
    NI = GDN_H // HP
    U = 4
    k.ob = k.sb("o_gdn", [P, NJ, D])
    A = range(HP)
    mk = lambda n: [k.sem(f"gdn_{n}{a}") for a in A]
    (s_qk, s_vg, s_p1, s_diff, s_ex, s_sc, s_nb, s_lt, s_lv, s_vs, s_vp, s_zz, s_x, s_uw, s_uws, s_ws, s_vn,
     s_kv, s_s, s_hd) = (
        mk(n) for n in ("qk_staged", "v_g_staged", "first_products", "diffs_done", "exps_done", "masked",
                        "natural_done", "L_turned", "L_done", "level_masked", "level_product", "update_product",
                        "inverse_done", "uw_product", "uw_out", "ws_product", "v_new_done", "kv_product",
                        "state_done", "head_done"))
    scope = ExitStack()
    k.scope = scope
    with scope:
        sb = lambda n, sh: [k.sb(f"gdn_{n}{a}", sh) for a in A]
        q, kk, v = sb("q", [P, T]), sb("k", [P, T]), sb("v", [P, T])
        gB = sb("gB", [P, 2, NJ, P])
        kbg, ktl, vb = (sb(n, [P, 2, NJ, P]) for n in ("kbg", "ktl", "vb"))
        mx, mn = sb("mx", [P, 2, NJ, P]), sb("mn", [P, 2, NJ, P])
        nL, aT = sb("nL", [P, 2, NJ, P]), sb("aT", [P, 2, NJ, P])
        X, XT, V = (sb(n, [P, 2, NJ, P]) for n in ("X", "XT", "V"))
        us, wT, vn = gB, mx, mn
        S = sb("S", [P, 2, P])
        B = [[k.ps(f"gdn_ps{a}_{b}", [P, 2, NJ, P]) for b in range(4)] for a in A]

        def rows(d, n):
            m = n if d == 0 else 3 - n
            return m // 2, m % 2

        def col(small, h):
            return small[:, :, :, bass.ds(h, 1)].broadcast_to([P, 2, NJ, P])

        def mask(name, n=0):
            return k.tab[:, OFF[name] + 2 * n * P:OFF[name] + (2 * n + 2) * P].rearrange(
                "p (d t) -> p d t", d=2)

        def masked(eng, out, in0, name, n=0):
            ins = []
            for d in range(2):
                ins.append(eng.tensor_tensor(out[:, d], in0[:, d], bc(mask(name, n)[:, d], 1, NJ), ALU.mult))
            return ins

        with nc.Block() as block:
            @block.gpsimd
            def _(pool):
                o = Order(pool, k.order["pool"])
                with nc.gpsimd.Fori(0, NI) as it:
                    o.restart()
                    for a in A:
                        h = it * HP + a
                        flat = lambda x: x.rearrange("p o t -> p (o t)")
                        nc.gpsimd.tensor_tensor(q[a][:], flat(k.conv[:, bass.ds(h, 1), :]),
                                                flat(k.rn[:, bass.ds(h, 1), :]), ALU.mult).then_inc(s_qk[a], 1)
                        nc.gpsimd.tensor_tensor(kk[a][:], flat(k.conv[:, bass.ds(h + GDN_H, 1), :]),
                                                flat(k.rn[:, bass.ds(h + GDN_H, 1), :]), ALU.mult).then_inc(s_qk[a], 1)
                    for a in A:
                        h = it * HP + a
                        pool.wait_ge(s_ex[a], it * 2 + 2)
                        for ins in masked(nc.gpsimd, mx[a], mx[a], "strictn"):
                            o(ins)
                        nc.gpsimd.tensor_tensor(mx[a][:], mx[a][:], col(k.beta, h), ALU.mult).then_inc(s_sc[a], 1)
                        for ins in masked(nc.gpsimd, mn[a], mn[a], "incl"):
                            ins.then_inc(s_sc[a], 1)
                    for a in A:
                        pool.wait_ge(s_lv[a], it * 2 + 1)
                        for ins in masked(nc.gpsimd, X[a], nL[a], "lev0"):
                            o(ins)
                        nc.gpsimd.tensor_tensor(X[a][:].rearrange("p d j t -> p (d j) t"),
                                                X[a][:].rearrange("p d j t -> p (d j) t"),
                                                bc(k.table("ident"), 1, U), ALU.add).then_inc(s_x[a], 1)
                    for a in A:
                        pool.wait_ge(s_hd[a], it + 1)
                o.restart()

            @block.scalar
            def _(act):
                with nc.scalar.Fori(0, NI) as it:
                    for a in A:
                        h = it * HP + a
                        nc.scalar.activation(v[a][:], k.conv[:, bass.ds(h + 2 * GDN_H, 1), :].rearrange("p o t -> p (o t)"),
                                             ACT.Copy).then_inc(s_vg[a], 1)
                        nc.scalar.activation(gB[a][:], col(k.g, h), ACT.Copy).then_inc(s_vg[a], 1)
                    for a in A:
                        act.wait_ge(s_diff[a], it * 2 + 2)
                        nc.scalar.activation(mx[a][:], mx[a][:], ACT.Exp, scale=-1.0).then_inc(s_ex[a], 1)
                        nc.scalar.activation(mn[a][:], mn[a][:], ACT.Exp).then_inc(s_ex[a], 1)
                    for a in A:
                        act.wait_ge(s_uw[a], it + 1)
                        nc.scalar.activation(us[a][:], B[a][1][:], ACT.Copy).then_inc(s_uws[a], 1)
                        nc.scalar.activation(wT[a][:], B[a][2][:], ACT.Copy).then_inc(s_uws[a], 1)
                    for a in A:
                        act.wait_ge(s_hd[a], it + 1)

            @block.vector
            def _(dve):
                o = Order(dve, k.order["dve"])
                with nc.vector.Fori(0, NI) as it:
                    o.restart()
                    for a in A:
                        h = it * HP + a
                        dve.wait_ge(s_p1[a], it * 3 + 3)
                        o(nc.vector.tensor_tensor(mx[a][:], B[a][2][:], col(k.gcum, h), ALU.subtract))
                        nc.vector.tensor_scalar(mn[a][:], mx[a][:], 0.0, None, ALU.min).then_inc(s_diff[a], 1)
                        nc.vector.tensor_scalar(mx[a][:], mx[a][:], 0.0, None, ALU.max).then_inc(s_diff[a], 1)
                        tk = B[a][0][:, 0]
                        tv = B[a][0][:, 1]
                        for dst, src, f in ((kbg, tk, k.beg), (ktl, tk, k.et), (vb, tv, k.beta)):
                            nc.vector.tensor_tensor(dst[a][:], bc(src, 1, 2), col(f, h), ALU.mult).then_inc(s_nb[a], 1)
                    for a in A:
                        dve.wait_ge(s_sc[a], it * 3 + 3)
                        nc.vector.tensor_tensor(nL[a][:], bc(B[a][1][:, 0], 1, 2), mx[a][:], ALU.mult).then_inc(s_lv[a], 1)
                        nc.vector.tensor_tensor(aT[a][:], bc(B[a][1][:, 1], 1, 2), mn[a][:], ALU.mult).then_inc(s_lv[a], 1)
                    for a in A:
                        dve.wait_ge(s_lt[a], it + 1)
                        for ins in masked(nc.vector, XT[a], B[a][0], "lev"):
                            o(ins)
                        nc.vector.tensor_tensor(XT[a][:].rearrange("p d j t -> p (d j) t"),
                                                XT[a][:].rearrange("p d j t -> p (d j) t"),
                                                bc(k.table("ident"), 1, U), ALU.add).then_inc(s_x[a], 1)
                    for l in range(1, LEVELS):
                        for a in A:
                            dve.wait_ge(s_vp[a], it * (LEVELS - 1) + l)
                            for ins in masked(nc.vector, V[a], B[a][0], "lev", l):
                                ins.then_inc(s_vs[a], 1)
                        for a in A:
                            dve.wait_ge(s_zz[a], it * (LEVELS - 1) + l)
                            nc.vector.tensor_tensor(XT[a][:], XT[a][:], B[a][2][:], ALU.add).then_inc(s_x[a], 1)
                            if l < LEVELS - 1:
                                nc.vector.tensor_tensor(X[a][:], X[a][:], B[a][1][:], ALU.add).then_inc(s_x[a], 1)
                    for a in A:
                        o(nc.vector.memset(S[a][:], 0.0))
                        dve.sem_inc(s_s[a], 1)
                    for n in range(4):
                        for a in A:
                            if n:
                                dve.wait_ge(s_ws[a], it * 3 + n)
                                for d in range(2):
                                    j, c = rows(d, n)
                                    r = slice(c * CH, (c + 1) * CH)
                                    nc.vector.tensor_tensor(vn[a][r, d, j], us[a][r, d, j], B[a][3][r, 0, d],
                                                            ALU.subtract).then_inc(s_vn[a], 1)
                        for a in A:
                            if n < 3:
                                h = it * HP + a
                                dve.wait_ge(s_kv[a], it * 4 + (n + 1))
                                for d in range(2):
                                    j, c = rows(d, n)
                                    nc.vector.scalar_tensor_tensor(
                                        out=S[a][:, d], in0=S[a][:, d], scalar=k.dec[:, c, d, j, bass.ds(h, 1)],
                                        in1=B[a][3][:, 1, d], op0=ALU.mult, op1=ALU.add).then_inc(s_s[a], 1)
                    for a in A:
                        h = it * HP + a
                        dve.wait_ge(s_kv[a], it * 4 + 4)
                        o(nc.vector.tensor_tensor(V[a][:], B[a][0][:], col(k.eg, h), ALU.mult))
                        o(nc.vector.tensor_tensor(V[a][:], V[a][:], B[a][1][:], ALU.add))
                        nc.vector.tensor_tensor(k.ob[:, :, bass.ds(h * GDN_D, GDN_D)], V[a][:, 0], V[a][:, 1],
                                                ALU.add).then_inc(s_hd[a], 1)
                    for a in A:
                        dve.wait_ge(s_hd[a], it + 1)
                o.restart()

            @block.tensor
            def _(pe):
                def each(a, fn):
                    for d in range(2):
                        for j in range(NJ):
                            last = fn(a, d, j)
                    return last

                mm = nc.tensor.matmul
                po = Order(pe, k.order["pe"])
                with nc.tensor.Fori(0, NI) as it:
                    po.restart()
                    for a in A:
                        pe.wait_ge(s_vg[a], it * 2 + 2)
                        each(a, lambda a, d, j: mm(B[a][2][:, d, j], gB[a][:, d, j], k.table("cum", d),
                                                   start=True, stop=True)).then_inc(s_p1[a], 1)
                        pe.wait_ge(s_qk[a], it * 2 + 2)
                        for x, half in ((kk, 0), (v, 1)):
                            for j in range(NJ):
                                last = nc.tensor.transpose(B[a][0][:, half, j], x[a][:, j * P:(j + 1) * P], k.table("ident"))
                        last.then_inc(s_p1[a], 1)
                        for x, half in ((kk, 0), (q, 1)):
                            for j in range(NJ):
                                t = slice(j * P, (j + 1) * P)
                                last = mm(B[a][1][:, half, j], kk[a][:, t], x[a][:, t], start=True, stop=True)
                        last.then_inc(s_p1[a], 1)
                    for a in A:
                        pe.wait_ge(s_nb[a], it * 3 + 3)
                        pe.wait_ge(s_lv[a], it * 2 + 2)
                        each(a, lambda a, d, j: nc.tensor.transpose(B[a][0][:, d, j], nL[a][:, d, j],
                                                                    k.table("ident"))).then_inc(s_lt[a], 1)
                    per = 2 + 2 * (LEVELS - 2) + 1
                    for l in range(1, LEVELS):
                        for a in A:
                            pe.wait_ge(s_x[a], it * per + 2 * l)
                            each(a, lambda a, d, j: mm(B[a][0][:, d, j], nL[a][:, d, j], XT[a][:, d, j],
                                                       start=True, stop=True)).then_inc(s_vp[a], 1)
                        for a in A:
                            pe.wait_ge(s_vs[a], it * 2 * (LEVELS - 1) + 2 * l)
                            last = each(a, lambda a, d, j: mm(B[a][2][:, d, j], X[a][:, d, j], V[a][:, d, j],
                                                              start=True, stop=True))
                            if l < LEVELS - 1:
                                last = each(a, lambda a, d, j: mm(B[a][1][:, d, j], V[a][:, d, j], X[a][:, d, j],
                                                                  start=True, stop=True))
                            last.then_inc(s_zz[a], 1)
                    for a in A:
                        pe.wait_ge(s_x[a], it * per + per)
                        each(a, lambda a, d, j: mm(B[a][1][:, d, j], XT[a][:, d, j], vb[a][:, d, j],
                                                   start=True, stop=True))
                        each(a, lambda a, d, j: mm(B[a][2][:, d, j], kbg[a][:, d, j], XT[a][:, d, j],
                                                   start=True, stop=True)).then_inc(s_uw[a], 1)
                    for n in range(4):
                        for a in A:
                            if n == 0:
                                pe.wait_ge(s_uws[a], it * 2 + 2)
                            pe.wait_ge(s_s[a], it * 7 + (2 * n + 1))
                            if n:
                                for d in range(2):
                                    j, c = rows(d, n)
                                    r = slice(c * CH, (c + 1) * CH)
                                    last = mm(B[a][3][r, 0, d], wT[a][:, d, j, r], S[a][:, d], start=True, stop=True)
                                last.then_inc(s_ws[a], 1)
                            for d in range(2):
                                j, c = rows(d, n)
                                r = slice(c * CH, (c + 1) * CH)
                                mm(B[a][0][r, d, j], q[a][:, j * P + c * CH:j * P + (c + 1) * CH], S[a][:, d],
                                   start=True, stop=True)
                        for a in A:
                            new = us[a] if n == 0 else vn[a]
                            if n:
                                pe.wait_ge(s_vn[a], it * 6 + 2 * n)
                            for d in range(2):
                                j, c = rows(d, n)
                                r = slice(c * CH, (c + 1) * CH)
                                mm(B[a][3][:, 1, d], ktl[a][r, d, j], new[r, d, j], start=True, stop=True)
                                last = mm(B[a][1][r, d, j], aT[a][r, d, j, r], new[r, d, j], start=True, stop=True)
                                if d == 0:
                                    po(last)
                            last.then_inc(s_kv[a], 1)
                    for a in A:
                        pe.wait_ge(s_hd[a], it + 1)
    k.scope = k.ctx


def stage_combine(k):
    nc, i = k.nc, k.i
    s_ld, s_act, s_ss, s_inv, s_rs, s_gate, s_sq = (k.sem(f"comb_{n}") for n in (
        "loaded", "act_done", "sumsq_done", "inv_done", "rstd_done", "gate_done", "squares"))
    scope = ExitStack()
    k.scope = scope
    with scope:
        wa = k.sb("gla_norm", [P, GLA_DV])
        wb = k.sb("gdn_norm", [P, GDN_D])
        tmp = k.sb("comb_sq", [P, 2, NJ, D])
        v = k.sb("comb_var", [P, NJ, GLA_H + GDN_H])
        inv = k.sb("comb_inv", [P, NJ, GLA_H + GDN_H])
        rs = k.sb("comb_rstd", [P, NJ, GLA_H + GDN_H])
        heads = lambda x, n: x.rearrange("p j (h d) -> p j h d", h=n)
        with nc.Block() as block:
            @block.sync
            def _(sp):
                sp.dma_start(wa[:], i["gla_norm_w"].broadcast_to([P, GLA_DV])).then_inc(s_ld, 16)
                sp.dma_start(wb[:], i["gdn_norm_w"].broadcast_to([P, GDN_D])).then_inc(s_ld, 16)

            @block.scalar
            def _(act):
                nc.scalar.activation(k.nat[:, 1:3], k.nat[:, 1:3], ACT.Silu).then_inc(s_act, 1)
                nc.scalar.activation(k.nat[:, 3:5], k.nat[:, 3:5], ACT.Sigmoid).then_inc(s_act, 1)
                act.wait_ge(s_inv, 1)
                nc.scalar.activation(rs[:], inv[:], ACT.Sqrt).then_inc(s_rs, 1)

            @block.gpsimd
            def _(pool):
                o = Order(pool, k.order["pool"])
                nc.gpsimd.tensor_tensor(tmp[:, 0], k.oa[:], k.oa[:], ALU.mult).then_inc(s_sq, 1)
                nc.gpsimd.tensor_tensor(tmp[:, 1], k.ob[:], k.ob[:], ALU.mult).then_inc(s_sq, 1)
                pool.wait_ge(s_act, 1)
                pool.wait_ge(s_ld, 32)
                for n, w, hh in ((0, wa, GLA_H), (1, wb, GDN_H)):
                    for j in range(NJ):
                        r = k.nat[:, 1 + n, j].rearrange("p (h d) -> p h d", h=hh)
                        o(nc.gpsimd.tensor_tensor(r, r, bc(w[:], 1, hh), ALU.mult))
                pool.wait_ge(s_act, 2)
                for n in range(2):
                    nc.gpsimd.tensor_tensor(k.nat[:, 1 + n], k.nat[:, 1 + n], k.nat[:, 3 + n],
                                            ALU.mult).then_inc(s_gate, 1)
                o.restart()

            @block.vector
            def _(dve):
                o = Order(dve, k.order["dve"])
                for n, x, hh in ((0, k.oa, GLA_H), (1, k.ob, GDN_H)):
                    dve.wait_ge(s_sq, n + 1)
                    c = slice(0, GLA_H) if n == 0 else slice(GLA_H, GLA_H + GDN_H)
                    o(nc.vector.tensor_reduce(v[:, :, c], heads(tmp[:, n], hh), AX.X, ALU.add))
                    o(nc.vector.tensor_scalar(v[:, :, c], v[:, :, c], hh / D, EPS, ALU.mult, ALU.add))
                nc.vector.reciprocal(inv[:], v[:]).then_inc(s_inv, 1)
                dve.wait_ge(s_rs, 1)
                refine(nc, o, rs[:], v[:], inv[:])
                for n, x, hh in ((0, k.oa, GLA_H), (1, k.ob, GDN_H)):
                    c = slice(0, GLA_H) if n == 0 else slice(GLA_H, GLA_H + GDN_H)
                    o(nc.vector.tensor_tensor(heads(x[:], hh), heads(x[:], hh), bc(rs[:, :, c], 3, D // hh), ALU.mult))
                    dve.wait_ge(s_gate, n + 1)
                    o(nc.vector.tensor_tensor(x[:], x[:], k.nat[:, 1 + n], ALU.mult))
                o(nc.vector.tensor_tensor(k.oa[:], k.oa[:], k.ob[:], ALU.add))
                o.restart()
    k.scope = k.ctx


def stage_out(k, tag, weight, alpha):
    nc = k.nc
    s_w, s_p = k.sem(f"w_out_loaded_{tag}"), k.sem(f"out_product_{tag}")
    scope = ExitStack()
    k.scope = scope
    with scope:
        w = k.sb(f"w_out_{tag}", [P, KC, D])
        y = k.ps(f"out_ps_{tag}", [P, NJ, 2, W])
        with nc.Block() as block:
            @block.sync
            def _(sp):
                for c in range(0, KC, 2):
                    sp.dma_start(w[:, c:c + 2, :], weight[:, c:c + 2, :]).then_inc(s_w, 16)

            @block.tensor
            def _(pe):
                pe.wait_ge(s_w, 16 * (KC // 2))
                for j in range(NJ):
                    for n in range(2):
                        for c in range(KC):
                            last = nc.tensor.matmul(y[:, j, n, :], k.hT[:, c, j * P:(j + 1) * P],
                                                    w[:, c, n * W:(n + 1) * W], start=(c == 0), stop=(c == KC - 1))
                        last.then_inc(s_p, 1)

            @block.vector
            def _(dve):
                for j in range(NJ):
                    for n in range(2):
                        dve.wait_ge(s_p, 2 * j + n + 1)
                        xs = k.x[:, j, n * W:(n + 1) * W]
                        nc.vector.scalar_tensor_tensor(out=xs, in0=xs, scalar=alpha, in1=y[:, j, n, :],
                                                       op0=ALU.mult, op1=ALU.add)
    k.scope = k.ctx


def stage_norm(k, tag, gain, bias=None):
    nc = k.nc
    eps = EPS if bias is None else LN_EPS
    s_ld, s_ss, s_inv, s_rs, s_c = (k.sem(f"{n}_{tag}") for n in
                                    ("norm_w_loaded", "sumsq", "inv", "rstd", "centred"))
    scope = ExitStack()
    k.scope = scope
    with scope:
        g = k.sb(f"gain_{tag}", [P, D])
        b = k.sb(f"bias_{tag}", [P, D])
        sq = k.sb(f"sq_{tag}", [P, NJ, D])
        mu, v, inv, rs = (k.sb(f"{n}_{tag}", [P, NJ]) for n in ("mu", "var", "inv", "rstd"))
        with nc.Block() as block:
            @block.sync
            def _(sp):
                sp.dma_start(g[:], gain.broadcast_to([P, D])).then_inc(s_ld, 16)
                if bias is not None:
                    sp.dma_start(b[:], bias.broadcast_to([P, D])).then_inc(s_ld, 16)

            @block.scalar
            def _(act):
                for j in range(NJ):
                    if bias is not None:
                        act.wait_ge(s_c, j + 1)
                    nc.scalar.activation(sq[:, j], k.x[:, j], ACT.Square, accum_out=v[:, j:j + 1]).then_inc(s_ss, 1)
                act.wait_ge(s_inv, 1)
                nc.scalar.activation(rs[:], inv[:], ACT.Sqrt).then_inc(s_rs, 1)

            @block.vector
            def _(dve):
                o = Order(dve, k.order["dve"])
                if bias is not None:
                    o(nc.vector.tensor_reduce(mu[:], k.x[:], AX.X, ALU.add))
                    o(nc.vector.tensor_scalar(mu[:], mu[:], 1.0 / D, None, ALU.mult))
                    for j in range(NJ):
                        nc.vector.tensor_scalar(k.x[:, j], k.x[:, j], mu[:, j:j + 1], None,
                                                ALU.subtract).then_inc(s_c, 1)
                dve.wait_ge(s_ss, NJ)
                o(nc.vector.tensor_scalar(v[:], v[:], 1.0 / D, eps, ALU.mult, ALU.add))
                nc.vector.reciprocal(inv[:], v[:]).then_inc(s_inv, 1)
                dve.wait_ge(s_rs, 1)
                refine(nc, o, rs[:], v[:], inv[:])
                dve.wait_ge(s_ld, 16 if bias is None else 32)
                for j in range(NJ):
                    o(nc.vector.scalar_tensor_tensor(out=k.x[:, j], in0=k.x[:, j], scalar=rs[:, j:j + 1],
                                                     in1=g[:], op0=ALU.mult, op1=ALU.mult))
                if bias is not None:
                    o(nc.vector.tensor_tensor(k.x[:], k.x[:], bc(b[:], 1, NJ), ALU.add))
                o.restart()
    k.scope = k.ctx


def stage_router(k, tag, w_group, w_fine, b_group=None, b_fine=None):
    nc = k.nc
    NL = NG + NE
    s_ld, s_b, s_p, s_d, s_e, s_sel, s_pos = (k.sem(f"{n}_{tag}") for n in (
        "router_loaded", "router_b_loaded", "logits", "logit_diffs", "logit_exps", "selected", "places"))
    scope = ExitStack()
    k.scope = scope
    with scope:
        w = k.sb(f"router_w_{tag}", [P, KC, NL])
        b = k.sb(f"router_b_{tag}", [P, NL])
        lg = k.sb(f"logits_{tag}", [P, NJ, NL])
        eq = k.sb(f"eq_{tag}", [P, NJ, NL])
        s1 = k.sb(f"sel1_{tag}", [P, NJ, NE])
        m = k.sb(f"max_{tag}", [P, 8, NJ])
        ge = k.sb(f"gexp_{tag}", [P, NJ, NG])
        sel = k.sb(f"sel_{tag}", [P, NJ, NE])
        cnt = k.sb(f"count_{tag}", [P, 2])
        lp = k.ps(f"logit_ps_{tag}", [P, NJ, NL])
        pp = k.ps(f"place_ps_{tag}", [P, NJ + 1, NE])
        rank = k.tab[:, OFF["rank"]:OFF["rank"] + NL]
        with nc.Block() as block:
            @block.sync
            def _(sp):
                sp.dma_start(w[:, :, 0:NG], w_group.rearrange("(p c) n -> p c n", c=KC)).then_inc(s_ld, 16)
                sp.dma_start(w[:, :, NG:], w_fine.rearrange("(p c) n -> p c n", c=KC)).then_inc(s_ld, 16)
                if b_group is not None:
                    sp.dma_start(b[:, 0:NG], b_group.broadcast_to([P, NG])).then_inc(s_b, 16)
                    sp.dma_start(b[:, NG:], b_fine.broadcast_to([P, NE])).then_inc(s_b, 16)

            @block.tensor
            def _(pe):
                pe.wait_ge(s_ld, 32)
                for j in range(NJ):
                    for c in range(KC):
                        last = nc.tensor.matmul(lp[:, j, :], k.hT[:, c, j * P:(j + 1) * P], w[:, c, :],
                                                start=(c == 0), stop=(c == KC - 1))
                last.then_inc(s_p, 1)
                pe.wait_ge(s_sel, 1)
                for j in range(NJ + 1):
                    for i in range(min(j + 1, NJ)):
                        t = k.table("before" if i == j else "ones")
                        last = nc.tensor.matmul(pp[:, j], t, sel[:, i], start=(i == 0), stop=(i == min(j, NJ - 1)))
                last.then_inc(s_pos, 1)

            @block.scalar
            def _(act):
                act.wait_ge(s_d, 1)
                nc.scalar.activation(ge[:], ge[:], ACT.Exp).then_inc(s_e, 1)
                act.wait_ge(s_d, 2)
                nc.scalar.activation(m[:, 3], m[:, 3], ACT.Exp).then_inc(s_e, 1)

            @block.vector
            def _(dve):
                o = Order(dve, k.order["dve"])
                tt, ts = nc.vector.tensor_tensor, nc.vector.tensor_scalar

                def first_max(x, n, r, top, sel):
                    o(nc.vector.tensor_reduce(top, x, AX.X, ALU.max))
                    o(tt(sel, x, bc(top, 2, n), ALU.is_equal))
                    o(tt(sel, sel, bc(r, 1, NJ), ALU.mult))
                    o(nc.vector.tensor_reduce(m[:, 7], sel, AX.X, ALU.max))
                    o(tt(sel, sel, bc(m[:, 7], 2, n), ALU.is_equal))

                dve.wait_ge(s_p, 1)
                if b_group is not None:
                    dve.wait_ge(s_b, 32)
                    o(tt(lg[:], lp[:], bc(b[:], 1, NJ), ALU.add))
                else:
                    o(nc.vector.tensor_copy(lg[:], lp[:]))
                grp, fine = lg[:, :, 0:NG], lg[:, :, NG:]
                gs, s2 = eq[:, :, 0:NG], eq[:, :, NG:]
                first_max(grp, NG, rank[:, 0:NG], m[:, 0], gs)
                tt(ge[:], grp, bc(m[:, 0], 2, NG), ALU.subtract).then_inc(s_d, 1)
                o(ts(gs, gs, -1.0, BIG, ALU.add, ALU.mult))
                for j in range(NJ):
                    f = fine[:, j].rearrange("p (g e) -> p g e", g=NG)
                    o(tt(f, f, bc(gs[:, j], 2, EPG), ALU.add))
                first_max(fine, NE, rank[:, NG:], m[:, 1], s1[:])
                o(ts(s2, s1[:], -BIG, None, ALU.mult))
                o(tt(fine, fine, s2, ALU.add))
                first_max(fine, NE, rank[:, NG:], m[:, 2], s2)
                tt(m[:, 3], m[:, 2], m[:, 1], ALU.subtract).then_inc(s_d, 1)
                tt(sel[:], s1[:], s2, ALU.add).then_inc(s_sel, 1)
                o(nc.vector.memset(k.gates[:, :, NE:], 0.0))
                o(nc.vector.memset(k.place[:, :, NE:], -1.0))
                dve.wait_ge(s_e, 1)
                o(nc.vector.tensor_reduce(m[:, 4], ge[:], AX.X, ALU.add))
                dve.wait_ge(s_e, 2)
                o(ts(m[:, 5], m[:, 3], 1.0, None, ALU.add))
                o(tt(m[:, 5], m[:, 5], m[:, 4], ALU.mult))
                o(nc.vector.reciprocal(m[:, 5], m[:, 5]))
                o(tt(m[:, 6], m[:, 5], m[:, 3], ALU.mult))
                o(tt(s1[:], s1[:], bc(m[:, 5], 2, NE), ALU.mult))
                o(tt(s2, s2, bc(m[:, 6], 2, NE), ALU.mult))
                g, pl = k.gates[:, :, 0:NE], k.place[:, :, 0:NE]
                o(tt(g, s1[:], s2, ALU.add))
                dve.wait_ge(s_pos, 1)
                dve.wait_ge(s_sel, 1)
                o(nc.vector.scalar_tensor_tensor(out=pl, in0=pp[:, 0:NJ], scalar=1.0, in1=sel[:],
                                                 op0=ALU.add, op1=ALU.mult))
                o(ts(pl, pl, -1.0, None, ALU.add))
                o(ts(sel[:], pl, float(CAP), None, ALU.is_ge))
                o(tt(k.over[:], sel[:], g, ALU.mult))
                o(nc.vector.tensor_reduce(cnt[:, 0:1], pp[:, NJ], AX.X, ALU.max))
                o(ts(cnt[:, 1:2], cnt[:, 0:1], float(CAP), None, ALU.is_gt))
                o(nc.vector.tensor_copy(k.over_flag[:], cnt[0:1, 1:2]))
                o.restart()
    k.scope = k.ctx


def stage_experts(k, tag, H, w_gate, w_up, w_down, alpha):
    stage_packed(k, tag, H, w_gate, w_up, w_down, alpha)
    full = k.nc.values_load(k.over_flag[0:1, 0:1], min_val=0, max_val=1)
    with k.nc.If(full > 0):
        stage_general(k, tag + "g", H, w_gate, w_up, w_down)
    with k.nc.Else():
        k.nc.all_engine_barrier()


def stage_packed(k, tag, H, w_gate, w_up, w_down, alpha):
    nc = k.nc
    HT = H // P
    NI = NE // 2
    rows = k.h_rows
    (s_lg, s_lu, s_ld, s_pm, s_gx, s_xg, s_g, s_u, s_sg, s_hid, s_pg, s_pt, s_pgs, s_ht, s_hts, s_y, s_ys,
     s_sc, s_add, s_x, s_z) = (k.sem(f"{n}_{tag}") for n in (
         "w_gate_loaded", "w_up_loaded", "w_down_loaded", "onehot_done", "rows_gathered", "gathered_out",
         "gate_product", "up_product", "silu_done", "hidden_done", "gated_onehot_done", "onehot_turned",
         "turned_onehot_out", "hidden_turned", "turned_hidden_out", "y_product", "y_out", "y_scattered",
         "y_added", "x_scaled", "zeroed"))
    scope = ExitStack()
    k.scope = scope
    with scope:
        wg = k.sb(f"w_gate_{tag}", [P, 2, KC, H])
        wu = k.sb(f"w_up_{tag}", [P, 2, KC, H])
        wd = k.sb(f"w_down_{tag}", [P, 2, HT, D])
        one = k.sb(f"onehot_{tag}", [P, NJ, 2, CAP])
        gone = k.sb(f"gated_onehot_{tag}", [P, NJ, 2, CAP])
        goneT = k.sb(f"gated_onehot_T_{tag}", [P, T])
        xgT = k.sb(f"gathered_T_{tag}", [P, KC, P])
        sg = k.sb(f"silu_{tag}", [P, H])
        hid = k.sb(f"hidden_{tag}", [P, H])
        hidT = k.sb(f"hidden_T_{tag}", [P, HT, P])
        y = k.sb(f"y_{tag}", [P, 2, W])
        XG = k.ps(f"gather_ps_{tag}", [P, 2, W])
        SC = k.ps(f"scatter_ps_{tag}", [P, W])
        G = k.ps(f"gate_ps_{tag}", [P, W])
        Up = k.ps(f"up_ps_{tag}", [P, W])
        TP = k.ps(f"turn_ps_{tag}", [P, W])
        Y = k.ps(f"y_ps_{tag}", [P, 2, W])
        vg = w_gate.rearrange("e (p c) n -> e p c n", c=KC)
        vu = w_up.rearrange("e (p c) n -> e p c n", c=KC)
        vd = w_down.rearrange("e (c p) n -> e p c n", p=P)
        scatter_bank = [XG[:, 0], XG[:, 1], SC[:], XG[:, 0]]
        with nc.Block() as block:
            @block.sync
            def _(sp):
                def load(w, v, pair, s_l):
                    for b in range(2):
                        sp.dma_start(w[:, b], v[pair * 2 + b]).then_inc(s_l, 16)

                for w, v, s_l in ((wg, vg, s_lg), (wu, vu, s_lu), (wd, vd, s_ld)):
                    load(w, v, 0, s_l)
                with nc.sync.Fori(1, NI) as it:
                    sp.wait_ge(s_g, it)
                    load(wg, vg, it, s_lg)
                    sp.wait_ge(s_u, it)
                    load(wu, vu, it, s_lu)
                    sp.wait_ge(s_y, it * 2)
                    load(wd, vd, it, s_ld)

            @block.tensor
            def _(pe):
                mm = nc.tensor.matmul

                def gather():
                    for n in range(2):
                        for c in range(4):
                            for j in range(NJ):
                                last = mm(XG[:, n, c * P:(c + 1) * P], rows[:, j, 4 * n + c:D:KC],
                                          one[:, j], start=(j == 0), stop=(j == NJ - 1))
                        last.then_inc(s_gx, 1)

                def both_experts(out, stationary, w, s_done):
                    for c in range(len(w[0])):
                        for b in range(2):
                            last = mm(out[b * CAP:(b + 1) * CAP, 0:w[b][c].shape[-1]],
                                      stationary(c)[:, b * CAP:(b + 1) * CAP], w[b][c],
                                      start=(c == 0), stop=(c == len(w[0]) - 1))
                    last.then_inc(s_done, 1)

                def scatter(base):
                    for o in range(4):
                        if o == 3:
                            pe.wait_ge(s_add, base + 1)
                        mm(scatter_bank[o], goneT[:, (o // 2) * P:(o // 2 + 1) * P], y[:, o % 2],
                           start=True, stop=True).then_inc(s_sc, 1)

                pe.wait_ge(s_pm, 1)
                gather()
                with nc.tensor.Fori(0, NI) as it:
                    pe.wait_ge(s_xg, it * 2 + 2)
                    pe.wait_ge(s_lg, it * 32 + 32)
                    both_experts(G, lambda c: xgT[:, c], [[wg[:, b, c] for c in range(KC)] for b in range(2)], s_g)
                    pe.wait_ge(s_lu, it * 32 + 32)
                    both_experts(Up, lambda c: xgT[:, c], [[wu[:, b, c] for c in range(KC)] for b in range(2)], s_u)
                    pe.wait_ge(s_ys, it * 2 + 2)
                    pe.wait_ge(s_pgs, it + 1)
                    scatter(it * 4)
                    pe.wait_ge(s_pg, it + 1)
                    for j in range(NJ):
                        last = nc.tensor.transpose(TP[:, j * P:(j + 1) * P],
                                                   gone[:, j].rearrange("p b s -> p (b s)"), k.table("ident"))
                    last.then_inc(s_pt, 1)
                    pe.wait_ge(s_pm, it + 2)
                    pe.wait_ge(s_add, it * 4 + 4)
                    gather()
                    pe.wait_ge(s_hid, it + 1)
                    pe.wait_ge(s_pgs, it + 2)
                    for m in range(HT):
                        last = nc.tensor.transpose(TP[:, m * P:(m + 1) * P], hid[:, m * P:(m + 1) * P],
                                                   k.table("ident"))
                    last.then_inc(s_ht, 1)
                    pe.wait_ge(s_hts, it + 1)
                    pe.wait_ge(s_ld, it * 32 + 32)
                    for n in range(2):
                        both_experts(Y[:, n], lambda c: hidT[:, c],
                                     [[wd[:, b, c, n * W:(n + 1) * W] for c in range(HT)] for b in range(2)], s_y)
                pe.wait_ge(s_ys, 2 * NI + 2)
                pe.wait_ge(s_xg, 2 * NI + 2)
                scatter(4 * NI)

            @block.scalar
            def _(act):
                def gathered(base):
                    for n in range(2):
                        act.wait_ge(s_gx, base + (n + 1))
                        nc.scalar.activation(xgT[:, 4 * n:4 * n + 4].rearrange("p c s -> p (c s)"), XG[:, n],
                                             ACT.Copy).then_inc(s_xg, 1)

                gathered(0)
                with nc.scalar.Fori(0, NI) as it:
                    act.wait_ge(s_g, it + 1)
                    nc.scalar.activation(sg[:], G[:, 0:H], ACT.Silu).then_inc(s_sg, 1)
                    act.wait_ge(s_pt, it + 1)
                    nc.scalar.activation(goneT[:], TP[:, 0:T], ACT.Copy).then_inc(s_pgs, 1)
                    gathered(it * 2 + 2)
                    act.wait_ge(s_ht, it + 1)
                    nc.scalar.activation(hidT[:].rearrange("p c s -> p (c s)"), TP[:, 0:HT * P],
                                         ACT.Copy).then_inc(s_hts, 1)
                    for n in range(2):
                        act.wait_ge(s_y, it * 2 + (n + 1))
                        nc.scalar.activation(y[:, n], Y[:, n], ACT.Copy).then_inc(s_ys, 1)

            @block.vector
            def _(dve):
                slots = bc(bc(k.tab[:, OFF["slot"]:OFF["slot"] + CAP], 1, 2), 1, NJ)

                def onehot(pair):
                    nc.vector.tensor_tensor(one[:], slots, bc(k.place[:, :, bass.ds(pair * 2, 2)], 3, CAP),
                                            ALU.is_equal).then_inc(s_pm, 1)

                def gated(pair):
                    nc.vector.tensor_tensor(gone[:], one[:], bc(k.gates[:, :, bass.ds(pair * 2, 2)], 3, CAP),
                                            ALU.mult).then_inc(s_pg, 1)

                def add(base):
                    for o in range(4):
                        dve.wait_ge(s_sc, base + (o + 1))
                        xs = k.x[:, o // 2, (o % 2) * W:(o % 2 + 1) * W]
                        nc.vector.tensor_tensor(xs, xs, scatter_bank[o], ALU.add).then_inc(s_add, 1)

                nc.vector.memset(y[:], 0.0).then_inc(s_ys, 2)
                nc.vector.memset(goneT[:], 0.0).then_inc(s_pgs, 1)
                nc.vector.tensor_scalar(k.x[:], k.x[:], alpha, None, ALU.mult).then_inc(s_x, 1)
                nc.vector.tensor_tensor(one[:], slots, bc(k.place[:, :, 0:2], 3, CAP), ALU.is_equal).then_inc(s_pm, 1)
                dve.wait_ge(s_x, 1)
                dve.wait_ge(s_pm, 1)
                nc.vector.tensor_tensor(gone[:], one[:], bc(k.gates[:, :, 0:2], 3, CAP), ALU.mult).then_inc(s_pg, 1)
                with nc.vector.Fori(0, NI) as it:
                    dve.wait_ge(s_gx, it * 2 + 2)
                    dve.wait_ge(s_pg, it + 1)
                    onehot(it + 1)
                    dve.wait_ge(s_u, it + 1)
                    dve.wait_ge(s_sg, it + 1)
                    nc.vector.tensor_tensor(hid[:], sg[:], Up[:, 0:H], ALU.mult).then_inc(s_hid, 1)
                    add(it * 4)
                    dve.wait_ge(s_pm, it + 2)
                    dve.wait_ge(s_pt, it + 1)
                    gated(it + 1)
                    dve.wait_ge(s_add, it * 4 + 4)
                add(4 * NI)
    k.scope = k.ctx


def stage_general(k, tag, H, w_gate, w_up, w_down):
    nc = k.nc
    HT = H // P
    NP2 = HT // 2
    NI = NE // 2
    s_lg, s_lu, s_ld = ([k.sem(f"{n}_{tag}{b}") for b in range(2)] for n in
                        ("w_gate_loaded", "w_up_loaded", "w_down_loaded"))
    s_g, s_u, s_sg, s_hid, s_dn, s_yp, s_y, s_used = (k.sem(f"{n}_{tag}") for n in (
        "gate_product", "up_product", "silu_done", "hidden_done", "down_used", "down_product", "y_added",
        "up_used"))
    scope = ExitStack()
    k.scope = scope
    with scope:
        wg = [k.sb(f"w_gate_{tag}{b}", [P, KC, H]) for b in range(2)]
        wu = [k.sb(f"w_up_{tag}{b}", [P, KC, H]) for b in range(2)]
        wd = [k.sb(f"w_down_{tag}{b}", [P, HT, D]) for b in range(2)]
        sg = k.sb(f"silu_{tag}", [P, NP2, 2 * T])
        hid = [k.sb(f"hid_{tag}{b}", [P, NP2, 2 * T]) for b in range(2)]
        pg = k.ps(f"gate_ps_{tag}", [P, NP2, 2 * T])
        pu = k.ps(f"up_ps_{tag}", [P, NP2, 2 * T])
        py = k.ps(f"y_ps_{tag}", [P, NJ, 2, W])
        vg = w_gate.rearrange("e (p c) n -> e p c n", c=KC)
        vu = w_up.rearrange("e (p c) n -> e p c n", c=KC)
        vd = w_down.rearrange("e (c p) n -> e p c n", p=P)
        with nc.Block() as block:
            @block.sync
            def _(sp):
                def load(b, e):
                    sp.dma_start(wg[b][:], vg[e]).then_inc(s_lg[b], 16)
                    sp.dma_start(wu[b][:], vu[e]).then_inc(s_lu[b], 16)

                for b in range(2):
                    load(b, b)
                    sp.dma_start(wd[b][:], vd[b]).then_inc(s_ld[b], 16)
                with nc.sync.Fori(1, NI) as it:
                    for b in range(2):
                        sp.wait_ge(s_used, it * 2 + (b - 1))
                        load(b, it * 2 + b)
                        sp.wait_ge(s_dn, it * 2 + (b + 1))
                        sp.dma_start(wd[b][:], vd[it * 2 + b]).then_inc(s_ld[b], 16)

            @block.tensor
            def _(pe):
                pe.sem_inc(s_dn, 2)
                with nc.tensor.Fori(0, NI) as it:
                    for b in range(2):
                        for pr in range(NP2):
                            pe.wait_ge(s_hid, it * (2 * NP2) + (b * NP2 + pr + 1))
                            for w, ps, s_l, s_p in ((wg, pg, s_lg, s_g), (wu, pu, s_lu, s_u)):
                                if pr == 0:
                                    pe.wait_ge(s_l[b], it * 16 + 16)
                                for m in range(2):
                                    for c in range(KC):
                                        n0 = (2 * pr + m) * P
                                        last = nc.tensor.matmul(ps[:, pr, m * T:(m + 1) * T],
                                                                w[b][:, c, n0:n0 + P], k.hT[:, c, :],
                                                                start=(c == 0), stop=(c == KC - 1))
                                last.then_inc(s_p, 1)
                        pe.wait_ge(s_u, it * (2 * NP2) + (b + 1) * NP2)
                        pe.sem_inc(s_used, 1)
                        pe.wait_ge(s_ld[b], it * 16 + 16)
                        pe.wait_ge(s_hid, it * (2 * NP2) + (b + 2) * NP2)
                        for j in range(NJ):
                            for n in range(2):
                                g = 2 * j + n
                                pe.wait_ge(s_y, it * 8 + (4 * b + g + 1))
                                for m in range(HT):
                                    hm = hid[b][:, m // 2, (m % 2) * T + j * P:(m % 2) * T + (j + 1) * P]
                                    last = nc.tensor.matmul(py[:, j, n, :], hm, wd[b][:, m, n * W:(n + 1) * W],
                                                            start=(m == 0), stop=(m == HT - 1))
                                last.then_inc(s_yp, 1)
                        pe.wait_ge(s_yp, it * 8 + (4 * b + 4))
                        pe.sem_inc(s_dn, 1)

            @block.scalar
            def _(act):
                with nc.scalar.Fori(0, NI) as it:
                    for b in range(2):
                        for pr in range(NP2):
                            n = it * (2 * NP2) + (b * NP2 + pr + 1)
                            act.wait_ge(s_hid, n)
                            act.wait_ge(s_g, n)
                            nc.scalar.activation(sg[:, pr], pg[:, pr], ACT.Silu).then_inc(s_sg, 1)

            @block.vector
            def _(dve):
                dve.sem_inc(s_hid, NP2)
                dve.sem_inc(s_y, 4)
                with nc.vector.Fori(0, NI) as it:
                    for b in range(2):
                        dve.wait_ge(s_dn, it * 2 + (b + 1))
                        for pr in range(NP2):
                            n = it * (2 * NP2) + (b * NP2 + pr + 1)
                            dve.wait_ge(s_u, n)
                            dve.wait_ge(s_sg, n)
                            nc.vector.tensor_tensor(hid[b][:, pr], sg[:, pr], pu[:, pr], ALU.mult).then_inc(s_hid, 1)
                        for j in range(NJ):
                            for h in range(2):
                                n = it * 8 + (4 * b + 2 * j + h + 1)
                                dve.wait_ge(s_y, n)
                                dve.wait_ge(s_yp, n)
                                xs = k.x[:, j, h * W:(h + 1) * W]
                                nc.vector.scalar_tensor_tensor(
                                    out=xs, in0=py[:, j, h, :], scalar=k.over[:, j, bass.ds(it * 2 + b, 1)],
                                    in1=xs, op0=ALU.mult, op1=ALU.add).then_inc(s_y, 1)
                dve.wait_ge(s_y, 4 * NE + 4)
    k.scope = k.ctx


def stage_even_project(k):
    nc, i = k.nc, k.i
    N = i["w_in_even"].shape[1]
    k.en = k.sb("even_nat", [P, NJ, N])
    s_w = [k.sem(f"w_even_loaded{b}") for b in range(3)]
    s_p, s_o = k.sem("even_product"), k.sem("even_out")
    scope = ExitStack()
    k.scope = scope
    src = i["w_in_even"].rearrange("(p c) n -> p c n", c=KC)
    cuts = [(n, min(W, N - n)) for n in range(0, N, W)]
    with scope:
        w = [k.sb(f"w_even{b}", [P, KC, W]) for b in range(3)]
        ps = k.ps("even_ps", [P, 2, NJ, W])
        with nc.Block() as block:
            @block.sync
            def _(sp):
                for n, (a, width) in enumerate(cuts):
                    if n >= 3:
                        sp.wait_ge(s_p, n - 2)
                    sp.dma_start(w[n % 3][:, :, 0:width], src[:, :, a:a + width]).then_inc(s_w[n % 3], 16)

            @block.tensor
            def _(pe):
                for n, (a, width) in enumerate(cuts):
                    pe.wait_ge(s_w[n % 3], 16 * (n // 3 + 1))
                    if n >= 2:
                        pe.wait_ge(s_o, n - 1)
                    for j in range(NJ):
                        for c in range(KC):
                            last = nc.tensor.matmul(ps[:, n % 2, j, 0:width], k.hT[:, c, j * P:(j + 1) * P],
                                                    w[n % 3][:, c, 0:width], start=(c == 0), stop=(c == KC - 1))
                    last.then_inc(s_p, 1)

            @block.scalar
            def _(act):
                for n, (a, width) in enumerate(cuts):
                    act.wait_ge(s_p, n + 1)
                    nc.scalar.activation(k.en[:, :, a:a + width], ps[:, n % 2, :, 0:width], ACT.Copy).then_inc(s_o, 1)
    k.scope = k.ctx


def stage_even_mix(k):
    nc, i = k.nc, k.i
    RD = 128
    k.mix = k.sb("even_mix", [P, NJ, D])
    names = ("tables", "rot_a", "rot_b", "rot_c", "rot_d", "rotated", "turned", "turned_out", "lg_abs", "lg_exp",
             "lg_ln", "dist", "dist_exp", "ret_scores", "ret_weighted", "ret_product", "win_scores", "win_masked",
             "win_diff", "win_exp", "p_turned", "p_out", "win_product", "sink_diff", "ret_out", "gn_sq", "gn_inv",
             "gn_rstd", "silu")
    s = {n: k.sem(f"even_{n}") for n in names}
    scope = ExitStack()
    k.scope = scope
    with scope:
        tb = k.sb("even_tab", [P, ROPE_N + 6 * T])
        lgt = k.sb("ret_logit", [P, 2 * RET_H])
        lga = k.sb("ret_logit_abs", [P, 2 * RET_H])
        gn = k.sb("ret_gain", [P, W])
        sink = k.sb("sink", [P, WIN_H])
        rot = k.sb("rotated", [P, NJ, W * 2 + 640])
        ta = k.sb("rot_tmp", [P, NJ, 8, 64])
        tc_ = k.sb("rot_tmp2", [P, NJ, 8, 64])
        rT = k.sb("ret_T", [P, 8, T])
        wT = k.sb("win_T", [P, 5, T])
        dm = k.sb("ret_decay", [P, RET_H, NJ * T])
        st = k.sb("ret_weights", [P, RET_H, NJ, T])
        sc = k.sb("win_scores_sb", [P, WIN_H, NJ, T])
        pT = k.sb("win_pT", [P, WIN_H, NJ, T])
        ya = k.sb("ret_y", [P, NJ, RET_H, RD])
        sq = k.sb("ret_sq", [P, NJ, RET_H, RD])
        sm = k.sb("even_small", [P, 10, NJ, WIN_H])
        pb = [k.ps(f"even_ps{b}", [P, W]) for b in range(8)]
        o64 = 2 * 64 * NJ
        cos = {64: tb[:, 0:64 * NJ], 32: tb[:, o64:o64 + 32 * NJ]}
        sin = {64: tb[:, 64 * NJ:o64], 32: tb[:, o64 + 32 * NJ:ROPE_N]}
        ahead, behind = tb[:, ROPE_N:ROPE_N + 2 * T], tb[:, ROPE_N + 2 * T:ROPE_N + 4 * T]
        wmask = tb[:, ROPE_N + 4 * T:]
        groups = [(0, 8, 64, 0, 128), (4 * W, 4, 32, 2 * W, 128), (4 * W + 256, 4, 32, 2 * W + 64, 128),
                  (5 * W, 2, 32, 2 * W + 512, 64)]

        def halves(x, a, n, half, j, step):
            if step == 2 * half:
                v = x[:, j, a:a + n * step].rearrange("p (h s d) -> p h s d", h=n, s=2)
                return v[:, :, 0], v[:, :, 1]
            at = 2 * W + (a - 2 * W) % step
            v = x[:, j, 2 * W:2 * W + n * step].rearrange("p (h s) -> p h s", h=n)
            return v[:, :, at - 2 * W:at - 2 * W + half], v[:, :, at - 2 * W + half:at - 2 * W + 2 * half]

        def angle(t, half, j, n):
            return bc(t[half][:, j * half:(j + 1) * half], 1, n)

        def turn_list():
            out = []
            for h in range(8):
                out.append((h // 2, (h % 2) * 2, lambda j, h=h: rot[:, j, h * RD:(h + 1) * RD]))
            for m in range(4):
                out.append((4 + m // 2, (m % 2) * 2,
                            lambda j, m=m: rot[:, j, 2 * W + m * P:2 * W + (m + 1) * P]))
            out.append((6, 0, lambda j: rot[:, j, 2 * W + 512:2 * W + 640]))
            return out

        with nc.Block() as block:
            @block.sync
            def _(sp):
                sp.dma_start(tb[:], i["even_tables"]).then_inc(s["tables"], 16)
                sp.dma_start(lgt[:], i["ret_decay_logit"].broadcast_to([P, 2 * RET_H])).then_inc(s["tables"], 16)
                sp.dma_start(gn[:], i["ret_gn_gain"].broadcast_to([P, W])).then_inc(s["tables"], 16)
                sp.dma_start(sink[:], i["sink_logit"].broadcast_to([P, WIN_H])).then_inc(s["tables"], 16)

            @block.gpsimd
            def _(pool):
                o = Order(pool, k.order["pool"])
                pool.wait_ge(s["tables"], 64)
                tt = nc.gpsimd.tensor_tensor
                for a, n, half, b, step in groups:
                    for j in range(NJ):
                        x1, x2 = halves(k.en, a, n, half, j, 2 * half)
                        _, y2 = halves(rot, b, n, half, j, step)
                        t1 = tc_[:, j, 0:n, 0:half]
                        o(tt(t1, x1, angle(sin, half, j, n), ALU.mult))
                        o(tt(y2, x2, angle(cos, half, j, n), ALU.mult))
                        o(tt(y2, y2, t1, ALU.add))
                pool.sem_inc(s["rotated"], 1)
                o.restart()

            @block.vector
            def _(dve):
                o = Order(dve, k.order["dve"])
                tt, ts, stt = nc.vector.tensor_tensor, nc.vector.tensor_scalar, nc.vector.scalar_tensor_tensor
                red = nc.vector.tensor_reduce
                dve.wait_ge(s["tables"], 64)
                o(ts(lga[:], lgt[:], -1.0, None, ALU.mult))
                tt(lga[:], lga[:], lgt[:], ALU.max).then_inc(s["lg_abs"], 1)
                for a, n, half, b, step in groups:
                    for j in range(NJ):
                        x1, x2 = halves(k.en, a, n, half, j, 2 * half)
                        y1, _ = halves(rot, b, n, half, j, step)
                        t1 = ta[:, j, 0:n, 0:half]
                        o(tt(t1, x2, angle(sin, half, j, n), ALU.mult))
                        o(tt(y1, x1, angle(cos, half, j, n), ALU.mult))
                        o(tt(y1, y1, t1, ALU.subtract))
                dve.sem_inc(s["rotated"], 1)
                dve.wait_ge(s["lg_ln"], 1)
                o(ts(lgt[:], lgt[:], 0.0, None, ALU.min))
                o(tt(lgt[:], lgt[:], lga[:], ALU.subtract))
                for h in range(RET_H):
                    o(ts(dm[:, h], ahead, lgt[:, h:h + 1], None, ALU.mult))
                    stt(out=dm[:, h], in0=behind, scalar=lgt[:, RET_H + h:RET_H + h + 1], in1=dm[:, h],
                        op0=ALU.mult, op1=ALU.add).then_inc(s["dist"], 1)
                for h in range(RET_H):
                    dve.wait_ge(s["ret_scores"], h + 1)
                    dve.wait_ge(s["dist_exp"], h + 1)
                    tt(st[:, h].rearrange("p a t -> p (a t)"), pb[h][:], dm[:, h], ALU.mult).then_inc(s["ret_weighted"], 1)
                for h in range(WIN_H):
                    dve.wait_ge(s["win_scores"], h + 1)
                    tt(sc[:, h].rearrange("p a t -> p (a t)"), pb[4 + h % 4][:], wmask, ALU.add).then_inc(s["win_masked"], 1)
                dve.wait_ge(s["win_masked"], WIN_H)
                hj = "p a h -> p h a"
                o(red(sm[:, 0].rearrange(hj), sc[:], AX.X, ALU.max))
                o(tt(sm[:, 0], sm[:, 0], bc(sink[:], 1, NJ), ALU.max))
                o(tt(sm[:, 1], bc(sink[:], 1, NJ), sm[:, 0], ALU.subtract))
                for j in range(NJ):
                    tt(sc[:, :, j], sc[:, :, j], bc(sm[:, 0, j], 2, T), ALU.subtract).then_inc(s["win_diff"], 1)
                dve.wait_ge(s["ret_product"], 1)
                yp = pb[0][:].rearrange("p (h d) -> p h d", h=RET_H), pb[1][:].rearrange("p (h d) -> p h d", h=RET_H)
                for j in range(NJ):
                    o(nc.vector.tensor_copy(ya[:, j], yp[j]))
                o(red(sm[:, 2, :, 0:RET_H], ya[:], AX.X, ALU.add))
                o(ts(sm[:, 2, :, 0:RET_H], sm[:, 2, :, 0:RET_H], 1.0 / RD, None, ALU.mult))
                o(tt(ya[:], ya[:], bc(sm[:, 2, :, 0:RET_H], 3, RD), ALU.subtract))
                o(tt(sq[:], ya[:], ya[:], ALU.mult))
                o(red(sm[:, 3, :, 0:RET_H], sq[:], AX.X, ALU.add))
                o(ts(sm[:, 3, :, 0:RET_H], sm[:, 3, :, 0:RET_H], 1.0 / RD, GN_EPS, ALU.mult, ALU.add))
                nc.vector.reciprocal(sm[:, 4, :, 0:RET_H], sm[:, 3, :, 0:RET_H]).then_inc(s["gn_inv"], 1)
                dve.wait_ge(s["gn_rstd"], 1)
                refine(nc, o, sm[:, 5, :, 0:RET_H], sm[:, 3, :, 0:RET_H], sm[:, 4, :, 0:RET_H])
                o(tt(ya[:], ya[:], bc(sm[:, 5, :, 0:RET_H], 3, RD), ALU.mult))
                ma = k.mix[:, :, 0:W]
                o(tt(ma, ya[:].rearrange("p j h d -> p j (h d)"), bc(gn[:], 1, NJ), ALU.mult))
                dve.wait_ge(s["silu"], 1)
                o(tt(ma, ma, k.en[:, :, 3 * W:4 * W], ALU.mult))
                dve.wait_ge(s["win_exp"], 3)
                o(red(sm[:, 6].rearrange(hj), sc[:], AX.X, ALU.add))
                o(tt(sm[:, 6], sm[:, 6], sm[:, 7], ALU.add))
                o(nc.vector.reciprocal(sm[:, 8], sm[:, 6]))
                for h in range(WIN_H):
                    if h % 2:
                        dve.wait_ge(s["p_turned"], h + 1)
                        nc.vector.tensor_copy(pT[:, h].rearrange("p a t -> p (a t)"), pb[h][:]).then_inc(s["p_out"], 1)
                dve.wait_ge(s["win_product"], 1)
                for j in range(NJ):
                    o(tt(k.mix[:, j, W:].rearrange("p (h d) -> p h d", h=WIN_H),
                         pb[6 + j][:].rearrange("p (h d) -> p h d", h=WIN_H), bc(sm[:, 8, j], 2, WIN_D), ALU.mult))
                o.restart()

            @block.scalar
            def _(act):
                act.wait_ge(s["lg_abs"], 1)
                nc.scalar.activation(lga[:], lga[:], ACT.Exp, scale=-1.0).then_inc(s["lg_exp"], 1)
                act.wait_ge(s["lg_exp"], 1)
                nc.scalar.activation(lga[:], lga[:], ACT.Ln, bias=1.0).then_inc(s["lg_ln"], 1)
                for b in range(7):
                    act.wait_ge(s["turned"], b + 1)
                    got = pb[b][:].rearrange("p (h t) -> p h t", h=2)
                    if b < 4:
                        dst, scale = rT[:, 2 * b:2 * b + 2], (1.0 if b < 2 else RD ** -0.5)
                    elif b < 6:
                        dst, scale = wT[:, 2 * (b - 4):2 * (b - 4) + 2], WIN_D ** -0.5
                    else:
                        dst, scale, got = wT[:, 4:5], 1.0, got[:, 0:1]
                    nc.scalar.activation(dst, got, ACT.Copy, scale=scale).then_inc(s["turned_out"], 1)
                for h in range(RET_H):
                    act.wait_ge(s["dist"], h + 1)
                    nc.scalar.activation(dm[:, h], dm[:, h], ACT.Exp).then_inc(s["dist_exp"], 1)
                act.wait_ge(s["win_diff"], 2)
                nc.scalar.activation(sc[:], sc[:], ACT.Exp).then_inc(s["win_exp"], 2)
                nc.scalar.activation(sm[:, 7], sm[:, 1], ACT.Exp).then_inc(s["win_exp"], 1)
                act.wait_ge(s["gn_inv"], 1)
                nc.scalar.activation(sm[:, 5, :, 0:RET_H], sm[:, 4, :, 0:RET_H], ACT.Sqrt).then_inc(s["gn_rstd"], 1)
                nc.scalar.activation(k.en[:, :, 3 * W:4 * W], k.en[:, :, 3 * W:4 * W], ACT.Silu).then_inc(s["silu"], 1)
                for h in range(0, WIN_H, 2):
                    act.wait_ge(s["p_turned"], h + 1)
                    nc.scalar.activation(pT[:, h].rearrange("p a t -> p (a t)"), pb[h][:], ACT.Copy).then_inc(s["p_out"], 1)

            @block.tensor
            def _(pe):
                mm = nc.tensor.matmul
                pe.wait_ge(s["rotated"], 2)
                turns = turn_list()
                for n, (b, place, cols) in enumerate(turns):
                    for j in range(NJ):
                        last = nc.tensor.transpose(pb[b][:, (place + j) * P:(place + j + 1) * P], cols(j), k.table("ident"))
                    if n == len(turns) - 1 or turns[n + 1][0] != b:
                        last.then_inc(s["turned"], 1)
                pe.wait_ge(s["turned_out"], 7)
                for h in range(RET_H):
                    for sj in range(NJ):
                        last = mm(pb[h][:, sj * T:(sj + 1) * T], rT[:, RET_H + h, sj * P:(sj + 1) * P], rT[:, h, :],
                                  start=True, stop=True)
                    last.then_inc(s["ret_scores"], 1)
                for h in range(WIN_H):
                    m, r = h % 4, slice(64 * (h // 4), 64 * (h // 4) + 64)
                    if h >= 4:
                        pe.wait_ge(s["win_masked"], h - 3)
                    for j in range(NJ):
                        last = mm(pb[4 + h % 4][:, j * T:(j + 1) * T], wT[r, m, j * P:(j + 1) * P], wT[r, 4, :],
                                  start=True, stop=True)
                    last.then_inc(s["win_scores"], 1)
                pe.wait_ge(s["ret_weighted"], RET_H)
                for j in range(NJ):
                    for h in range(RET_H):
                        for sj in range(NJ):
                            last = mm(pb[j][:, h * RD:(h + 1) * RD], st[:, h, sj, j * P:(j + 1) * P],
                                      k.en[:, sj, 2 * W + h * RD:2 * W + (h + 1) * RD],
                                      start=(sj == 0), stop=(sj == NJ - 1))
                last.then_inc(s["ret_product"], 1)
                pe.wait_ge(s["win_exp"], 3)
                pe.wait_ge(s["gn_inv"], 1)
                for h in range(WIN_H):
                    for sj in range(NJ):
                        for j in range(NJ):
                            last = nc.tensor.transpose(pb[h][:, sj * T + j * P:sj * T + (j + 1) * P],
                                                       sc[:, h, j, sj * P:(sj + 1) * P], k.table("ident"))
                    last.then_inc(s["p_turned"], 1)
                pe.wait_ge(s["p_out"], WIN_H)
                for j in range(NJ):
                    for h in range(WIN_H):
                        kv = h // 4
                        for sj in range(NJ):
                            last = mm(pb[6 + j][:, h * WIN_D:(h + 1) * WIN_D], pT[:, h, sj, j * P:(j + 1) * P],
                                      k.en[:, sj, 5 * W + 128 + kv * WIN_D:5 * W + 128 + (kv + 1) * WIN_D],
                                      start=(sj == 0), stop=(sj == NJ - 1))
                last.then_inc(s["win_product"], 1)
    k.scope = k.ctx


def stage_fourier(k):
    nc = k.nc
    s_t, s_a, s_ao, s_b = (k.sem(f"dft_{n}") for n in ("loaded", "rows_product", "rows_out", "columns_product"))
    scope = ExitStack()
    k.scope = scope
    with scope:
        tab = k.sb("dft_tab", [P, NJ, 2, T])
        a = k.sb("dft_rows", [P, KC, 2, T])
        ps = [k.ps(f"dft_ps{b}", [P, 2, T]) for b in range(8)]
        with nc.Block() as block:
            @block.sync
            def _(sp):
                sp.dma_start(tab[:], k.i["dft"]).then_inc(s_t, 16)

            @block.tensor
            def _(pe):
                pe.wait_ge(s_t, 16)
                for c in range(KC):
                    for j in range(NJ):
                        last = nc.tensor.matmul(ps[c][:], k.x[:, j, c * P:(c + 1) * P], tab[:, j],
                                                start=(j == 0), stop=(j == NJ - 1))
                    last.then_inc(s_a, 1)
                for g in range(KC // 2):
                    pe.wait_ge(s_ao, 4 * (g + 1))
                    for o in range(2):
                        n = 0
                        for f in range(2):
                            for q in range(2):
                                last = nc.tensor.matmul(ps[2 * g + o][:, 0, :], tab[:, q, f, o * P:(o + 1) * P],
                                                        a[:, 2 * g + q, f, :], start=(n == 0), stop=(n == 3))
                                n += 1
                        last.then_inc(s_b, 1)

            @block.scalar
            def _(act):
                for c in range(KC):
                    act.wait_ge(s_a, c + 1)
                    nc.scalar.activation(a[:, c, 0], ps[c][:, 0], ACT.Copy).then_inc(s_ao, 1)
                    nc.scalar.activation(a[:, c, 1], ps[c][:, 1], ACT.Copy, scale=-1.0).then_inc(s_ao, 1)
                for c in range(KC):
                    act.wait_ge(s_b, c + 1)
                    nc.scalar.activation(k.hT[:, c, :], ps[c][:, 0], ACT.Copy, scale=1.0 / T)
    k.scope = k.ctx


def stage_store(k):
    s_o = k.sem("stored")
    with k.nc.Block() as block:
        @block.sync
        def _(sp):
            sp.dma_start(k.out.rearrange("a (j p) d -> p (a j) d", p=P), k.x[:]).then_inc(s_o, 16)
            sp.wait_ge(s_o, 16)


def build(nc, ins, out):
    with ExitStack() as ctx:
        k = Core(nc, ins, out, ctx)
        i = ins
        stage_load(k)
        k.live = []
        k.gates = k.sb("gates", [P, NJ, NE + 2])
        k.place = k.sb("place", [P, NJ, NE + 2])
        k.over = k.sb("over", [P, NJ, NE])
        k.over_flag = k.sb("over_flag", [1, 1], I32)
        with ExitStack() as mixer:
            k.ctx2, k.ctx = k.ctx, mixer
            k.scope = mixer
            hn = k.sb("h1_rows", [P, NJ, D])
            stage_norm_t(k, "n1", k.x, i["norm1_w"], hn)
            stage_project(k)
            stage_gates(k)
            stage_gla(k)
            stage_gdn(k)
            stage_combine(k)
            stage_norm_t(k, "mix1", k.oa, None, None)
            k.ctx = k.ctx2
            k.scope = k.ctx
        with ExitStack() as room:
            k.scope = room
            stage_out(k, "one", i["w_out"][0].rearrange("(p c) n -> p c n", c=KC), 1.0)
        k.h_rows = k.sb("h_rows", [P, NJ, D])
        stage_norm_t(k, "n2", k.x, i["norm2_w"], k.h_rows)
        k.retire()
        stage_router(k, "one", i["moe_w_group"][0], i["moe_w_router"][0])
        stage_experts(k, "one", H1, i["moe_w_gate"][0], i["moe_w_up"][0], i["moe_w_down"][0], 1.0)
        stage_norm(k, "f", i["norm_f_w"])
        for layer in range(2):
            k.retire()
            if layer == 0:
                stage_norm_t(k, "e", k.x, None, None)
                with ExitStack() as mixer:
                    k.ctx2, k.ctx = k.ctx, mixer
                    k.scope = mixer
                    stage_even_project(k)
                    stage_even_mix(k)
                    stage_norm_t(k, "mix2", k.mix, None, None)
                    k.ctx = k.ctx2
                    k.scope = k.ctx
                stage_out(k, "even", i["w_out_even"].rearrange("(p c) n -> p c n", c=KC), ALPHA)
            else:
                stage_fourier(k)
                stage_out(k, "fourier", i["w_out_fourier"].rearrange("(c p) n -> p c n", p=P), ALPHA)
            stage_norm(k, f"a{layer}", i["ln1_gain"][layer:layer + 1], i["ln1_bias"][layer:layer + 1])
            stage_norm_t(k, f"moe{layer}", k.x, None, k.h_rows)
            stage_router(k, f"l{layer}", i["router_coarse_w"][layer], i["router_fine_w"][layer],
                         i["router_coarse_b"][layer:layer + 1], i["router_fine_b"][layer:layer + 1])
            stage_experts(k, f"l{layer}", H2, i["expert_w_gate"][layer], i["expert_w_up"][layer],
                          i["expert_w_down"][layer], ALPHA)
            stage_norm(k, f"b{layer}", i["ln2_gain"][layer:layer + 1], i["ln2_bias"][layer:layer + 1])
        stage_store(k)


def lay_out(inputs):
    a = {n: np.ascontiguousarray(v) for n, v in inputs.items()}
    w = a["w_in"][0]
    starts = ([0, 512]
              + [3104 + W * n for n in range(6)]
              + [1024, 1536, 2048, 2560]
              + [6176, 6688] + [7232, 7744, 8256, 8768])
    g = 3 * GDN_H
    return {
        "x": a["x"], "norm1_w": a["norm1_w"], "norm2_w": a["norm2_w"], "tables": tables(),
        "w_in_blocks": np.ascontiguousarray(np.stack([w[:, s:s + W] for s in starts])),
        "w_in_small": np.ascontiguousarray(np.concatenate([w[:, 3072:3104], w[:, 7200:7232]], 1)),
        "conv_w": np.ascontiguousarray(
            a["gdn_conv_w"][0].T.reshape(g, P, TAPS).transpose(1, 0, 2).reshape(P, g * TAPS)),
        **{n: a[n] for n in ("gla_gate_w2_fwd", "gla_gate_w2_bwd", "gla_gate_b_fwd", "gla_gate_b_bwd",
                             "gdn_a_log_fwd", "gdn_a_log_bwd", "gdn_dt_bias_fwd", "gdn_dt_bias_bwd",
                             "gla_norm_w", "gdn_norm_w", "w_out", "moe_w_group", "moe_w_router",
                             "moe_w_gate", "moe_w_up", "moe_w_down")},
        "norm_f_w": a["norm_f_w"].reshape(1, D),
        "w_in_even": a["w_in_even_2"][0], "w_out_even": a["w_out_even_2"][0],
        "w_out_fourier": a["w_out_fourier_2"][0],
        "even_tables": even_tables(), "dft": dft_table(),
        "ret_decay_logit": a["ret_decay_logit_2"].reshape(1, 2 * RET_H),
        "ret_gn_gain": a["ret_gn_gain_2"], "sink_logit": a["sink_logit_2"],
        "router_coarse_w": a["router_coarse_w_2"], "router_coarse_b": a["router_coarse_b_2"],
        "router_fine_w": a["router_fine_w_2"], "router_fine_b": a["router_fine_b_2"],
        "expert_w_gate": a["expert_w_gate_2"], "expert_w_up": a["expert_w_up_2"],
        "expert_w_down": a["expert_w_down_2"],
        "ln1_gain": a["ln1_gain_2"], "ln1_bias": a["ln1_bias_2"],
        "ln2_gain": a["ln2_gain_2"], "ln2_bias": a["ln2_bias_2"],
    }


def kernel(**inputs):
    import concourse.bacc as bacc
    from concourse.bass_utils import run_bass_kernel_spmd

    nc = bacc.Bacc("TRN2", target_bir_lowering=False, num_devices=1)
    arrays, args = {}, {}
    for name, a in lay_out(inputs).items():
        arrays[f"in_{name}"] = a
        args[name] = nc.dram_tensor(f"in_{name}", a.shape, F32, kind="ExternalInput").ap()
    out = nc.dram_tensor("out", (1, T, D), F32, kind="ExternalOutput").ap()
    build(nc, args, out)
    r = run_bass_kernel_spmd(nc, [arrays], core_ids=[0])
    return r.results[0]["out"]
```

```python
from contextlib import ExitStack

import numpy as np

import concourse.bass as bass
from concourse import mybir

ALU = mybir.AluOpType
ACT = mybir.ActivationFunctionType
AX = mybir.AxisListType
F32 = mybir.dt.float32
I32 = mybir.dt.int32

P = 128
T = 256
NJ = T // P
D = 1024
KC = D // P
W = 512
EPS = 1e-6
CH = 64

GLA_H, GLA_DK, GLA_DV, RANK, TAU = 4, 128, 256, 16, 16.0
GDN_H, GDN_D, TAPS = 8, 128, 5
NG, NE, EPG = 4, 32, 8
H1, H2 = 256, 512
RET_H, WIN_H, WIN_KV, WIN_D = 4, 8, 2, 64
ALPHA = 4.0 ** 0.25
LN_EPS, GN_EPS = 1e-5, 1e-6
NT_BLOCKS, NN_BLOCKS = 8, 10
BIG = 1e30
CAP = 64


class Order:

    def __init__(self, eng, sem):
        self.eng, self.sem, self.n = eng, sem, 0

    def __call__(self, ins):
        self.n += 1
        ins.then_inc(self.sem, 1)
        self.eng.wait_ge(self.sem, self.n)

    def restart(self):
        self.eng.sem_clear(self.sem)
        self.n = 0


LEVELS = 6
TABLE = dict(ident=P, ones=P, cum=2 * P, blk=P, half=2 * P, strictn=2 * P, incl=2 * P,
             lev=LEVELS * 2 * P, lev0=2 * P, rank=NG + NE,
             before=P, slot=CAP)
OFF = {}
_at = 0
for _k, _n in TABLE.items():
    OFF[_k] = _at
    _at += _n
TABLE_N = _at


def tables():
    p = np.arange(P)[:, None]
    x = np.arange(P)[None, :]
    same = (p // CH) == (x // CH)
    f = lambda m: m.astype(np.float32)
    out = dict(
        ident=f(p == x), ones=np.ones((P, P), np.float32),
        cum=np.concatenate([f(same & (p <= x)), f(same & (p >= x))], 1),
        blk=f(same),
        half=np.concatenate([f((p < CH) & (x >= 0)), f((p >= CH) & (x >= 0))], 1),
        strictn=np.concatenate([-f(same & (x < p)), -f(same & (x > p))], 1),
        incl=np.concatenate([f(same & (p <= x)), f(same & (p >= x))], 1),
    )
    lev = []
    for l in range(LEVELS):
        pair = (p >> (l + 1)) == (x >> (l + 1))
        lev.append(f(pair & (((p >> l) & 1) == 0) & (((x >> l) & 1) == 1)))
        lev.append(f(pair & (((p >> l) & 1) == 1) & (((x >> l) & 1) == 0)))
    out["lev"] = np.concatenate(lev, 1)
    out["lev0"] = np.concatenate([lev[1], lev[0]], 1)
    out["rank"] = np.tile(np.concatenate([np.arange(NG, 0, -1), np.arange(NE, 0, -1)]).astype(np.float32), (P, 1))
    out["before"] = f(p < x)
    out["slot"] = np.tile(np.arange(CAP, dtype=np.float32), (P, 1))
    return np.ascontiguousarray(np.concatenate([out[k] for k in TABLE], 1))


def dft_table():
    t = np.arange(T)
    ang = 2 * np.pi * ((t[:, None] * t[None, :]) % T) / T
    both = np.stack([np.cos(ang), np.sin(ang)], 1).astype(np.float32)
    return np.ascontiguousarray(both.reshape(NJ, P, 2, T).transpose(1, 0, 2, 3))


ROPE_N = 2 * (64 + 32) * NJ


def even_tables():
    pos = np.arange(T, dtype=np.float32)
    parts = []
    for half in (64, 32):
        inv = np.float32(10000.0) ** (-np.arange(half, dtype=np.float32) / np.float32(half))
        ang = pos[:, None] * inv[None, :]
        for f in (np.cos, np.sin):
            parts.append(f(ang).astype(np.float32).reshape(NJ, P, half).transpose(1, 0, 2).reshape(P, -1))
    s, t = pos[:, None], pos[None, :]
    rows = lambda m: m.astype(np.float32).reshape(NJ, P, T).transpose(1, 0, 2).reshape(P, -1)
    parts += [rows(np.maximum(t - s, 0)), rows(np.maximum(s - t, 0)),
              rows(np.where(np.abs(s - t) <= P, 0.0, -BIG))]
    return np.ascontiguousarray(np.concatenate(parts, 1))


class Core:

    def __init__(self, nc, ins, out, ctx):
        self.nc, self.i, self.out, self.ctx = nc, ins, out, ctx
        self.live = None
        self.order = {e: self.sem(f"{e}_order") for e in ("dve", "act", "pool", "pe")}
        self.scope = ctx

    def sem(self, name):
        s = self.nc.alloc_semaphore(name=name)
        if self.live is not None:
            self.live.append(s)
        return s

    def retire(self):
        self.nc.all_engine_barrier()
        self.nc.clear_and_free_semaphores(self.live)
        self.nc.all_engine_barrier()
        self.live = []

    def sb(self, name, shape, dt=F32):
        return self.scope.enter_context(self.nc.sbuf_tensor(name, shape, dt))

    def ps(self, name, shape):
        return self.scope.enter_context(self.nc.psum_tensor(name, shape, F32))

    def carve(self, region, at, shape):
        n = int(np.prod(shape[1:]))
        assert at + n <= region.shape[1]
        flat = region[:, at:at + n]
        if len(shape) == 2:
            return flat
        names = "abcd"[:len(shape) - 1]
        return flat.rearrange(f"p ({' '.join(names)}) -> p {' '.join(names)}",
                              **dict(zip(names[1:], shape[2:])))

    def table(self, name, n=0):
        a = OFF[name] + n * P
        return self.tab[:, a:a + P]


def bc(ap, axis, n):
    shape = list(ap.shape)
    return ap.unsqueeze(axis).broadcast_to(shape[:axis] + [n] + shape[axis:])


def refine(nc, o, r, v, tmp):
    o(nc.vector.tensor_tensor(tmp, r, r, ALU.mult))
    o(nc.vector.tensor_tensor(tmp, tmp, v, ALU.mult))
    o(nc.vector.tensor_scalar(tmp, tmp, -0.5, 1.5, ALU.mult, ALU.add))
    o(nc.vector.tensor_tensor(r, r, tmp, ALU.mult))


def stage_load(k):
    nc, i = k.nc, k.i
    k.tab = k.sb("tables", [P, TABLE_N])
    k.x = k.sb("x", [P, NJ, D])
    k.hT = k.sb("hT", [P, KC, T])
    k.pool = k.sb("pool", [P, POOL_N])
    k.store = k.sb("store", [P, STORE_N])
    k.s_small = k.sem("small_loaded")
    with nc.Block() as block:
        @block.sync
        def _(sp):
            sp.dma_start(k.x[:], i["x"].rearrange("a (j p) d -> p (a j) d", p=P)).then_inc(k.s_small, 16)
            sp.dma_start(k.tab[:], i["tables"]).then_inc(k.s_small, 16)
            sp.wait_ge(k.s_small, 32)


def stage_norm_t(k, tag, src, weight, hn, ahead=None):
    nc = k.nc
    s_w, s_ss, s_inv, s_rs, s_h, s_t = (k.sem(f"{n}_{tag}") for n in (
        "norm_weight_loaded", "sumsq_done", "inv_done", "rstd_done", "h_done", "turned"))
    scope = ExitStack()
    k.scope = scope
    ss = k.sb(f"ss_{tag}", [P, NJ])
    inv = k.sb(f"inv_{tag}", [P, NJ])
    rstd = k.sb(f"rstd_{tag}", [P, NJ])
    turned = k.ps(f"turned_ps_{tag}", [P, 4, W])
    rows = hn if weight is not None else src
    wrow = k.sb(f"norm_row_{tag}", [P, D]) if weight is not None else None
    with scope, nc.Block() as block:
        @block.sync
        def _(sp):
            if ahead is not None:
                ahead(sp)
            if weight is not None:
                sp.dma_start(wrow[:], weight.broadcast_to([P, D])).then_inc(s_w, 16)

        @block.scalar
        def _(act):
            if weight is None:
                if hn is not None:
                    nc.scalar.activation(hn[:], src[:], ACT.Copy)
                return
            for j in range(NJ):
                nc.scalar.activation(hn[:, j, :], src[:, j, :], ACT.Square,
                                     accum_out=ss[:, j:j + 1]).then_inc(s_ss, 1)
            act.wait_ge(s_inv, 1)
            nc.scalar.activation(rstd[:], inv[:], ACT.Sqrt).then_inc(s_rs, 1)

        @block.vector
        def _(dve):
            o = Order(dve, k.order["dve"])
            if weight is not None:
                dve.wait_ge(s_ss, NJ)
                o(nc.vector.tensor_scalar(ss[:], ss[:], 1.0 / D, EPS, ALU.mult, ALU.add))
                nc.vector.reciprocal(inv[:], ss[:]).then_inc(s_inv, 1)
                dve.wait_ge(s_rs, 1)
                refine(nc, o, rstd[:], ss[:], inv[:])
                dve.wait_ge(s_w, 16)
                for j in range(NJ):
                    nc.vector.scalar_tensor_tensor(out=hn[:, j, :], in0=src[:, j, :], scalar=rstd[:, j:j + 1],
                                                   in1=wrow[:], op0=ALU.mult, op1=ALU.mult).then_inc(s_h, 1)
            for b in range(4):
                j, c0 = b // 2, 4 * (b % 2)
                dve.wait_ge(s_t, b + 1)
                dst = k.hT[:, c0:c0 + 4, j * P:(j + 1) * P]
                got = turned[:, b, :].rearrange("p (c t) -> p c t", c=4)
                nc.vector.tensor_copy(dst, got)
            o.restart()

        @block.tensor
        def _(pe):
            for b in range(4):
                j, c0 = b // 2, 4 * (b % 2)
                if weight is not None:
                    pe.wait_ge(s_h, j + 1)
                for c in range(4):
                    last = nc.tensor.transpose(turned[:, b, c * P:(c + 1) * P],
                                               rows[:, j, c0 + c:D:KC], k.table("ident"))
                last.then_inc(s_t, 1)
    k.scope = k.ctx


POOL_N, STORE_N = 24576, KC * D
AT_CONV, AT_LA, AT_QK, AT_FREE = 0, 3 * GDN_H * T, 3 * GDN_H * T + 2 * NJ * W, 3 * GDN_H * T + 2 * NJ * W + 2 * GLA_H * T


def stage_project(k):
    nc, i = k.nc, k.i
    k.qkT = k.carve(k.pool, AT_QK, [P, 2, GLA_H, T])
    k.conv = k.carve(k.pool, AT_CONV, [P, 3 * GDN_H, T])
    k.la = k.carve(k.pool, AT_LA, [P, 2, NJ, W])
    k.nat = k.sb("nat", [P, 5, NJ, 2 * W])
    small = [P, 2, NJ, GDN_H]
    k.g, k.gcum, k.eg, k.et, k.beta, k.beg = (k.sb(n, small) for n in (
        "g", "g_cum", "exp_g_cum", "exp_g_tail", "beta", "beta_exp_g"))
    k.dec = k.sb("chunk_decay", [P, 2, 2, NJ, GDN_H])
    PAD = TAPS // 2
    s_wf = [k.sem(f"w_in_loaded{b}") for b in range(2)]
    (s_ws, s_cw, s_ld, s_pad, s_prod, s_out, s_sm, s_smo, s_z, s_abs, s_log, s_mn, s_spz, s_spl, s_rate, s_be,
     s_g, s_sum, s_td, s_ge, s_conv, s_silu, s_sq, s_np, s_ni, s_ne) = (k.sem(n) for n in (
         "w_small_loaded", "conv_w_loaded", "gate_w_loaded", "pad_zeroed", "block_product", "block_out",
         "small_product", "small_out", "z_product", "z_abs", "z_log", "z_min", "softplus_z", "softplus_log",
         "rate_done", "beta_exp", "g_done", "g_sums", "tail_diff", "g_exps", "conv_done", "conv_silu",
         "squares_done", "norm_product", "norm_inv", "norm_done"))
    scope = ExitStack()
    k.scope = scope
    with scope:
        wbuf = [k.carve(k.pool, AT_FREE + b * KC * W, [P, KC, W]) for b in range(2)]
        wsm = k.sb("w_small", [P, KC, 64])
        cin = k.carve(k.store, 0, [P, 3 * GDN_H, T + 2 * PAD])
        at = AT_FREE + 2 * KC * W
        zabs = k.carve(k.pool, at, [P, 2, NJ, W])
        w2 = k.carve(k.pool, at + 4 * W, [P, 2, W])[0:RANK]
        gb = k.carve(k.store, 3 * GDN_H * (T + 2 * PAD), [P, 2, W])[0:1]
        rows = k.sb("gdn_rows", [P, 2, 2 * GDN_H])
        glrT = k.carve(k.pool, at + 6 * W, [P, 2, T])[0:RANK]
        dab = k.sb("dab", [P, NJ, 4 * GDN_H])
        sp = k.sb("sp", [P, 2] + small[1:])
        cw = k.sb("conv_w", [P, 3 * GDN_H, TAPS])
        sq = k.carve(k.pool, at + 7 * W, [P, 2, T])
        rn = k.carve(k.pool, at + 8 * W, [P, 2 * T])
        pp = k.ps("proj_ps", [P, 2, 2 * W])
        aux = k.ps("aux_ps", [P, 4, W])
        wsrc = i["w_in_blocks"].rearrange("b (p c) n -> b p c n", c=KC)
        nblk = NT_BLOCKS + NN_BLOCKS
        HC = 2 * GDN_H // 2
        with nc.Block() as block:
            @block.sync
            def _(sy):
                sy.dma_start(wsm[:], i["w_in_small"].rearrange("(p c) n -> p c n", c=KC)).then_inc(s_ws, 16)
                for b in range(2):
                    sy.dma_start(wbuf[b][:], wsrc[b]).then_inc(s_wf[b], 16)
                for d, n in enumerate(("fwd", "bwd")):
                    sy.dma_start(w2[:, d, :], i[f"gla_gate_w2_{n}"][0]).then_inc(s_ld, 16)
                    sy.dma_start(gb[:, d, :], i[f"gla_gate_b_{n}"]).then_inc(s_ld, 16)
                    h = slice(d * GDN_H, (d + 1) * GDN_H)
                    sy.dma_start(rows[:, 0, h], i[f"gdn_a_log_{n}"].broadcast_to([P, GDN_H])).then_inc(s_ld, 16)
                    sy.dma_start(rows[:, 1, h], i[f"gdn_dt_bias_{n}"].broadcast_to([P, GDN_H])).then_inc(s_ld, 16)
                sy.dma_start(cw[:], i["conv_w"].rearrange("p (g t) -> p g t", t=TAPS)).then_inc(s_cw, 16)
                with nc.sync.Fori(1, nblk // 2) as it:
                    for b in range(2):
                        sy.wait_ge(s_prod, it * 2 + (b - 1))
                        sy.dma_start(wbuf[b][:], wsrc[it * 2 + b]).then_inc(s_wf[b], 16)

            def turned_block(b):
                for m in range(4):
                    for c in range(KC):
                        last = nc.tensor.matmul(pp[:, b, m * T:(m + 1) * T],
                                                wbuf[b][:, c, m * P:(m + 1) * P], k.hT[:, c, :],
                                                start=(c == 0), stop=(c == KC - 1))
                return last

            def straight_block(b):
                for j in range(NJ):
                    for c in range(KC):
                        last = nc.tensor.matmul(pp[:, b, j * W:(j + 1) * W],
                                                k.hT[:, c, j * P:(j + 1) * P], wbuf[b][:, c, :],
                                                start=(c == 0), stop=(c == KC - 1))
                return last

            @block.tensor
            def _(pe):
                pe.wait_ge(s_ws, 16)
                for d in range(2):
                    for c in range(KC):
                        nc.tensor.matmul(aux[0:RANK, d, 0:T], wsm[:, c, d * RANK:(d + 1) * RANK],
                                         k.hT[:, c, :], start=(c == 0), stop=(c == KC - 1))
                for j in range(NJ):
                    for c in range(KC):
                        last = nc.tensor.matmul(aux[:, 2, j * 32:(j + 1) * 32],
                                                k.hT[:, c, j * P:(j + 1) * P], wsm[:, c, 32:64],
                                                start=(c == 0), stop=(c == KC - 1))
                last.then_inc(s_sm, 1)
                pe.wait_ge(s_wf[0], 16)
                turned_block(0).then_inc(s_prod, 1)
                pe.wait_ge(s_ld, 128)
                pe.wait_ge(s_smo, 2)
                for d in range(2):
                    for j in range(NJ):
                        zb = aux[:, 2 * d + j, :]
                        nc.tensor.matmul(zb, glrT[:, d, j * P:(j + 1) * P], w2[:, d, :], start=True, stop=False)
                        last = nc.tensor.matmul(zb, k.table("ones")[0:1, :], gb[:, d, :], start=False, stop=True)
                last.then_inc(s_z, 1)
                pe.wait_ge(s_wf[1], 16)
                turned_block(1).then_inc(s_prod, 1)
                pe.wait_ge(s_g, 1)
                pe.wait_ge(s_mn, 1)
                n = NJ * GDN_H
                for d in range(2):
                    nc.tensor.matmul(aux[:, 0, d * n:(d + 1) * n], k.table("cum", d), k.g[:, d], start=True, stop=True)
                nc.tensor.matmul(aux[:, 0, 2 * n:4 * n], k.table("blk"), k.g[:], start=True, stop=True)
                for c in range(2):
                    last = nc.tensor.matmul(aux[:, 0, (4 + 2 * c) * n:(6 + 2 * c) * n],
                                            k.table("half", c), k.g[:], start=True, stop=True)
                last.then_inc(s_sum, 1)
                with nc.tensor.Fori(1, NT_BLOCKS // 2) as it:
                    for b in range(2):
                        pe.wait_ge(s_wf[b], it * 16 + 16)
                        pe.wait_ge(s_out, it * 2 + (b - 1))
                        turned_block(b).then_inc(s_prod, 1)
                with nc.tensor.Fori(NT_BLOCKS // 2, nblk // 2) as it:
                    for b in range(2):
                        pe.wait_ge(s_wf[b], it * 16 + 16)
                        pe.wait_ge(s_out, it * 2 + (b - 1))
                        straight_block(b).then_inc(s_prod, 1)
                        pe.wait_ge(s_sq, it * 2 + (b + 1 - NT_BLOCKS))
                        nc.tensor.matmul(aux[:, 2, :], k.table("ones"), sq[:], start=True, stop=True).then_inc(s_np, 1)

            @block.scalar
            def _(act):
                act.wait_ge(s_sm, 1)
                nc.scalar.activation(glrT[:], aux[0:RANK, 0:2, 0:T], ACT.Copy).then_inc(s_smo, 1)
                nc.scalar.activation(dab[:], aux[:, 2, 0:64].rearrange("p (j n) -> p j n", j=NJ), ACT.Copy).then_inc(s_smo, 1)
                act.wait_ge(s_prod, 1)
                nc.scalar.activation(k.qkT[:, 0], pp[:, 0, :].rearrange("p (m t) -> p m t", m=4),
                                     ACT.Copy).then_inc(s_out, 1)
                act.wait_ge(s_z, 1)
                nc.scalar.activation(zabs[:], aux[:].rearrange("p (d j) n -> p d j n", d=2), ACT.Abs).then_inc(s_abs, 1)
                act.wait_ge(s_abs, 1)
                nc.scalar.activation(zabs[:], zabs[:], ACT.Exp, scale=-1.0).then_inc(s_abs, 1)
                act.wait_ge(s_spz, 2)
                nc.scalar.activation(sp[:, 1], sp[:, 1], ACT.Exp, scale=-1.0).then_inc(s_abs, 1)
                nc.scalar.activation(rows[:, 0, :], rows[:, 0, :], ACT.Exp).then_inc(s_rate, 1)
                act.wait_ge(s_smo, 2)
                nc.scalar.activation(k.beta[:], dab[:, :, 2 * GDN_H:].rearrange("p j (d h) -> p d j h", d=2),
                                     ACT.Exp, scale=-1.0).then_inc(s_be, 1)
                act.wait_ge(s_abs, 3)
                nc.scalar.activation(sp[:, 1], sp[:, 1], ACT.Ln, bias=1.0).then_inc(s_spl, 1)
                nc.scalar.activation(zabs[:], zabs[:], ACT.Ln, bias=1.0).then_inc(s_log, 1)
                act.wait_ge(s_prod, 2)
                nc.scalar.activation(k.qkT[:, 1], pp[:, 1, :].rearrange("p (m t) -> p m t", m=4),
                                     ACT.Copy).then_inc(s_out, 1)
                act.wait_ge(s_td, 1)
                nc.scalar.activation(k.eg[:], k.gcum[:], ACT.Exp).then_inc(s_ge, 1)
                nc.scalar.activation(k.et[:], k.et[:], ACT.Exp).then_inc(s_ge, 1)
                nc.scalar.activation(k.dec[:], k.dec[:], ACT.Exp).then_inc(s_ge, 1)
                act.wait_ge(s_pad, 2)
                with nc.scalar.Fori(1, NT_BLOCKS // 2) as it:
                    for b in range(2):
                        act.wait_ge(s_prod, it * 2 + (b + 1))
                        nc.scalar.activation(cin[:, bass.ds(it * 8 + (4 * b - 8), 4), PAD:PAD + T],
                                             pp[:, b, :].rearrange("p (m t) -> p m t", m=4),
                                             ACT.Copy).then_inc(s_out, 1)
                act.wait_ge(s_conv, 1)
                nc.scalar.activation(k.conv[:, 0:2 * GDN_H], k.conv[:, 0:2 * GDN_H], ACT.Silu).then_inc(s_silu, 1)
                with nc.scalar.Fori(NT_BLOCKS // 2, nblk // 2) as it:
                    for b in range(2):
                        act.wait_ge(s_prod, it * 2 + (b + 1))
                        nc.scalar.activation(k.nat[:, bass.ds(it - NT_BLOCKS // 2, 1), :, b * W:(b + 1) * W],
                                             pp[:, b, :].rearrange("p (o j n) -> p o j n", o=1, j=NJ),
                                             ACT.Copy).then_inc(s_out, 1)
                        act.wait_ge(s_ni, it * 2 + (b + 1 - NT_BLOCKS))
                        nc.scalar.activation(rn[:], rn[:], ACT.Sqrt).then_inc(s_ne, 1)
                act.wait_ge(s_conv, 2)
                nc.scalar.activation(k.conv[:, 2 * GDN_H:], k.conv[:, 2 * GDN_H:], ACT.Silu)

            @block.vector
            def _(dve):
                o = Order(dve, k.order["dve"])
                nc.vector.memset(cin[:, :, 0:PAD], 0.0).then_inc(s_pad, 1)
                nc.vector.memset(cin[:, :, PAD + T:], 0.0).then_inc(s_pad, 1)
                dve.wait_ge(s_ld, 128)
                dve.wait_ge(s_smo, 2)
                z = dab[:, :, 0:2 * GDN_H].rearrange("p j (d h) -> p d j h", d=2)
                for d in range(2):
                    o(nc.vector.tensor_tensor(sp[:, 0, d], z[:, d],
                                              bc(rows[:, 1, d * GDN_H:(d + 1) * GDN_H], 1, NJ), ALU.add))
                o(nc.vector.tensor_scalar(sp[:, 1], sp[:, 0], -1.0, None, ALU.mult))
                nc.vector.tensor_tensor(sp[:, 1], sp[:, 1], sp[:, 0], ALU.max).then_inc(s_spz, 1)
                dve.wait_ge(s_spz, 1)
                nc.vector.tensor_scalar(sp[:, 0], sp[:, 0], 0.0, None, ALU.max).then_inc(s_spz, 1)
                dve.wait_ge(s_abs, 1)
                nc.vector.tensor_scalar(k.la[:], aux[:].rearrange("p (d j) n -> p d j n", d=2), 0.0, None,
                                        ALU.min).then_inc(s_mn, 1)
                dve.wait_ge(s_spl, 1)
                dve.wait_ge(s_spz, 2)
                o(nc.vector.tensor_tensor(sp[:, 0], sp[:, 0], sp[:, 1], ALU.add))
                dve.wait_ge(s_rate, 1)
                for d in range(2):
                    o(nc.vector.tensor_tensor(k.g[:, d], sp[:, 0, d],
                                              bc(rows[:, 0, d * GDN_H:(d + 1) * GDN_H], 1, NJ), ALU.mult))
                nc.vector.tensor_scalar(k.g[:], k.g[:], -1.0, None, ALU.mult).then_inc(s_g, 1)
                dve.wait_ge(s_be, 1)
                o(nc.vector.tensor_scalar(k.beta[:], k.beta[:], 1.0, None, ALU.add))
                o(nc.vector.reciprocal(k.beta[:], k.beta[:]))
                dve.wait_ge(s_log, 1)
                dve.wait_ge(s_mn, 1)
                o(nc.vector.tensor_tensor(k.la[:], k.la[:], zabs[:], ALU.subtract))
                n = 2 * NJ * GDN_H
                dve.wait_ge(s_sum, 1)
                flat = "p d j h -> p (d j h)"
                o(nc.vector.tensor_copy(k.gcum[:].rearrange(flat), aux[:, 0, 0:n]))
                o(nc.vector.tensor_copy(k.dec[:].rearrange("p c d j h -> p (c d j h)"), aux[:, 0, 2 * n:4 * n]))
                nc.vector.tensor_tensor(k.et[:].rearrange(flat), aux[:, 0, n:2 * n], k.gcum[:].rearrange(flat),
                                        ALU.subtract).then_inc(s_td, 1)
                dve.wait_ge(s_ge, 3)
                o(nc.vector.tensor_tensor(k.beg[:], k.beta[:], k.eg[:], ALU.mult))
                dve.wait_ge(s_pad, 2)
                dve.wait_ge(s_cw, 16)

                def convolve(it):
                    for b in range(2):
                        dve.wait_ge(s_out, it * 2 + (b + 1))
                        for t in range(TAPS):
                            for m in range(4):
                                g = it * 8 + (4 * b - 8 + m)
                                acc = k.conv[:, bass.ds(g, 1), :]
                                seen = cin[:, bass.ds(g, 1), t:t + T]
                                tap = cw[:, bass.ds(g, 1), t]
                                if t == 0:
                                    ins = nc.vector.tensor_scalar(acc, seen, tap, None, ALU.mult)
                                else:
                                    ins = nc.vector.scalar_tensor_tensor(
                                        out=acc, in0=seen, scalar=tap, in1=acc, op0=ALU.mult, op1=ALU.add)
                                o(ins)

                with nc.vector.Fori(1, NT_BLOCKS // 2) as it:
                    o.restart()
                    convolve(it)
                o.restart()
                dve.sem_inc(s_conv, 2)
                dve.wait_ge(s_silu, 1)
                with nc.vector.Fori(0, HC // 2) as it:
                    o.restart()
                    for b in range(2):
                        heads = k.conv[:, bass.ds(it * 4 + 2 * b, 2), :]
                        nc.vector.tensor_tensor(sq[:], heads, heads, ALU.mult).then_inc(s_sq, 1)
                        dve.wait_ge(s_np, it * 2 + (b + 1))
                        o(nc.vector.tensor_scalar(rn[:], aux[:, 2, :], EPS, None, ALU.add))
                        nc.vector.reciprocal(rn[:], rn[:]).then_inc(s_ni, 1)
                        dve.wait_ge(s_ne, it * 2 + (b + 1))
                        o(nc.vector.tensor_tensor(heads, heads, rn[:].rearrange("p (a t) -> p a t", a=2), ALU.mult))
                o.restart()
                dve.sem_inc(s_sq, 2)
                for n in range(2):
                    dve.wait_ge(s_ne, HC + n)
                    dve.sem_inc(s_ni, 1)
    k.scope = k.ctx


def stage_gla(k):
    nc = k.nc
    HP = 2
    NI = GLA_H // HP
    U = 4
    k.oa = k.carve(k.pool, POOL_N - NJ * D, [P, NJ, D])
    k.ob = k.carve(k.pool, POOL_N - 2 * NJ * D, [P, NJ, D])
    A = range(HP)
    mk = lambda n: [k.sem(f"gla_{n}{a}") for a in A]
    (s_stg, s_cum, s_tot, s_exp, s_te, s_dk, s_sc, s_kt, s_at, s_ktn, s_kv, s_st, s_o, s_hd, s_zero, s_v) = (
        mk(n) for n in ("staged", "cum_product", "total_out", "exps_done", "tail_exp", "decayed", "scores",
                        "tail_turned", "scores_masked", "tail_natural", "chunk_kv", "state_done",
                        "out_product", "head_done", "zeroed", "v_staged"))
    scope = ExitStack()
    k.scope = scope
    with scope:
        used = [AT_FREE]

        def sb(n, sh):
            views = []
            for a in A:
                views.append(k.carve(k.pool, used[0], sh))
                used[0] += int(np.prod(sh[1:]))
            return views

        q, kk = sb("q", [P, T]), sb("k", [P, T])
        la, v = sb("la", [P, U, P]), sb("v", [P, NJ, GLA_DV])
        tot, dec = sb("tot", [P, U, 2]), sb("dec", [P, U, 2])
        ep, en, et = sb("ep", [P, U, P]), sb("en", [P, U, P]), sb("et", [P, U, P])
        at, ktn = sb("at", [P, U, P]), sb("ktn", [P, U, P])
        st = sb("st", [P, 3, 2, GLA_DV])
        B0 = [k.ps(f"gla_cum_ps{a}", [P, U, P]) for a in A]
        B1 = [k.ps(f"gla_sc_ps{a}", [P, U, P]) for a in A]
        BO = [k.ps(f"gla_out_ps{a}", [P, NJ, W]) for a in A]

        def rows(d, n):
            m = n if d == 0 else 3 - n
            return m // 2, m % 2

        with nc.Block() as block:
            @block.scalar
            def _(act):
                with nc.scalar.Fori(0, NI) as it:
                    for a in A:
                        h = it * HP + a
                        nc.scalar.activation(la[a][:], k.la[:, :, :, bass.ds(h * P, P)].rearrange("p d j n -> p (d j) n"),
                                             ACT.Copy, scale=1.0 / TAU).then_inc(s_stg[a], 1)
                        nc.scalar.activation(q[a][:], k.qkT[:, 0, bass.ds(h, 1), :].rearrange("p o t -> p (o t)"), ACT.Copy,
                                             scale=float(GLA_DK) ** -0.5).then_inc(s_stg[a], 1)
                        nc.scalar.activation(kk[a][:], k.qkT[:, 1, bass.ds(h, 1), :].rearrange("p o t -> p (o t)"), ACT.Copy).then_inc(s_stg[a], 1)
                        nc.scalar.activation(v[a][:], k.nat[:, 0, :, bass.ds(h * GLA_DV, GLA_DV)],
                                             ACT.Copy).then_inc(s_v[a], 1)
                    for a in A:
                        act.wait_ge(s_cum[a], it + 1)
                        act.wait_ge(s_tot[a], it * 2 + 2)
                        nc.scalar.activation(ep[a][:], B0[a][:], ACT.Exp).then_inc(s_exp[a], 1)
                        nc.scalar.activation(en[a][:], B0[a][:], ACT.Exp, scale=-1.0).then_inc(s_exp[a], 1)
                        nc.scalar.activation(et[a][:], et[a][:], ACT.Exp).then_inc(s_exp[a], 1)
                        nc.scalar.activation(dec[a][:], tot[a][:], ACT.Exp).then_inc(s_exp[a], 1)
                    for a in A:
                        act.wait_ge(s_kt[a], it + 1)
                        nc.scalar.activation(ktn[a][:], B0[a][:], ACT.Copy).then_inc(s_ktn[a], 1)
                    for a in A:
                        act.wait_ge(s_hd[a], it + 1)

            @block.vector
            def _(dve):
                o = Order(dve, k.order["dve"])
                for a in A:
                    nc.vector.memset(at[a][:], 0.0).then_inc(s_zero[a], 1)
                with nc.vector.Fori(0, NI) as it:
                    o.restart()
                    for a in A:
                        dve.wait_ge(s_cum[a], it + 1)
                        o(nc.vector.tensor_copy(tot[a][:, 0:2], B0[a][:, 0:2, CH - 1::CH]))
                        o(nc.vector.tensor_copy(tot[a][:, 2:4], B0[a][:, 2:4, 0::CH]))
                        for d in range(2):
                            nc.vector.tensor_tensor(
                                et[a][:, 2 * d:2 * d + 2].rearrange("p j (c t) -> p (j c) t", c=2),
                                bc(tot[a][:, 2 * d:2 * d + 2].rearrange("p j c -> p (j c)"), 2, CH),
                                B0[a][:, 2 * d:2 * d + 2].rearrange("p j (c t) -> p (j c) t", c=2),
                                ALU.subtract).then_inc(s_tot[a], 1)
                    for a in A:
                        dve.wait_ge(s_exp[a], it * 4 + 4)
                        dve.wait_ge(s_stg[a], it * 3 + 3)
                        for e, x in ((ep, q), (en, kk), (et, kk)):
                            e4 = e[a][:].rearrange("p (d j) t -> p d (j t)", d=2)
                            nc.vector.tensor_tensor(e4, e4, bc(x[a][:], 1, 2), ALU.mult).then_inc(s_dk[a], 1)
                    for a in A:
                        dve.wait_ge(s_zero[a], 1)
                        dve.wait_ge(s_sc[a], it + 1)
                        for d in range(2):
                            nc.vector.copy_predicated(at[a][:, 2 * d:2 * d + 2], bc(k.table("incl", d).bitcast(I32), 1, NJ),
                                                      B1[a][:, 2 * d:2 * d + 2]).then_inc(s_at[a], 1)
                    for n in range(3):
                        for a in A:
                            dve.wait_ge(s_kv[a], it * 3 + (n + 1))
                            kv = B1[a][:].rearrange("p u t -> p (u t)")
                            for d in range(2):
                                j, c = rows(d, n)
                                got = kv[:, d * GLA_DV:(d + 1) * GLA_DV]
                                if n == 0:
                                    ins = nc.vector.tensor_copy(st[a][:, 0, d], got)
                                else:
                                    ins = nc.vector.scalar_tensor_tensor(
                                        out=st[a][:, n, d], in0=st[a][:, n - 1, d],
                                        scalar=dec[a][:, 2 * d + j, c:c + 1], in1=got, op0=ALU.mult, op1=ALU.add)
                                ins.then_inc(s_st[a], 1)
                            dve.wait_ge(s_st[a], it * 6 + (2 * n + 2))
                    for a in A:
                        dve.wait_ge(s_o[a], it + 1)
                        h = it * HP + a
                        nc.vector.tensor_copy(k.oa[:, :, bass.ds(h * GLA_DV, GLA_DV)],
                                              BO[a][:, :, 0:GLA_DV]).then_inc(s_hd[a], 1)
                    for a in A:
                        dve.wait_ge(s_hd[a], it + 1)
                o.restart()

            @block.tensor
            def _(pe):
                po = Order(pe, k.order["pe"])
                with nc.tensor.Fori(0, NI) as it:
                    po.restart()
                    for a in A:
                        pe.wait_ge(s_stg[a], it * 3 + 3)
                        for u in range(U):
                            last = nc.tensor.matmul(B0[a][:, u], la[a][:, u], k.table("cum", u // 2),
                                                    start=True, stop=True)
                        last.then_inc(s_cum[a], 1)
                    for a in A:
                        pe.wait_ge(s_dk[a], it * 3 + 3)
                        for u in range(U):
                            last = nc.tensor.matmul(B1[a][:, u], en[a][:, u], ep[a][:, u], start=True, stop=True)
                        last.then_inc(s_sc[a], 1)
                        for u in range(U):
                            last = nc.tensor.transpose(B0[a][:, u], et[a][:, u], k.table("ident"))
                        last.then_inc(s_kt[a], 1)
                    for a in A:
                        pe.wait_ge(s_v[a], it + 1)
                        pe.wait_ge(s_at[a], it * 2 + 2)
                        for j in range(NJ):
                            for d in range(2):
                                nc.tensor.matmul(BO[a][:, j, 0:GLA_DV], at[a][:, 2 * d + j], v[a][:, j],
                                                 start=(d == 0), stop=True, skip_group_check=True)
                    for n in range(4):
                        for a in A:
                            if n < 3:
                                pe.wait_ge(s_ktn[a], it + 1)
                                if n:
                                    pe.wait_ge(s_st[a], it * 6 + 2 * n)
                                kv = B1[a][:].rearrange("p u t -> p (u t)")
                                for d in range(2):
                                    j, c = rows(d, n)
                                    r = slice(c * CH, (c + 1) * CH)
                                    last = nc.tensor.matmul(kv[:, d * GLA_DV:(d + 1) * GLA_DV],
                                                            ktn[a][r, 2 * d + j], v[a][r, j],
                                                            start=True, stop=True)
                                    if d == 0:
                                        po(last)
                                last.then_inc(s_kv[a], 1)
                            if n:
                                pe.wait_ge(s_st[a], it * 6 + 2 * n)
                                for d in range(2):
                                    j, c = rows(d, n)
                                    r = slice(c * CH, (c + 1) * CH)
                                    last = nc.tensor.matmul(BO[a][r, j, 0:GLA_DV], ep[a][:, 2 * d + j, r],
                                                            st[a][:, n - 1, d], start=False, stop=True,
                                                            skip_group_check=True)
                                if n == 3:
                                    last.then_inc(s_o[a], 1)
                    for a in A:
                        pe.wait_ge(s_hd[a], it + 1)
    k.scope = k.ctx


def stage_gdn(k, ahead=None):
    nc = k.nc
    HP = 2
    NI = GDN_H // HP
    U = 4
    A = range(HP)
    mk = lambda n: [k.sem(f"gdn_{n}{a}") for a in A]
    (s_qk, s_vg, s_p1, s_diff, s_ex, s_sc, s_nb, s_lt, s_lv, s_vs, s_vp, s_zz, s_x, s_uw, s_uws, s_ws, s_vn,
     s_kv, s_s, s_hd, s_xt, s_xs) = (
        mk(n) for n in ("qk_staged", "v_g_staged", "first_products", "diffs_done", "exps_done", "masked",
                        "natural_done", "L_turned", "L_done", "level_masked", "level_product", "update_product",
                        "inverse_done", "uw_product", "uw_out", "ws_product", "v_new_done", "kv_product",
                        "state_done", "head_done", "inverse_turned", "inverse_out"))
    scope = ExitStack()
    k.scope = scope
    with scope:
        used = [AT_LA]

        def sb(n, sh):
            views = []
            for a in A:
                views.append(k.carve(k.pool, used[0], sh))
                used[0] += int(np.prod(sh[1:]))
            return views

        q, kk, v = sb("q", [P, T]), sb("k", [P, T]), sb("v", [P, T])
        gB = sb("gB", [P, 2, NJ, P])
        kbg, ktl, vb = (sb(n, [P, 2, NJ, P]) for n in ("kbg", "ktl", "vb"))
        mx, mn = sb("mx", [P, 2, NJ, P]), sb("mn", [P, 2, NJ, P])
        nL, aT = sb("nL", [P, 2, NJ, P]), sb("aT", [P, 2, NJ, P])
        X, XT, V = (sb(n, [P, 2, NJ, P]) for n in ("X", "XT", "V"))
        us, wT, vn = gB, mx, mn
        S = sb("S", [P, 2, P])
        B = [[k.ps(f"gdn_ps{a}_{b}", [P, 2, NJ, P]) for b in range(4)] for a in A]

        def rows(d, n):
            m = n if d == 0 else 3 - n
            return m // 2, m % 2

        def col(small, h):
            return small[:, :, :, bass.ds(h, 1)].broadcast_to([P, 2, NJ, P])

        def mask(name, n=0):
            return k.tab[:, OFF[name] + 2 * n * P:OFF[name] + (2 * n + 2) * P].rearrange(
                "p (d t) -> p d t", d=2)

        def masked(eng, out, in0, name, n=0):
            ins = []
            for d in range(2):
                ins.append(eng.tensor_tensor(out[:, d], in0[:, d], bc(mask(name, n)[:, d], 1, NJ), ALU.mult))
            return ins

        with nc.Block() as block:
            @block.sync
            def _(sp):
                if ahead is not None:
                    ahead(sp)

            @block.gpsimd
            def _(pool):
                o = Order(pool, k.order["pool"])
                with nc.gpsimd.Fori(0, NI) as it:
                    o.restart()
                    for a in A:
                        h = it * HP + a
                        flat = lambda x: x.rearrange("p o t -> p (o t)")
                        nc.gpsimd.tensor_copy(kk[a][:], flat(k.conv[:, bass.ds(h + GDN_H, 1), :])).then_inc(s_qk[a], 1)
                        o(nc.gpsimd.tensor_copy(q[a][:], flat(k.conv[:, bass.ds(h, 1), :])))
                        nc.gpsimd.tensor_scalar(q[a][:], q[a][:], float(GDN_D) ** -0.5, None, ALU.mult).then_inc(s_qk[a], 1)
                    for a in A:
                        h = it * HP + a
                        pool.wait_ge(s_ex[a], it * 2 + 2)
                        for ins in masked(nc.gpsimd, mx[a], mx[a], "strictn"):
                            o(ins)
                        nc.gpsimd.tensor_tensor(mx[a][:], mx[a][:], col(k.beta, h), ALU.mult).then_inc(s_sc[a], 1)
                        for ins in masked(nc.gpsimd, mn[a], mn[a], "incl"):
                            ins.then_inc(s_sc[a], 1)
                    for a in A:
                        pool.wait_ge(s_lv[a], it * 2 + 1)
                        for ins in masked(nc.gpsimd, X[a], nL[a], "lev0"):
                            o(ins)
                        nc.gpsimd.tensor_tensor(X[a][:].rearrange("p d j t -> p (d j) t"),
                                                X[a][:].rearrange("p d j t -> p (d j) t"),
                                                bc(k.table("ident"), 1, U), ALU.add).then_inc(s_x[a], 1)
                    for a in A:
                        pool.wait_ge(s_hd[a], it + 1)
                o.restart()

            @block.scalar
            def _(act):
                with nc.scalar.Fori(0, NI) as it:
                    for a in A:
                        h = it * HP + a
                        nc.scalar.activation(v[a][:], k.conv[:, bass.ds(h + 2 * GDN_H, 1), :].rearrange("p o t -> p (o t)"),
                                             ACT.Copy).then_inc(s_vg[a], 1)
                        nc.scalar.activation(gB[a][:], col(k.g, h), ACT.Copy).then_inc(s_vg[a], 1)
                    for a in A:
                        act.wait_ge(s_diff[a], it * 2 + 2)
                        nc.scalar.activation(mx[a][:], mx[a][:], ACT.Exp, scale=-1.0).then_inc(s_ex[a], 1)
                        nc.scalar.activation(mn[a][:], mn[a][:], ACT.Exp).then_inc(s_ex[a], 1)
                    for l in range(2, LEVELS):
                        for a in A:
                            act.wait_ge(s_xt[a], it * (LEVELS - 2) + (l - 1))
                            act.wait_ge(s_zz[a], it * (LEVELS - 1) + (l - 1))
                            nc.scalar.activation(X[a][:], B[a][1][:], ACT.Copy).then_inc(s_xs[a], 1)
                    for a in A:
                        act.wait_ge(s_uw[a], it + 1)
                        nc.scalar.activation(us[a][:], B[a][1][:], ACT.Copy).then_inc(s_uws[a], 1)
                        nc.scalar.activation(wT[a][:], B[a][2][:], ACT.Copy).then_inc(s_uws[a], 1)
                    for a in A:
                        act.wait_ge(s_hd[a], it + 1)

            @block.vector
            def _(dve):
                o = Order(dve, k.order["dve"])
                with nc.vector.Fori(0, NI) as it:
                    o.restart()
                    for a in A:
                        h = it * HP + a
                        dve.wait_ge(s_p1[a], it * 3 + 3)
                        o(nc.vector.tensor_tensor(mx[a][:], B[a][2][:], col(k.gcum, h), ALU.subtract))
                        nc.vector.tensor_scalar(mn[a][:], mx[a][:], 0.0, None, ALU.min).then_inc(s_diff[a], 1)
                        nc.vector.tensor_scalar(mx[a][:], mx[a][:], 0.0, None, ALU.max).then_inc(s_diff[a], 1)
                        tk = B[a][0][:, 0]
                        tv = B[a][0][:, 1]
                        for dst, src, f in ((kbg, tk, k.beg), (ktl, tk, k.et), (vb, tv, k.beta)):
                            nc.vector.tensor_tensor(dst[a][:], bc(src, 1, 2), col(f, h), ALU.mult).then_inc(s_nb[a], 1)
                    for a in A:
                        dve.wait_ge(s_sc[a], it * 3 + 3)
                        nc.vector.tensor_tensor(nL[a][:], bc(B[a][1][:, 0], 1, 2), mx[a][:], ALU.mult).then_inc(s_lv[a], 1)
                        nc.vector.tensor_tensor(aT[a][:], bc(B[a][1][:, 1], 1, 2), mn[a][:], ALU.mult).then_inc(s_lv[a], 1)
                    for a in A:
                        dve.wait_ge(s_lt[a], it + 1)
                        for ins in masked(nc.vector, XT[a], B[a][0], "lev"):
                            o(ins)
                        nc.vector.tensor_tensor(XT[a][:].rearrange("p d j t -> p (d j) t"),
                                                XT[a][:].rearrange("p d j t -> p (d j) t"),
                                                bc(k.table("ident"), 1, U), ALU.add).then_inc(s_x[a], 1)
                    for l in range(1, LEVELS):
                        for a in A:
                            dve.wait_ge(s_vp[a], it * (LEVELS - 1) + l)
                            for ins in masked(nc.vector, V[a], B[a][0], "lev", l):
                                ins.then_inc(s_vs[a], 1)
                        for a in A:
                            dve.wait_ge(s_zz[a], it * (LEVELS - 1) + l)
                            nc.vector.tensor_tensor(XT[a][:], XT[a][:], B[a][2][:], ALU.add).then_inc(s_x[a], 1)
                    for a in A:
                        o(nc.vector.memset(S[a][:], 0.0))
                        dve.sem_inc(s_s[a], 1)
                    for n in range(4):
                        for a in A:
                            if n:
                                dve.wait_ge(s_ws[a], it * 3 + n)
                                for d in range(2):
                                    j, c = rows(d, n)
                                    r = slice(c * CH, (c + 1) * CH)
                                    nc.vector.tensor_tensor(vn[a][r, d, j], us[a][r, d, j], B[a][3][r, 0, d],
                                                            ALU.subtract).then_inc(s_vn[a], 1)
                        for a in A:
                            if n < 3:
                                h = it * HP + a
                                dve.wait_ge(s_kv[a], it * 4 + (n + 1))
                                for d in range(2):
                                    j, c = rows(d, n)
                                    nc.vector.scalar_tensor_tensor(
                                        out=S[a][:, d], in0=S[a][:, d], scalar=k.dec[:, c, d, j, bass.ds(h, 1)],
                                        in1=B[a][3][:, 1, d], op0=ALU.mult, op1=ALU.add).then_inc(s_s[a], 1)
                    for a in A:
                        h = it * HP + a
                        dve.wait_ge(s_kv[a], it * 4 + 4)
                        o(nc.vector.tensor_tensor(V[a][:], B[a][0][:], col(k.eg, h), ALU.mult))
                        o(nc.vector.tensor_tensor(V[a][:], V[a][:], B[a][1][:], ALU.add))
                        nc.vector.tensor_tensor(k.ob[:, :, bass.ds(h * GDN_D, GDN_D)], V[a][:, 0], V[a][:, 1],
                                                ALU.add).then_inc(s_hd[a], 1)
                    for a in A:
                        dve.wait_ge(s_hd[a], it + 1)
                o.restart()

            @block.tensor
            def _(pe):
                def each(a, fn):
                    for d in range(2):
                        for j in range(NJ):
                            last = fn(a, d, j)
                    return last

                mm = nc.tensor.matmul
                po = Order(pe, k.order["pe"])
                with nc.tensor.Fori(0, NI) as it:
                    po.restart()
                    for a in A:
                        pe.wait_ge(s_vg[a], it * 2 + 2)
                        each(a, lambda a, d, j: mm(B[a][2][:, d, j], gB[a][:, d, j], k.table("cum", d),
                                                   start=True, stop=True)).then_inc(s_p1[a], 1)
                        pe.wait_ge(s_qk[a], it * 2 + 2)
                        for x, half in ((kk, 0), (v, 1)):
                            for j in range(NJ):
                                last = nc.tensor.transpose(B[a][0][:, half, j], x[a][:, j * P:(j + 1) * P], k.table("ident"))
                        last.then_inc(s_p1[a], 1)
                        for x, half in ((kk, 0), (q, 1)):
                            for j in range(NJ):
                                t = slice(j * P, (j + 1) * P)
                                last = mm(B[a][1][:, half, j], kk[a][:, t], x[a][:, t], start=True, stop=True)
                        last.then_inc(s_p1[a], 1)
                    for a in A:
                        pe.wait_ge(s_nb[a], it * 3 + 3)
                        pe.wait_ge(s_lv[a], it * 2 + 2)
                        each(a, lambda a, d, j: nc.tensor.transpose(B[a][0][:, d, j], nL[a][:, d, j],
                                                                    k.table("ident"))).then_inc(s_lt[a], 1)
                    per = LEVELS + 1
                    for l in range(1, LEVELS):
                        for a in A:
                            pe.wait_ge(s_x[a], it * per + (l + 1))
                            each(a, lambda a, d, j: mm(B[a][0][:, d, j], nL[a][:, d, j], XT[a][:, d, j],
                                                       start=True, stop=True)).then_inc(s_vp[a], 1)
                            if l > 1:
                                each(a, lambda a, d, j: nc.tensor.transpose(B[a][1][:, d, j], XT[a][:, d, j],
                                                                            k.table("ident"))).then_inc(s_xt[a], 1)
                        for a in A:
                            pe.wait_ge(s_vs[a], it * 2 * (LEVELS - 1) + 2 * l)
                            if l > 1:
                                pe.wait_ge(s_xs[a], it * (LEVELS - 2) + (l - 1))
                            each(a, lambda a, d, j: mm(B[a][2][:, d, j], X[a][:, d, j], V[a][:, d, j],
                                                       start=True, stop=True)).then_inc(s_zz[a], 1)
                    for a in A:
                        pe.wait_ge(s_x[a], it * per + per)
                        each(a, lambda a, d, j: mm(B[a][1][:, d, j], XT[a][:, d, j], vb[a][:, d, j],
                                                   start=True, stop=True))
                        each(a, lambda a, d, j: mm(B[a][2][:, d, j], kbg[a][:, d, j], XT[a][:, d, j],
                                                   start=True, stop=True)).then_inc(s_uw[a], 1)
                    for n in range(4):
                        for a in A:
                            if n == 0:
                                pe.wait_ge(s_uws[a], it * 2 + 2)
                            pe.wait_ge(s_s[a], it * 7 + (2 * n + 1))
                            if n:
                                for d in range(2):
                                    j, c = rows(d, n)
                                    r = slice(c * CH, (c + 1) * CH)
                                    last = mm(B[a][3][r, 0, d], wT[a][:, d, j, r], S[a][:, d], start=True, stop=True)
                                last.then_inc(s_ws[a], 1)
                            for d in range(2):
                                j, c = rows(d, n)
                                r = slice(c * CH, (c + 1) * CH)
                                mm(B[a][0][r, d, j], q[a][:, j * P + c * CH:j * P + (c + 1) * CH], S[a][:, d],
                                   start=True, stop=True)
                        for a in A:
                            new = us[a] if n == 0 else vn[a]
                            if n:
                                pe.wait_ge(s_vn[a], it * 6 + 2 * n)
                            for d in range(2):
                                j, c = rows(d, n)
                                r = slice(c * CH, (c + 1) * CH)
                                mm(B[a][3][:, 1, d], ktl[a][r, d, j], new[r, d, j], start=True, stop=True)
                                last = mm(B[a][1][r, d, j], aT[a][r, d, j, r], new[r, d, j], start=True, stop=True)
                                if d == 0:
                                    po(last)
                            last.then_inc(s_kv[a], 1)
                    for a in A:
                        pe.wait_ge(s_hd[a], it + 1)
    k.scope = k.ctx


def stage_combine(k, ahead=None):
    nc, i = k.nc, k.i
    s_ld, s_act, s_ss, s_inv, s_rs, s_gate, s_sq = (k.sem(f"comb_{n}") for n in (
        "loaded", "act_done", "sumsq_done", "inv_done", "rstd_done", "gate_done", "squares"))
    scope = ExitStack()
    k.scope = scope
    with scope:
        wa = k.sb("gla_norm", [P, GLA_DV])
        wb = k.sb("gdn_norm", [P, GDN_D])
        tmp = k.carve(k.pool, POOL_N // 2, [P, 2, NJ, D])
        v = k.sb("comb_var", [P, NJ, GLA_H + GDN_H])
        inv = k.sb("comb_inv", [P, NJ, GLA_H + GDN_H])
        rs = k.sb("comb_rstd", [P, NJ, GLA_H + GDN_H])
        heads = lambda x, n: x.rearrange("p j (h d) -> p j h d", h=n)
        with nc.Block() as block:
            @block.sync
            def _(sp):
                if ahead is not None:
                    ahead(sp)
                sp.dma_start(wa[:], i["gla_norm_w"].broadcast_to([P, GLA_DV])).then_inc(s_ld, 16)
                sp.dma_start(wb[:], i["gdn_norm_w"].broadcast_to([P, GDN_D])).then_inc(s_ld, 16)

            @block.scalar
            def _(act):
                nc.scalar.activation(k.nat[:, 1:3], k.nat[:, 1:3], ACT.Silu).then_inc(s_act, 1)
                nc.scalar.activation(k.nat[:, 3:5], k.nat[:, 3:5], ACT.Sigmoid).then_inc(s_act, 1)
                act.wait_ge(s_inv, 1)
                nc.scalar.activation(rs[:], inv[:], ACT.Sqrt).then_inc(s_rs, 1)

            @block.gpsimd
            def _(pool):
                o = Order(pool, k.order["pool"])
                nc.gpsimd.tensor_tensor(tmp[:, 0], k.oa[:], k.oa[:], ALU.mult).then_inc(s_sq, 1)
                nc.gpsimd.tensor_tensor(tmp[:, 1], k.ob[:], k.ob[:], ALU.mult).then_inc(s_sq, 1)
                pool.wait_ge(s_act, 1)
                pool.wait_ge(s_ld, 32)
                for n, w, hh in ((0, wa, GLA_H), (1, wb, GDN_H)):
                    for j in range(NJ):
                        r = k.nat[:, 1 + n, j].rearrange("p (h d) -> p h d", h=hh)
                        o(nc.gpsimd.tensor_tensor(r, r, bc(w[:], 1, hh), ALU.mult))
                pool.wait_ge(s_act, 2)
                for n in range(2):
                    nc.gpsimd.tensor_tensor(k.nat[:, 1 + n], k.nat[:, 1 + n], k.nat[:, 3 + n],
                                            ALU.mult).then_inc(s_gate, 1)
                o.restart()

            @block.vector
            def _(dve):
                o = Order(dve, k.order["dve"])
                for n, x, hh in ((0, k.oa, GLA_H), (1, k.ob, GDN_H)):
                    dve.wait_ge(s_sq, n + 1)
                    c = slice(0, GLA_H) if n == 0 else slice(GLA_H, GLA_H + GDN_H)
                    o(nc.vector.tensor_reduce(v[:, :, c], heads(tmp[:, n], hh), AX.X, ALU.add))
                    o(nc.vector.tensor_scalar(v[:, :, c], v[:, :, c], hh / D, EPS, ALU.mult, ALU.add))
                nc.vector.reciprocal(inv[:], v[:]).then_inc(s_inv, 1)
                dve.wait_ge(s_rs, 1)
                refine(nc, o, rs[:], v[:], inv[:])
                for n, x, hh in ((0, k.oa, GLA_H), (1, k.ob, GDN_H)):
                    c = slice(0, GLA_H) if n == 0 else slice(GLA_H, GLA_H + GDN_H)
                    o(nc.vector.tensor_tensor(heads(x[:], hh), heads(x[:], hh), bc(rs[:, :, c], 3, D // hh), ALU.mult))
                    dve.wait_ge(s_gate, n + 1)
                    o(nc.vector.tensor_tensor(x[:], x[:], k.nat[:, 1 + n], ALU.mult))
                o(nc.vector.tensor_tensor(k.oa[:], k.oa[:], k.ob[:], ALU.add))
                o.restart()
    k.scope = k.ctx


def load_out(k, sp, weight):
    w = k.carve(k.store, 0, [P, KC, D])
    for c in range(0, KC, 2):
        sp.dma_start(w[:, c:c + 2, :], weight[:, c:c + 2, :]).then_inc(k.s_out_w, 16)
    k.out_loads += 16 * (KC // 2)


def stage_out(k, tag, alpha):
    nc = k.nc
    s_p = k.sem(f"out_product_{tag}")
    scope = ExitStack()
    k.scope = scope
    with scope:
        w = k.carve(k.store, 0, [P, KC, D])
        y = k.ps(f"out_ps_{tag}", [P, NJ, 2, W])
        with nc.Block() as block:
            @block.tensor
            def _(pe):
                pe.wait_ge(k.s_out_w, k.out_loads)
                for j in range(NJ):
                    for n in range(2):
                        for c in range(KC):
                            last = nc.tensor.matmul(y[:, j, n, :], k.hT[:, c, j * P:(j + 1) * P],
                                                    w[:, c, n * W:(n + 1) * W], start=(c == 0), stop=(c == KC - 1))
                        last.then_inc(s_p, 1)

            @block.vector
            def _(dve):
                for j in range(NJ):
                    for n in range(2):
                        dve.wait_ge(s_p, 2 * j + n + 1)
                        xs = k.x[:, j, n * W:(n + 1) * W]
                        nc.vector.scalar_tensor_tensor(out=xs, in0=xs, scalar=alpha, in1=y[:, j, n, :],
                                                       op0=ALU.mult, op1=ALU.add)
    k.scope = k.ctx


def stage_norm(k, tag, gain, bias=None):
    nc = k.nc
    eps = EPS if bias is None else LN_EPS
    s_ld, s_ss, s_inv, s_rs, s_c = (k.sem(f"{n}_{tag}") for n in
                                    ("norm_w_loaded", "sumsq", "inv", "rstd", "centred"))
    scope = ExitStack()
    k.scope = scope
    with scope:
        g = k.sb(f"gain_{tag}", [P, D])
        b = k.sb(f"bias_{tag}", [P, D])
        sq = k.sb(f"sq_{tag}", [P, NJ, D])
        mu, v, inv, rs = (k.sb(f"{n}_{tag}", [P, NJ]) for n in ("mu", "var", "inv", "rstd"))
        with nc.Block() as block:
            @block.sync
            def _(sp):
                sp.dma_start(g[:], gain.broadcast_to([P, D])).then_inc(s_ld, 16)
                if bias is not None:
                    sp.dma_start(b[:], bias.broadcast_to([P, D])).then_inc(s_ld, 16)

            @block.scalar
            def _(act):
                for j in range(NJ):
                    if bias is not None:
                        act.wait_ge(s_c, j + 1)
                    nc.scalar.activation(sq[:, j], k.x[:, j], ACT.Square, accum_out=v[:, j:j + 1]).then_inc(s_ss, 1)
                act.wait_ge(s_inv, 1)
                nc.scalar.activation(rs[:], inv[:], ACT.Sqrt).then_inc(s_rs, 1)

            @block.vector
            def _(dve):
                o = Order(dve, k.order["dve"])
                if bias is not None:
                    o(nc.vector.tensor_reduce(mu[:], k.x[:], AX.X, ALU.add))
                    o(nc.vector.tensor_scalar(mu[:], mu[:], 1.0 / D, None, ALU.mult))
                    for j in range(NJ):
                        nc.vector.tensor_scalar(k.x[:, j], k.x[:, j], mu[:, j:j + 1], None,
                                                ALU.subtract).then_inc(s_c, 1)
                dve.wait_ge(s_ss, NJ)
                o(nc.vector.tensor_scalar(v[:], v[:], 1.0 / D, eps, ALU.mult, ALU.add))
                nc.vector.reciprocal(inv[:], v[:]).then_inc(s_inv, 1)
                dve.wait_ge(s_rs, 1)
                refine(nc, o, rs[:], v[:], inv[:])
                dve.wait_ge(s_ld, 16 if bias is None else 32)
                for j in range(NJ):
                    o(nc.vector.scalar_tensor_tensor(out=k.x[:, j], in0=k.x[:, j], scalar=rs[:, j:j + 1],
                                                     in1=g[:], op0=ALU.mult, op1=ALU.mult))
                if bias is not None:
                    o(nc.vector.tensor_tensor(k.x[:], k.x[:], bc(b[:], 1, NJ), ALU.add))
                o.restart()
    k.scope = k.ctx


def stage_router(k, tag, w_group, w_fine, b_group=None, b_fine=None):
    nc = k.nc
    NL = NG + NE
    s_ld, s_b, s_p, s_d, s_e, s_sel, s_pos = (k.sem(f"{n}_{tag}") for n in (
        "router_loaded", "router_b_loaded", "logits", "logit_diffs", "logit_exps", "selected", "places"))
    scope = ExitStack()
    k.scope = scope
    with scope:
        w = k.sb(f"router_w_{tag}", [P, KC, NL])
        b = k.sb(f"router_b_{tag}", [P, NL])
        lg = k.sb(f"logits_{tag}", [P, NJ, NL])
        eq = k.sb(f"eq_{tag}", [P, NJ, NL])
        s1 = k.sb(f"sel1_{tag}", [P, NJ, NE])
        m = k.sb(f"max_{tag}", [P, 8, NJ])
        ge = k.sb(f"gexp_{tag}", [P, NJ, NG])
        sel = k.sb(f"sel_{tag}", [P, NJ, NE])
        cnt = k.sb(f"count_{tag}", [P, 2])
        lp = k.ps(f"logit_ps_{tag}", [P, NJ, NL])
        pp = k.ps(f"place_ps_{tag}", [P, NJ + 1, NE])
        rank = k.tab[:, OFF["rank"]:OFF["rank"] + NL]
        with nc.Block() as block:
            @block.sync
            def _(sp):
                sp.dma_start(w[:, :, 0:NG], w_group.rearrange("(p c) n -> p c n", c=KC)).then_inc(s_ld, 16)
                sp.dma_start(w[:, :, NG:], w_fine.rearrange("(p c) n -> p c n", c=KC)).then_inc(s_ld, 16)
                if b_group is not None:
                    sp.dma_start(b[:, 0:NG], b_group.broadcast_to([P, NG])).then_inc(s_b, 16)
                    sp.dma_start(b[:, NG:], b_fine.broadcast_to([P, NE])).then_inc(s_b, 16)

            @block.tensor
            def _(pe):
                pe.wait_ge(s_ld, 32)
                for j in range(NJ):
                    for c in range(KC):
                        last = nc.tensor.matmul(lp[:, j, :], k.hT[:, c, j * P:(j + 1) * P], w[:, c, :],
                                                start=(c == 0), stop=(c == KC - 1))
                last.then_inc(s_p, 1)
                pe.wait_ge(s_sel, 1)
                for j in range(NJ + 1):
                    for i in range(min(j + 1, NJ)):
                        t = k.table("before" if i == j else "ones")
                        last = nc.tensor.matmul(pp[:, j], t, sel[:, i], start=(i == 0), stop=(i == min(j, NJ - 1)))
                last.then_inc(s_pos, 1)

            @block.scalar
            def _(act):
                act.wait_ge(s_d, 1)
                nc.scalar.activation(ge[:], ge[:], ACT.Exp).then_inc(s_e, 1)
                act.wait_ge(s_d, 2)
                nc.scalar.activation(m[:, 3], m[:, 3], ACT.Exp).then_inc(s_e, 1)

            @block.vector
            def _(dve):
                o = Order(dve, k.order["dve"])
                tt, ts = nc.vector.tensor_tensor, nc.vector.tensor_scalar

                def first_max(x, n, r, top, sel):
                    o(nc.vector.tensor_reduce(top, x, AX.X, ALU.max))
                    o(tt(sel, x, bc(top, 2, n), ALU.is_equal))
                    o(tt(sel, sel, bc(r, 1, NJ), ALU.mult))
                    o(nc.vector.tensor_reduce(m[:, 7], sel, AX.X, ALU.max))
                    o(tt(sel, sel, bc(m[:, 7], 2, n), ALU.is_equal))

                dve.wait_ge(s_p, 1)
                if b_group is not None:
                    dve.wait_ge(s_b, 32)
                    o(tt(lg[:], lp[:], bc(b[:], 1, NJ), ALU.add))
                else:
                    o(nc.vector.tensor_copy(lg[:], lp[:]))
                grp, fine = lg[:, :, 0:NG], lg[:, :, NG:]
                gs, s2 = eq[:, :, 0:NG], eq[:, :, NG:]
                first_max(grp, NG, rank[:, 0:NG], m[:, 0], gs)
                tt(ge[:], grp, bc(m[:, 0], 2, NG), ALU.subtract).then_inc(s_d, 1)
                o(ts(gs, gs, -1.0, BIG, ALU.add, ALU.mult))
                for j in range(NJ):
                    f = fine[:, j].rearrange("p (g e) -> p g e", g=NG)
                    o(tt(f, f, bc(gs[:, j], 2, EPG), ALU.add))
                first_max(fine, NE, rank[:, NG:], m[:, 1], s1[:])
                o(ts(s2, s1[:], -BIG, None, ALU.mult))
                o(tt(fine, fine, s2, ALU.add))
                first_max(fine, NE, rank[:, NG:], m[:, 2], s2)
                tt(m[:, 3], m[:, 2], m[:, 1], ALU.subtract).then_inc(s_d, 1)
                tt(sel[:], s1[:], s2, ALU.add).then_inc(s_sel, 1)
                o(nc.vector.memset(k.gates[:, :, NE:], 0.0))
                o(nc.vector.memset(k.place[:, :, NE:], -1.0))
                dve.wait_ge(s_e, 1)
                o(nc.vector.tensor_reduce(m[:, 4], ge[:], AX.X, ALU.add))
                dve.wait_ge(s_e, 2)
                o(ts(m[:, 5], m[:, 3], 1.0, None, ALU.add))
                o(tt(m[:, 5], m[:, 5], m[:, 4], ALU.mult))
                o(nc.vector.reciprocal(m[:, 5], m[:, 5]))
                o(tt(m[:, 6], m[:, 5], m[:, 3], ALU.mult))
                o(tt(s1[:], s1[:], bc(m[:, 5], 2, NE), ALU.mult))
                o(tt(s2, s2, bc(m[:, 6], 2, NE), ALU.mult))
                g, pl = k.gates[:, :, 0:NE], k.place[:, :, 0:NE]
                o(tt(g, s1[:], s2, ALU.add))
                dve.wait_ge(s_pos, 1)
                dve.wait_ge(s_sel, 1)
                o(nc.vector.scalar_tensor_tensor(out=pl, in0=pp[:, 0:NJ], scalar=1.0, in1=sel[:],
                                                 op0=ALU.add, op1=ALU.mult))
                o(ts(pl, pl, -1.0, None, ALU.add))
                o(ts(sel[:], pl, float(CAP), None, ALU.is_ge))
                o(tt(k.over[:], sel[:], g, ALU.mult))
                o(nc.vector.tensor_reduce(cnt[:, 0:1], pp[:, NJ], AX.X, ALU.max))
                o(ts(cnt[:, 1:2], cnt[:, 0:1], float(CAP), None, ALU.is_gt))
                o(nc.vector.tensor_copy(k.over_flag[:], cnt[0:1, 1:2]))
                o.restart()
    k.scope = k.ctx


class Experts:

    def __init__(self, k, tag, H, w_gate, w_up, w_down):
        HT = H // P
        self.tag, self.H, self.dram = tag, H, (w_gate, w_up, w_down)
        self.wg = k.carve(k.pool, 0, [P, 2, KC, H])
        self.wu = k.carve(k.pool, 2 * KC * H, [P, 2, KC, H])
        self.wd = k.carve(k.pool, 4 * KC * H, [P, 2, HT, D])
        self.views = (w_gate.rearrange("e (p c) n -> e p c n", c=KC), w_up.rearrange("e (p c) n -> e p c n", c=KC),
                      w_down.rearrange("e (c p) n -> e p c n", p=P))
        live, k.live = k.live, None
        self.sems = [k.sem(f"{n}_{tag}") for n in ("w_gate_loaded", "w_up_loaded", "w_down_loaded")]
        k.live = live

    def load(self, sp, which, pair):
        w = (self.wg, self.wu, self.wd)[which]
        for b in range(2):
            sp.dma_start(w[:, b], self.views[which][pair * 2 + b]).then_inc(self.sems[which], 16)

    def first(self, sp):
        for which in range(3):
            self.load(sp, which, 0)


def stage_experts(k, ex, alpha, ahead=None):
    stage_packed(k, ex, alpha, ahead)
    full = k.nc.values_load(k.over_flag[0:1, 0:1], min_val=0, max_val=1)
    with k.nc.If(full > 0):
        stage_general(k, ex.tag + "g", ex.H, *ex.dram)
    with k.nc.Else():
        k.nc.all_engine_barrier()


def stage_packed(k, ex, alpha, ahead):
    nc = k.nc
    tag, H = ex.tag, ex.H
    HT = H // P
    NI = NE // 2
    rows = k.h_rows
    s_lg, s_lu, s_ld = ex.sems
    wg, wu, wd = ex.wg, ex.wu, ex.wd
    (s_pm, s_gx, s_xg, s_g, s_u, s_sg, s_hid, s_pg, s_pt, s_pgs, s_ht, s_hts, s_y, s_ys,
     s_sc, s_add, s_x, s_z) = (k.sem(f"{n}_{tag}") for n in (
         "onehot_done", "rows_gathered", "gathered_out",
         "gate_product", "up_product", "silu_done", "hidden_done", "gated_onehot_done", "onehot_turned",
         "turned_onehot_out", "hidden_turned", "turned_hidden_out", "y_product", "y_out", "y_scattered",
         "y_added", "x_scaled", "zeroed"))
    scope = ExitStack()
    k.scope = scope
    with scope:
        one = k.sb(f"onehot_{tag}", [P, NJ, 2, CAP])
        gone = k.sb(f"gated_onehot_{tag}", [P, NJ, 2, CAP])
        goneT = k.sb(f"gated_onehot_T_{tag}", [P, T])
        xgT = k.sb(f"gathered_T_{tag}", [P, KC, P])
        sg = k.sb(f"silu_{tag}", [P, H])
        hid = k.sb(f"hidden_{tag}", [P, H])
        hidT = k.sb(f"hidden_T_{tag}", [P, HT, P])
        y = k.sb(f"y_{tag}", [P, 2, W])
        XG = k.ps(f"gather_ps_{tag}", [P, 2, W])
        SC = k.ps(f"scatter_ps_{tag}", [P, W])
        G = k.ps(f"gate_ps_{tag}", [P, W])
        Up = k.ps(f"up_ps_{tag}", [P, W])
        TP = k.ps(f"turn_ps_{tag}", [P, W])
        Y = k.ps(f"y_ps_{tag}", [P, 2, W])
        scatter_bank = [XG[:, 0], XG[:, 1], SC[:], XG[:, 0]]
        with nc.Block() as block:
            @block.sync
            def _(sp):
                with nc.sync.Fori(1, NI) as it:
                    sp.wait_ge(s_g, it)
                    ex.load(sp, 0, it)
                    sp.wait_ge(s_u, it)
                    ex.load(sp, 1, it)
                    sp.wait_ge(s_y, it * 2)
                    ex.load(sp, 2, it)
                if ahead is not None:
                    ahead(sp)

            @block.tensor
            def _(pe):
                mm = nc.tensor.matmul

                def gather():
                    for n in range(2):
                        for c in range(4):
                            for j in range(NJ):
                                last = mm(XG[:, n, c * P:(c + 1) * P], rows[:, j, 4 * n + c:D:KC],
                                          one[:, j], start=(j == 0), stop=(j == NJ - 1))
                        last.then_inc(s_gx, 1)

                def both_experts(out, stationary, w, s_done):
                    for c in range(len(w[0])):
                        for b in range(2):
                            last = mm(out[b * CAP:(b + 1) * CAP, 0:w[b][c].shape[-1]],
                                      stationary(c)[:, b * CAP:(b + 1) * CAP], w[b][c],
                                      start=(c == 0), stop=(c == len(w[0]) - 1))
                    last.then_inc(s_done, 1)

                def scatter(base):
                    for o in range(4):
                        if o == 3:
                            pe.wait_ge(s_add, base + 1)
                        mm(scatter_bank[o], goneT[:, (o // 2) * P:(o // 2 + 1) * P], y[:, o % 2],
                           start=True, stop=True).then_inc(s_sc, 1)

                pe.wait_ge(s_pm, 1)
                gather()
                with nc.tensor.Fori(0, NI) as it:
                    pe.wait_ge(s_xg, it * 2 + 2)
                    pe.wait_ge(s_lg, it * 32 + 32)
                    both_experts(G, lambda c: xgT[:, c], [[wg[:, b, c] for c in range(KC)] for b in range(2)], s_g)
                    pe.wait_ge(s_lu, it * 32 + 32)
                    both_experts(Up, lambda c: xgT[:, c], [[wu[:, b, c] for c in range(KC)] for b in range(2)], s_u)
                    pe.wait_ge(s_ys, it * 2 + 2)
                    pe.wait_ge(s_pgs, it + 1)
                    scatter(it * 4)
                    pe.wait_ge(s_pg, it + 1)
                    for j in range(NJ):
                        last = nc.tensor.transpose(TP[:, j * P:(j + 1) * P],
                                                   gone[:, j].rearrange("p b s -> p (b s)"), k.table("ident"))
                    last.then_inc(s_pt, 1)
                    pe.wait_ge(s_pm, it + 2)
                    pe.wait_ge(s_add, it * 4 + 4)
                    gather()
                    pe.wait_ge(s_hid, it + 1)
                    pe.wait_ge(s_pgs, it + 2)
                    for m in range(HT):
                        last = nc.tensor.transpose(TP[:, m * P:(m + 1) * P], hid[:, m * P:(m + 1) * P],
                                                   k.table("ident"))
                    last.then_inc(s_ht, 1)
                    pe.wait_ge(s_hts, it + 1)
                    pe.wait_ge(s_ld, it * 32 + 32)
                    for n in range(2):
                        both_experts(Y[:, n], lambda c: hidT[:, c],
                                     [[wd[:, b, c, n * W:(n + 1) * W] for c in range(HT)] for b in range(2)], s_y)
                pe.wait_ge(s_ys, 2 * NI + 2)
                pe.wait_ge(s_xg, 2 * NI + 2)
                scatter(4 * NI)

            @block.scalar
            def _(act):
                def gathered(base):
                    for n in range(2):
                        act.wait_ge(s_gx, base + (n + 1))
                        nc.scalar.activation(xgT[:, 4 * n:4 * n + 4].rearrange("p c s -> p (c s)"), XG[:, n],
                                             ACT.Copy).then_inc(s_xg, 1)

                gathered(0)
                with nc.scalar.Fori(0, NI) as it:
                    act.wait_ge(s_g, it + 1)
                    nc.scalar.activation(sg[:], G[:, 0:H], ACT.Silu).then_inc(s_sg, 1)
                    act.wait_ge(s_pt, it + 1)
                    nc.scalar.activation(goneT[:], TP[:, 0:T], ACT.Copy).then_inc(s_pgs, 1)
                    gathered(it * 2 + 2)
                    act.wait_ge(s_ht, it + 1)
                    nc.scalar.activation(hidT[:].rearrange("p c s -> p (c s)"), TP[:, 0:HT * P],
                                         ACT.Copy).then_inc(s_hts, 1)
                    for n in range(2):
                        act.wait_ge(s_y, it * 2 + (n + 1))
                        nc.scalar.activation(y[:, n], Y[:, n], ACT.Copy).then_inc(s_ys, 1)

            @block.vector
            def _(dve):
                slots = bc(bc(k.tab[:, OFF["slot"]:OFF["slot"] + CAP], 1, 2), 1, NJ)

                def onehot(pair):
                    nc.vector.tensor_tensor(one[:], slots, bc(k.place[:, :, bass.ds(pair * 2, 2)], 3, CAP),
                                            ALU.is_equal).then_inc(s_pm, 1)

                def gated(pair):
                    nc.vector.tensor_tensor(gone[:], one[:], bc(k.gates[:, :, bass.ds(pair * 2, 2)], 3, CAP),
                                            ALU.mult).then_inc(s_pg, 1)

                def add(base):
                    for o in range(4):
                        dve.wait_ge(s_sc, base + (o + 1))
                        xs = k.x[:, o // 2, (o % 2) * W:(o % 2 + 1) * W]
                        nc.vector.tensor_tensor(xs, xs, scatter_bank[o], ALU.add).then_inc(s_add, 1)

                nc.vector.memset(y[:], 0.0).then_inc(s_ys, 2)
                nc.vector.memset(goneT[:], 0.0).then_inc(s_pgs, 1)
                nc.vector.tensor_scalar(k.x[:], k.x[:], alpha, None, ALU.mult).then_inc(s_x, 1)
                nc.vector.tensor_tensor(one[:], slots, bc(k.place[:, :, 0:2], 3, CAP), ALU.is_equal).then_inc(s_pm, 1)
                dve.wait_ge(s_x, 1)
                dve.wait_ge(s_pm, 1)
                nc.vector.tensor_tensor(gone[:], one[:], bc(k.gates[:, :, 0:2], 3, CAP), ALU.mult).then_inc(s_pg, 1)
                with nc.vector.Fori(0, NI) as it:
                    dve.wait_ge(s_gx, it * 2 + 2)
                    dve.wait_ge(s_pg, it + 1)
                    onehot(it + 1)
                    dve.wait_ge(s_u, it + 1)
                    dve.wait_ge(s_sg, it + 1)
                    nc.vector.tensor_tensor(hid[:], sg[:], Up[:, 0:H], ALU.mult).then_inc(s_hid, 1)
                    add(it * 4)
                    dve.wait_ge(s_pm, it + 2)
                    dve.wait_ge(s_pt, it + 1)
                    gated(it + 1)
                    dve.wait_ge(s_add, it * 4 + 4)
                add(4 * NI)
    k.scope = k.ctx


def stage_general(k, tag, H, w_gate, w_up, w_down):
    nc = k.nc
    HT = H // P
    NP2 = HT // 2
    NI = NE // 2
    s_lg, s_lu, s_ld = ([k.sem(f"{n}_{tag}{b}") for b in range(2)] for n in
                        ("w_gate_loaded", "w_up_loaded", "w_down_loaded"))
    s_g, s_u, s_sg, s_hid, s_dn, s_yp, s_y, s_used = (k.sem(f"{n}_{tag}") for n in (
        "gate_product", "up_product", "silu_done", "hidden_done", "down_used", "down_product", "y_added",
        "up_used"))
    scope = ExitStack()
    k.scope = scope
    with scope:
        wg = [k.carve(k.pool, b * KC * H, [P, KC, H]) for b in range(2)]
        wu = [k.carve(k.pool, (2 + b) * KC * H, [P, KC, H]) for b in range(2)]
        wd = [k.carve(k.pool, (4 + b) * KC * H, [P, HT, D]) for b in range(2)]
        sg = k.sb(f"silu_{tag}", [P, NP2, 2 * T])
        hid = [k.sb(f"hid_{tag}{b}", [P, NP2, 2 * T]) for b in range(2)]
        pg = k.ps(f"gate_ps_{tag}", [P, NP2, 2 * T])
        pu = k.ps(f"up_ps_{tag}", [P, NP2, 2 * T])
        py = k.ps(f"y_ps_{tag}", [P, NJ, 2, W])
        vg = w_gate.rearrange("e (p c) n -> e p c n", c=KC)
        vu = w_up.rearrange("e (p c) n -> e p c n", c=KC)
        vd = w_down.rearrange("e (c p) n -> e p c n", p=P)
        with nc.Block() as block:
            @block.sync
            def _(sp):
                def load(b, e):
                    sp.dma_start(wg[b][:], vg[e]).then_inc(s_lg[b], 16)
                    sp.dma_start(wu[b][:], vu[e]).then_inc(s_lu[b], 16)

                for b in range(2):
                    load(b, b)
                    sp.dma_start(wd[b][:], vd[b]).then_inc(s_ld[b], 16)
                with nc.sync.Fori(1, NI) as it:
                    for b in range(2):
                        sp.wait_ge(s_used, it * 2 + (b - 1))
                        load(b, it * 2 + b)
                        sp.wait_ge(s_dn, it * 2 + (b + 1))
                        sp.dma_start(wd[b][:], vd[it * 2 + b]).then_inc(s_ld[b], 16)

            @block.tensor
            def _(pe):
                pe.sem_inc(s_dn, 2)
                with nc.tensor.Fori(0, NI) as it:
                    for b in range(2):
                        for pr in range(NP2):
                            pe.wait_ge(s_hid, it * (2 * NP2) + (b * NP2 + pr + 1))
                            for w, ps, s_l, s_p in ((wg, pg, s_lg, s_g), (wu, pu, s_lu, s_u)):
                                if pr == 0:
                                    pe.wait_ge(s_l[b], it * 16 + 16)
                                for m in range(2):
                                    for c in range(KC):
                                        n0 = (2 * pr + m) * P
                                        last = nc.tensor.matmul(ps[:, pr, m * T:(m + 1) * T],
                                                                w[b][:, c, n0:n0 + P], k.hT[:, c, :],
                                                                start=(c == 0), stop=(c == KC - 1))
                                last.then_inc(s_p, 1)
                        pe.wait_ge(s_u, it * (2 * NP2) + (b + 1) * NP2)
                        pe.sem_inc(s_used, 1)
                        pe.wait_ge(s_ld[b], it * 16 + 16)
                        pe.wait_ge(s_hid, it * (2 * NP2) + (b + 2) * NP2)
                        for j in range(NJ):
                            for n in range(2):
                                g = 2 * j + n
                                pe.wait_ge(s_y, it * 8 + (4 * b + g + 1))
                                for m in range(HT):
                                    hm = hid[b][:, m // 2, (m % 2) * T + j * P:(m % 2) * T + (j + 1) * P]
                                    last = nc.tensor.matmul(py[:, j, n, :], hm, wd[b][:, m, n * W:(n + 1) * W],
                                                            start=(m == 0), stop=(m == HT - 1))
                                last.then_inc(s_yp, 1)
                        pe.wait_ge(s_yp, it * 8 + (4 * b + 4))
                        pe.sem_inc(s_dn, 1)

            @block.scalar
            def _(act):
                with nc.scalar.Fori(0, NI) as it:
                    for b in range(2):
                        for pr in range(NP2):
                            n = it * (2 * NP2) + (b * NP2 + pr + 1)
                            act.wait_ge(s_hid, n)
                            act.wait_ge(s_g, n)
                            nc.scalar.activation(sg[:, pr], pg[:, pr], ACT.Silu).then_inc(s_sg, 1)

            @block.vector
            def _(dve):
                dve.sem_inc(s_hid, NP2)
                dve.sem_inc(s_y, 4)
                with nc.vector.Fori(0, NI) as it:
                    for b in range(2):
                        dve.wait_ge(s_dn, it * 2 + (b + 1))
                        for pr in range(NP2):
                            n = it * (2 * NP2) + (b * NP2 + pr + 1)
                            dve.wait_ge(s_u, n)
                            dve.wait_ge(s_sg, n)
                            nc.vector.tensor_tensor(hid[b][:, pr], sg[:, pr], pu[:, pr], ALU.mult).then_inc(s_hid, 1)
                        for j in range(NJ):
                            for h in range(2):
                                n = it * 8 + (4 * b + 2 * j + h + 1)
                                dve.wait_ge(s_y, n)
                                dve.wait_ge(s_yp, n)
                                xs = k.x[:, j, h * W:(h + 1) * W]
                                nc.vector.scalar_tensor_tensor(
                                    out=xs, in0=py[:, j, h, :], scalar=k.over[:, j, bass.ds(it * 2 + b, 1)],
                                    in1=xs, op0=ALU.mult, op1=ALU.add).then_inc(s_y, 1)
                dve.wait_ge(s_y, 4 * NE + 4)
    k.scope = k.ctx


def load_even(k, sp):
    sp.dma_start(k.w_even0[:], k.i["w_in_even"].rearrange("(p c) n -> p c n", c=KC)[:, :, 0:W]).then_inc(
        k.s_even0, 16)


def stage_even_project(k):
    nc, i = k.nc, k.i
    N = i["w_in_even"].shape[1]
    k.en = k.sb("even_nat", [P, NJ, N])
    s_w = [k.s_even0] + [k.sem(f"w_even_loaded{b}") for b in (1, 2)]
    s_p, s_o = k.sem("even_product"), k.sem("even_out")
    scope = ExitStack()
    k.scope = scope
    src = i["w_in_even"].rearrange("(p c) n -> p c n", c=KC)
    cuts = [(n, min(W, N - n)) for n in range(0, N, W)]
    with scope:
        w = [k.w_even0] + [k.carve(k.pool, b * KC * W, [P, KC, W]) for b in range(2)]
        ps = k.ps("even_ps", [P, 2, NJ, W])
        with nc.Block() as block:
            @block.sync
            def _(sp):
                for n, (a, width) in enumerate(cuts):
                    if n == 0:
                        continue
                    if n >= 3:
                        sp.wait_ge(s_p, n - 2)
                    sp.dma_start(w[n % 3][:, :, 0:width], src[:, :, a:a + width]).then_inc(s_w[n % 3], 16)

            @block.tensor
            def _(pe):
                for n, (a, width) in enumerate(cuts):
                    pe.wait_ge(s_w[n % 3], 16 * (n // 3 + 1))
                    if n >= 2:
                        pe.wait_ge(s_o, n - 1)
                    for j in range(NJ):
                        for c in range(KC):
                            last = nc.tensor.matmul(ps[:, n % 2, j, 0:width], k.hT[:, c, j * P:(j + 1) * P],
                                                    w[n % 3][:, c, 0:width], start=(c == 0), stop=(c == KC - 1))
                    last.then_inc(s_p, 1)

            @block.scalar
            def _(act):
                for n, (a, width) in enumerate(cuts):
                    act.wait_ge(s_p, n + 1)
                    nc.scalar.activation(k.en[:, :, a:a + width], ps[:, n % 2, :, 0:width], ACT.Copy).then_inc(s_o, 1)
    k.scope = k.ctx


def stage_even_mix(k):
    nc, i = k.nc, k.i
    RD = 128
    k.mix = k.h_rows
    names = ("tables", "rot_a", "rot_b", "rot_c", "rot_d", "rotated", "turned", "turned_out", "lg_abs", "lg_exp",
             "lg_ln", "dist", "dist_exp", "ret_scores", "ret_weighted", "ret_product", "win_scores", "win_masked",
             "win_diff", "win_exp", "p_turned", "p_out", "win_product", "sink_diff", "ret_out", "gn_sq", "gn_inv",
             "gn_rstd", "silu")
    s = {n: k.sem(f"even_{n}") for n in names}
    scope = ExitStack()
    k.scope = scope
    with scope:
        at = [0]

        def room(shape):
            at[0] += int(np.prod(shape[1:]))
            return k.carve(k.pool, at[0] - int(np.prod(shape[1:])), shape)

        lgt = k.sb("ret_logit", [P, 2 * RET_H])
        lga = k.sb("ret_logit_abs", [P, 2 * RET_H])
        sink = k.sb("sink", [P, WIN_H])
        gn = k.sb("ret_gain", [P, W])
        tb = room([P, ROPE_N + 6 * T])
        rot = room([P, NJ, W * 2 + 640])
        ta = room([P, NJ, 8, 64])
        tc_ = room([P, NJ, 8, 64])
        rT = room([P, 8, T])
        wT = room([P, 5, T])
        dm = room([P, RET_H, NJ * T])
        st = room([P, RET_H, NJ, T])
        sc = room([P, WIN_H, NJ, T])
        pT = room([P, WIN_H, NJ, T])
        ya = room([P, NJ, RET_H, RD])
        sq = ta[:].rearrange("p j (h a) d -> p j h (a d)", a=2)
        sm = k.sb("even_small", [P, 10, NJ, WIN_H])
        pb = [k.ps(f"even_ps{b}", [P, W]) for b in range(8)]
        o64 = 2 * 64 * NJ
        cos = {64: tb[:, 0:64 * NJ], 32: tb[:, o64:o64 + 32 * NJ]}
        sin = {64: tb[:, 64 * NJ:o64], 32: tb[:, o64 + 32 * NJ:ROPE_N]}
        ahead, behind = tb[:, ROPE_N:ROPE_N + 2 * T], tb[:, ROPE_N + 2 * T:ROPE_N + 4 * T]
        wmask = tb[:, ROPE_N + 4 * T:]
        groups = [(0, 8, 64, 0, 128), (4 * W, 4, 32, 2 * W, 128), (4 * W + 256, 4, 32, 2 * W + 64, 128),
                  (5 * W, 2, 32, 2 * W + 512, 64)]

        def halves(x, a, n, half, j, step):
            if step == 2 * half:
                v = x[:, j, a:a + n * step].rearrange("p (h s d) -> p h s d", h=n, s=2)
                return v[:, :, 0], v[:, :, 1]
            at = 2 * W + (a - 2 * W) % step
            v = x[:, j, 2 * W:2 * W + n * step].rearrange("p (h s) -> p h s", h=n)
            return v[:, :, at - 2 * W:at - 2 * W + half], v[:, :, at - 2 * W + half:at - 2 * W + 2 * half]

        def angle(t, half, j, n):
            return bc(t[half][:, j * half:(j + 1) * half], 1, n)

        def turn_list():
            out = []
            for h in range(8):
                out.append((h // 2, (h % 2) * 2, lambda j, h=h: rot[:, j, h * RD:(h + 1) * RD]))
            for m in range(4):
                out.append((4 + m // 2, (m % 2) * 2,
                            lambda j, m=m: rot[:, j, 2 * W + m * P:2 * W + (m + 1) * P]))
            out.append((6, 0, lambda j: rot[:, j, 2 * W + 512:2 * W + 640]))
            return out

        with nc.Block() as block:
            @block.sync
            def _(sp):
                sp.dma_start(tb[:], i["even_tables"]).then_inc(s["tables"], 16)
                sp.dma_start(lgt[:], i["ret_decay_logit"].broadcast_to([P, 2 * RET_H])).then_inc(s["tables"], 16)
                sp.dma_start(gn[:], i["ret_gn_gain"].broadcast_to([P, W])).then_inc(s["tables"], 16)
                sp.dma_start(sink[:], i["sink_logit"].broadcast_to([P, WIN_H])).then_inc(s["tables"], 16)

            @block.gpsimd
            def _(pool):
                o = Order(pool, k.order["pool"])
                pool.wait_ge(s["tables"], 64)
                tt = nc.gpsimd.tensor_tensor
                for a, n, half, b, step in groups:
                    for j in range(NJ):
                        x1, x2 = halves(k.en, a, n, half, j, 2 * half)
                        _, y2 = halves(rot, b, n, half, j, step)
                        t1 = tc_[:, j, 0:n, 0:half]
                        o(tt(t1, x1, angle(sin, half, j, n), ALU.mult))
                        o(tt(y2, x2, angle(cos, half, j, n), ALU.mult))
                        o(tt(y2, y2, t1, ALU.add))
                pool.sem_inc(s["rotated"], 1)
                o.restart()

            @block.vector
            def _(dve):
                o = Order(dve, k.order["dve"])
                tt, ts, stt = nc.vector.tensor_tensor, nc.vector.tensor_scalar, nc.vector.scalar_tensor_tensor
                red = nc.vector.tensor_reduce
                dve.wait_ge(s["tables"], 64)
                o(ts(lga[:], lgt[:], -1.0, None, ALU.mult))
                tt(lga[:], lga[:], lgt[:], ALU.max).then_inc(s["lg_abs"], 1)
                for a, n, half, b, step in groups:
                    for j in range(NJ):
                        x1, x2 = halves(k.en, a, n, half, j, 2 * half)
                        y1, _ = halves(rot, b, n, half, j, step)
                        t1 = ta[:, j, 0:n, 0:half]
                        o(tt(t1, x2, angle(sin, half, j, n), ALU.mult))
                        o(tt(y1, x1, angle(cos, half, j, n), ALU.mult))
                        o(tt(y1, y1, t1, ALU.subtract))
                dve.sem_inc(s["rotated"], 1)
                dve.wait_ge(s["lg_ln"], 1)
                o(ts(lgt[:], lgt[:], 0.0, None, ALU.min))
                o(tt(lgt[:], lgt[:], lga[:], ALU.subtract))
                for h in range(RET_H):
                    o(ts(dm[:, h], ahead, lgt[:, h:h + 1], None, ALU.mult))
                    stt(out=dm[:, h], in0=behind, scalar=lgt[:, RET_H + h:RET_H + h + 1], in1=dm[:, h],
                        op0=ALU.mult, op1=ALU.add).then_inc(s["dist"], 1)
                for h in range(RET_H):
                    dve.wait_ge(s["ret_scores"], h + 1)
                    dve.wait_ge(s["dist_exp"], h + 1)
                    tt(st[:, h].rearrange("p a t -> p (a t)"), pb[h][:], dm[:, h], ALU.mult).then_inc(s["ret_weighted"], 1)
                for h in range(WIN_H):
                    dve.wait_ge(s["win_scores"], h + 1)
                    tt(sc[:, h].rearrange("p a t -> p (a t)"), pb[4 + h % 4][:], wmask, ALU.add).then_inc(s["win_masked"], 1)
                dve.wait_ge(s["win_masked"], WIN_H)
                hj = "p a h -> p h a"
                o(red(sm[:, 0].rearrange(hj), sc[:], AX.X, ALU.max))
                o(tt(sm[:, 0], sm[:, 0], bc(sink[:], 1, NJ), ALU.max))
                o(tt(sm[:, 1], bc(sink[:], 1, NJ), sm[:, 0], ALU.subtract))
                for j in range(NJ):
                    tt(sc[:, :, j], sc[:, :, j], bc(sm[:, 0, j], 2, T), ALU.subtract).then_inc(s["win_diff"], 1)
                dve.wait_ge(s["ret_product"], 1)
                yp = pb[0][:].rearrange("p (h d) -> p h d", h=RET_H), pb[1][:].rearrange("p (h d) -> p h d", h=RET_H)
                for j in range(NJ):
                    o(nc.vector.tensor_copy(ya[:, j], yp[j]))
                o(red(sm[:, 2, :, 0:RET_H], ya[:], AX.X, ALU.add))
                o(ts(sm[:, 2, :, 0:RET_H], sm[:, 2, :, 0:RET_H], 1.0 / RD, None, ALU.mult))
                o(tt(ya[:], ya[:], bc(sm[:, 2, :, 0:RET_H], 3, RD), ALU.subtract))
                o(tt(sq[:], ya[:], ya[:], ALU.mult))
                o(red(sm[:, 3, :, 0:RET_H], sq[:], AX.X, ALU.add))
                o(ts(sm[:, 3, :, 0:RET_H], sm[:, 3, :, 0:RET_H], 1.0 / RD, GN_EPS, ALU.mult, ALU.add))
                nc.vector.reciprocal(sm[:, 4, :, 0:RET_H], sm[:, 3, :, 0:RET_H]).then_inc(s["gn_inv"], 1)
                dve.wait_ge(s["gn_rstd"], 1)
                refine(nc, o, sm[:, 5, :, 0:RET_H], sm[:, 3, :, 0:RET_H], sm[:, 4, :, 0:RET_H])
                o(tt(ya[:], ya[:], bc(sm[:, 5, :, 0:RET_H], 3, RD), ALU.mult))
                ma = k.mix[:, :, 0:W]
                o(tt(ma, ya[:].rearrange("p j h d -> p j (h d)"), bc(gn[:], 1, NJ), ALU.mult))
                dve.wait_ge(s["silu"], 1)
                o(tt(ma, ma, k.en[:, :, 3 * W:4 * W], ALU.mult))
                dve.wait_ge(s["win_exp"], 3)
                o(red(sm[:, 6].rearrange(hj), sc[:], AX.X, ALU.add))
                o(tt(sm[:, 6], sm[:, 6], sm[:, 7], ALU.add))
                o(nc.vector.reciprocal(sm[:, 8], sm[:, 6]))
                for h in range(WIN_H):
                    if h % 2:
                        dve.wait_ge(s["p_turned"], h + 1)
                        nc.vector.tensor_copy(pT[:, h].rearrange("p a t -> p (a t)"), pb[h][:]).then_inc(s["p_out"], 1)
                dve.wait_ge(s["win_product"], 1)
                for j in range(NJ):
                    o(tt(k.mix[:, j, W:].rearrange("p (h d) -> p h d", h=WIN_H),
                         pb[6 + j][:].rearrange("p (h d) -> p h d", h=WIN_H), bc(sm[:, 8, j], 2, WIN_D), ALU.mult))
                o.restart()

            @block.scalar
            def _(act):
                act.wait_ge(s["lg_abs"], 1)
                nc.scalar.activation(lga[:], lga[:], ACT.Exp, scale=-1.0).then_inc(s["lg_exp"], 1)
                act.wait_ge(s["lg_exp"], 1)
                nc.scalar.activation(lga[:], lga[:], ACT.Ln, bias=1.0).then_inc(s["lg_ln"], 1)
                for b in range(7):
                    act.wait_ge(s["turned"], b + 1)
                    got = pb[b][:].rearrange("p (h t) -> p h t", h=2)
                    if b < 4:
                        dst, scale = rT[:, 2 * b:2 * b + 2], (1.0 if b < 2 else RD ** -0.5)
                    elif b < 6:
                        dst, scale = wT[:, 2 * (b - 4):2 * (b - 4) + 2], WIN_D ** -0.5
                    else:
                        dst, scale, got = wT[:, 4:5], 1.0, got[:, 0:1]
                    nc.scalar.activation(dst, got, ACT.Copy, scale=scale).then_inc(s["turned_out"], 1)
                for h in range(RET_H):
                    act.wait_ge(s["dist"], h + 1)
                    nc.scalar.activation(dm[:, h], dm[:, h], ACT.Exp).then_inc(s["dist_exp"], 1)
                act.wait_ge(s["win_diff"], 2)
                nc.scalar.activation(sc[:], sc[:], ACT.Exp).then_inc(s["win_exp"], 2)
                nc.scalar.activation(sm[:, 7], sm[:, 1], ACT.Exp).then_inc(s["win_exp"], 1)
                act.wait_ge(s["gn_inv"], 1)
                nc.scalar.activation(sm[:, 5, :, 0:RET_H], sm[:, 4, :, 0:RET_H], ACT.Sqrt).then_inc(s["gn_rstd"], 1)
                nc.scalar.activation(k.en[:, :, 3 * W:4 * W], k.en[:, :, 3 * W:4 * W], ACT.Silu).then_inc(s["silu"], 1)
                for h in range(0, WIN_H, 2):
                    act.wait_ge(s["p_turned"], h + 1)
                    nc.scalar.activation(pT[:, h].rearrange("p a t -> p (a t)"), pb[h][:], ACT.Copy).then_inc(s["p_out"], 1)

            @block.tensor
            def _(pe):
                mm = nc.tensor.matmul
                pe.wait_ge(s["rotated"], 2)
                turns = turn_list()
                for n, (b, place, cols) in enumerate(turns):
                    for j in range(NJ):
                        last = nc.tensor.transpose(pb[b][:, (place + j) * P:(place + j + 1) * P], cols(j), k.table("ident"))
                    if n == len(turns) - 1 or turns[n + 1][0] != b:
                        last.then_inc(s["turned"], 1)
                pe.wait_ge(s["turned_out"], 7)
                for h in range(RET_H):
                    for sj in range(NJ):
                        last = mm(pb[h][:, sj * T:(sj + 1) * T], rT[:, RET_H + h, sj * P:(sj + 1) * P], rT[:, h, :],
                                  start=True, stop=True)
                    last.then_inc(s["ret_scores"], 1)
                for h in range(WIN_H):
                    m, r = h % 4, slice(64 * (h // 4), 64 * (h // 4) + 64)
                    if h >= 4:
                        pe.wait_ge(s["win_masked"], h - 3)
                    for j in range(NJ):
                        last = mm(pb[4 + h % 4][:, j * T:(j + 1) * T], wT[r, m, j * P:(j + 1) * P], wT[r, 4, :],
                                  start=True, stop=True)
                    last.then_inc(s["win_scores"], 1)
                pe.wait_ge(s["ret_weighted"], RET_H)
                for j in range(NJ):
                    for h in range(RET_H):
                        for sj in range(NJ):
                            last = mm(pb[j][:, h * RD:(h + 1) * RD], st[:, h, sj, j * P:(j + 1) * P],
                                      k.en[:, sj, 2 * W + h * RD:2 * W + (h + 1) * RD],
                                      start=(sj == 0), stop=(sj == NJ - 1))
                last.then_inc(s["ret_product"], 1)
                pe.wait_ge(s["win_exp"], 3)
                pe.wait_ge(s["gn_inv"], 1)
                for h in range(WIN_H):
                    for sj in range(NJ):
                        for j in range(NJ):
                            last = nc.tensor.transpose(pb[h][:, sj * T + j * P:sj * T + (j + 1) * P],
                                                       sc[:, h, j, sj * P:(sj + 1) * P], k.table("ident"))
                    last.then_inc(s["p_turned"], 1)
                pe.wait_ge(s["p_out"], WIN_H)
                for j in range(NJ):
                    for h in range(WIN_H):
                        kv = h // 4
                        for sj in range(NJ):
                            last = mm(pb[6 + j][:, h * WIN_D:(h + 1) * WIN_D], pT[:, h, sj, j * P:(j + 1) * P],
                                      k.en[:, sj, 5 * W + 128 + kv * WIN_D:5 * W + 128 + (kv + 1) * WIN_D],
                                      start=(sj == 0), stop=(sj == NJ - 1))
                last.then_inc(s["win_product"], 1)
    k.scope = k.ctx


def stage_fourier(k, ahead):
    nc = k.nc
    s_t, s_a, s_ao, s_b = (k.sem(f"dft_{n}") for n in ("loaded", "rows_product", "rows_out", "columns_product"))
    scope = ExitStack()
    k.scope = scope
    with scope:
        tab = k.sb("dft_tab", [P, NJ, 2, T])
        a = k.sb("dft_rows", [P, KC, 2, T])
        ps = [k.ps(f"dft_ps{b}", [P, 2, T]) for b in range(8)]
        with nc.Block() as block:
            @block.sync
            def _(sp):
                sp.dma_start(tab[:], k.i["dft"]).then_inc(s_t, 16)
                ahead(sp)

            @block.tensor
            def _(pe):
                pe.wait_ge(s_t, 16)
                for c in range(KC):
                    for j in range(NJ):
                        last = nc.tensor.matmul(ps[c][:], k.x[:, j, c * P:(c + 1) * P], tab[:, j],
                                                start=(j == 0), stop=(j == NJ - 1))
                    last.then_inc(s_a, 1)
                for g in range(KC // 2):
                    pe.wait_ge(s_ao, 4 * (g + 1))
                    for o in range(2):
                        n = 0
                        for f in range(2):
                            for q in range(2):
                                last = nc.tensor.matmul(ps[2 * g + o][:, 0, :], tab[:, q, f, o * P:(o + 1) * P],
                                                        a[:, 2 * g + q, f, :], start=(n == 0), stop=(n == 3))
                                n += 1
                        last.then_inc(s_b, 1)

            @block.scalar
            def _(act):
                for c in range(KC):
                    act.wait_ge(s_a, c + 1)
                    nc.scalar.activation(a[:, c, 0], ps[c][:, 0], ACT.Copy).then_inc(s_ao, 1)
                    nc.scalar.activation(a[:, c, 1], ps[c][:, 1], ACT.Copy, scale=-1.0).then_inc(s_ao, 1)
                for c in range(KC):
                    act.wait_ge(s_b, c + 1)
                    nc.scalar.activation(k.hT[:, c, :], ps[c][:, 0], ACT.Copy, scale=1.0 / T)
    k.scope = k.ctx


def stage_store(k):
    s_o = k.sem("stored")
    with k.nc.Block() as block:
        @block.sync
        def _(sp):
            sp.dma_start(k.out.rearrange("a (j p) d -> p (a j) d", p=P), k.x[:]).then_inc(s_o, 16)
            sp.wait_ge(s_o, 16)


def build(nc, ins, out):
    with ExitStack() as ctx:
        k = Core(nc, ins, out, ctx)
        i = ins
        k.s_out_w, k.s_even0, k.out_loads = k.sem("out_weights_loaded"), k.sem("w_even0_loaded"), 0
        stage_load(k)
        k.live = []
        k.gates = k.sb("gates", [P, NJ, NE + 2])
        k.place = k.sb("place", [P, NJ, NE + 2])
        k.over = k.sb("over", [P, NJ, NE])
        k.over_flag = k.sb("over_flag", [1, 1], I32)
        ex = [Experts(k, "one", H1, i["moe_w_gate"][0], i["moe_w_up"][0], i["moe_w_down"][0])]
        ex += [Experts(k, f"l{n}", H2, i["expert_w_gate"][n], i["expert_w_up"][n], i["expert_w_down"][n])
               for n in range(2)]
        rows_pc, rows_cp = "(p c) n -> p c n", "(c p) n -> p c n"
        with ExitStack() as mixer:
            outer, k.ctx = k.ctx, mixer
            k.scope = mixer
            stage_norm_t(k, "n1", k.x, i["norm1_w"], k.carve(k.pool, 0, [P, NJ, D]))
            stage_project(k)
            stage_gla(k)
            stage_gdn(k, lambda sp: load_out(k, sp, i["w_out"][0].rearrange(rows_pc, c=KC)))
            stage_combine(k, ex[0].first)
            stage_norm_t(k, "mix1", k.oa, None, None)
            k.ctx = k.scope = outer
        stage_out(k, "one", 1.0)
        k.h_rows = k.sb("h_rows", [P, NJ, D])
        stage_norm_t(k, "n2", k.x, i["norm2_w"], k.h_rows,
                     lambda sp: load_out(k, sp, i["w_out_even"].rearrange(rows_pc, c=KC)))
        k.retire()
        stage_router(k, "one", i["moe_w_group"][0], i["moe_w_router"][0])
        with ExitStack() as even:
            outer, k.ctx = k.ctx, even
            k.scope = even
            k.w_even0 = k.sb("w_even0", [P, KC, W])
            stage_experts(k, ex[0], 1.0, lambda sp: load_even(k, sp))
            stage_norm(k, "f", i["norm_f_w"])
            k.retire()
            stage_norm_t(k, "e", k.x, None, None)
            stage_even_project(k)
            stage_even_mix(k)
            stage_norm_t(k, "mix2", k.mix, None, None, ex[1].first)
            k.ctx = k.scope = outer
        for n in range(2):
            if n == 0:
                stage_out(k, "even", ALPHA)
            else:
                k.retire()
                stage_fourier(k, ex[2].first)
                stage_out(k, "fourier", ALPHA)
            stage_norm(k, f"a{n}", i["ln1_gain"][n:n + 1], i["ln1_bias"][n:n + 1])
            stage_norm_t(k, f"moe{n}", k.x, None, k.h_rows,
                         None if n else lambda sp: load_out(k, sp, i["w_out_fourier"].rearrange(rows_cp, p=P)))
            stage_router(k, f"l{n}", i["router_coarse_w"][n], i["router_fine_w"][n],
                         i["router_coarse_b"][n:n + 1], i["router_fine_b"][n:n + 1])
            stage_experts(k, ex[1 + n], ALPHA)
            stage_norm(k, f"b{n}", i["ln2_gain"][n:n + 1], i["ln2_bias"][n:n + 1])
        stage_store(k)


def lay_out(inputs):
    a = {n: np.ascontiguousarray(v) for n, v in inputs.items()}
    w = a["w_in"][0]
    starts = ([0, 512]
              + [3104 + W * n for n in range(6)]
              + [1024, 1536, 2048, 2560]
              + [6176, 6688] + [7232, 7744, 8256, 8768])
    g = 3 * GDN_H
    return {
        "x": a["x"], "norm1_w": a["norm1_w"], "norm2_w": a["norm2_w"], "tables": tables(),
        "w_in_blocks": np.ascontiguousarray(np.stack([w[:, s:s + W] for s in starts])),
        "w_in_small": np.ascontiguousarray(np.concatenate([w[:, 3072:3104], w[:, 7200:7232]], 1)),
        "conv_w": np.ascontiguousarray(
            a["gdn_conv_w"][0].T.reshape(g, P, TAPS).transpose(1, 0, 2).reshape(P, g * TAPS)),
        **{n: a[n] for n in ("gla_gate_w2_fwd", "gla_gate_w2_bwd", "gla_gate_b_fwd", "gla_gate_b_bwd",
                             "gdn_a_log_fwd", "gdn_a_log_bwd", "gdn_dt_bias_fwd", "gdn_dt_bias_bwd",
                             "gla_norm_w", "gdn_norm_w", "w_out", "moe_w_group", "moe_w_router",
                             "moe_w_gate", "moe_w_up", "moe_w_down")},
        "norm_f_w": a["norm_f_w"].reshape(1, D),
        "w_in_even": a["w_in_even_2"][0], "w_out_even": a["w_out_even_2"][0],
        "w_out_fourier": a["w_out_fourier_2"][0],
        "even_tables": even_tables(), "dft": dft_table(),
        "ret_decay_logit": a["ret_decay_logit_2"].reshape(1, 2 * RET_H),
        "ret_gn_gain": a["ret_gn_gain_2"], "sink_logit": a["sink_logit_2"],
        "router_coarse_w": a["router_coarse_w_2"], "router_coarse_b": a["router_coarse_b_2"],
        "router_fine_w": a["router_fine_w_2"], "router_fine_b": a["router_fine_b_2"],
        "expert_w_gate": a["expert_w_gate_2"], "expert_w_up": a["expert_w_up_2"],
        "expert_w_down": a["expert_w_down_2"],
        "ln1_gain": a["ln1_gain_2"], "ln1_bias": a["ln1_bias_2"],
        "ln2_gain": a["ln2_gain_2"], "ln2_bias": a["ln2_bias_2"],
    }


def kernel(**inputs):
    import concourse.bacc as bacc
    from concourse.bass_utils import run_bass_kernel_spmd

    nc = bacc.Bacc("TRN2", target_bir_lowering=False, num_devices=1)
    arrays, args = {}, {}
    for name, a in lay_out(inputs).items():
        arrays[f"in_{name}"] = a
        args[name] = nc.dram_tensor(f"in_{name}", a.shape, F32, kind="ExternalInput").ap()
    out = nc.dram_tensor("out", (1, T, D), F32, kind="ExternalOutput").ap()
    build(nc, args, out)
    r = run_bass_kernel_spmd(nc, [arrays], core_ids=[0])
    return r.results[0]["out"]
```

```python
from contextlib import ExitStack

import numpy as np

import concourse.bass as bass
from concourse import mybir

ALU = mybir.AluOpType
ACT = mybir.ActivationFunctionType
AX = mybir.AxisListType
F32 = mybir.dt.float32
F32R = mybir.dt.float32r
I32 = mybir.dt.int32

P = 128
T = 256
NJ = T // P
D = 1024
KC = D // P
W = 512
EPS = 1e-6
CH = 64

GLA_H, GLA_DK, GLA_DV, RANK, TAU = 4, 128, 256, 16, 16.0
GDN_H, GDN_D, TAPS = 8, 128, 5
NG, NE, EPG = 4, 32, 8
H1, H2 = 256, 512
RET_H, WIN_H, WIN_KV, WIN_D = 4, 8, 2, 64
ALPHA = 4.0 ** 0.25
LN_EPS, GN_EPS = 1e-5, 1e-6
NT_BLOCKS, NN_BLOCKS = 8, 10
BIG = 1e30
CAP = 64


class Order:

    def __init__(self, eng, sem):
        self.eng, self.sem, self.n = eng, sem, 0

    def __call__(self, ins):
        self.n += 1
        ins.then_inc(self.sem, 1)
        self.eng.wait_ge(self.sem, self.n)

    def restart(self):
        self.eng.sem_clear(self.sem)
        self.n = 0


LEVELS = 6
TABLE = dict(ident=P, ones=P, rank=NG + NE, before=P, slot=CAP,
             cum=2 * P, blk=P, half=2 * P, strictn=2 * P, incl=2 * P, lev=LEVELS * 2 * P, lev0=2 * P)
OFF = {}
_at = 0
for _k, _n in TABLE.items():
    OFF[_k] = _at
    _at += _n
TABLE_N, KEPT_N = _at, OFF["cum"]


def tables():
    p = np.arange(P)[:, None]
    x = np.arange(P)[None, :]
    same = (p // CH) == (x // CH)
    f = lambda m: m.astype(np.float32)
    out = dict(
        ident=f(p == x), ones=np.ones((P, P), np.float32),
        cum=np.concatenate([f(same & (p <= x)), f(same & (p >= x))], 1),
        blk=f(same),
        half=np.concatenate([f((p < CH) & (x >= 0)), f((p >= CH) & (x >= 0))], 1),
        strictn=np.concatenate([-f(same & (x < p)), -f(same & (x > p))], 1),
        incl=np.concatenate([f(same & (p <= x)), f(same & (p >= x))], 1),
    )
    lev = []
    for l in range(LEVELS):
        pair = (p >> (l + 1)) == (x >> (l + 1))
        lev.append(f(pair & (((p >> l) & 1) == 0) & (((x >> l) & 1) == 1)))
        lev.append(f(pair & (((p >> l) & 1) == 1) & (((x >> l) & 1) == 0)))
    out["lev"] = np.concatenate(lev, 1)
    out["lev0"] = np.concatenate([lev[1], lev[0]], 1)
    out["rank"] = np.tile(np.concatenate([np.arange(NG, 0, -1), np.arange(NE, 0, -1)]).astype(np.float32), (P, 1))
    out["before"] = f(p < x)
    out["slot"] = np.tile(np.arange(CAP, dtype=np.float32), (P, 1))
    return np.ascontiguousarray(np.concatenate([out[k] for k in TABLE], 1))


def dft_table():
    t = np.arange(T)
    ang = 2 * np.pi * ((t[:, None] * t[None, :]) % T) / T
    both = np.stack([np.cos(ang), np.sin(ang)], 1).astype(np.float32)
    return np.ascontiguousarray(both.reshape(NJ, P, 2, T).transpose(1, 0, 2, 3))


ROPE_N = 2 * (64 + 32) * NJ


def even_tables():
    pos = np.arange(T, dtype=np.float32)
    parts = []
    for half in (64, 32):
        inv = np.float32(10000.0) ** (-np.arange(half, dtype=np.float32) / np.float32(half))
        ang = pos[:, None] * inv[None, :]
        for f in (np.cos, np.sin):
            parts.append(f(ang).astype(np.float32).reshape(NJ, P, half).transpose(1, 0, 2).reshape(P, -1))
    s, t = pos[:, None], pos[None, :]
    rows = lambda m: m.astype(np.float32).reshape(NJ, P, T).transpose(1, 0, 2).reshape(P, -1)
    parts += [rows(np.maximum(t - s, 0)), rows(np.maximum(s - t, 0)),
              rows(np.where(np.abs(s - t) <= P, 0.0, -BIG))]
    return np.ascontiguousarray(np.concatenate(parts, 1))


class Core:

    def __init__(self, nc, ins, out, ctx):
        self.nc, self.i, self.out, self.ctx = nc, ins, out, ctx
        self.live = None
        self.order = {e: self.sem(f"{e}_order") for e in ("dve", "act", "pool", "pe")}
        self.scope = ctx

    def sem(self, name):
        s = self.nc.alloc_semaphore(name=name)
        if self.live is not None:
            self.live.append(s)
        return s

    def retire(self):
        self.nc.all_engine_barrier()
        self.nc.clear_and_free_semaphores(self.live)
        self.nc.all_engine_barrier()
        self.live = []

    def sb(self, name, shape, dt=F32):
        return self.scope.enter_context(self.nc.sbuf_tensor(name, shape, dt))

    def ps(self, name, shape):
        return self.scope.enter_context(self.nc.psum_tensor(name, shape, F32))

    def carve(self, region, at, shape):
        n = int(np.prod(shape[1:]))
        assert at + n <= region.shape[1]
        flat = region[:, at:at + n]
        if len(shape) == 2:
            return flat
        names = "abcd"[:len(shape) - 1]
        return flat.rearrange(f"p ({' '.join(names)}) -> p {' '.join(names)}",
                              **dict(zip(names[1:], shape[2:])))

    def table(self, name, n=0, cols=P):
        a = OFF[name] + n * P
        if a >= KEPT_N:
            return self.mixer_tab[:, a - KEPT_N:a - KEPT_N + cols]
        return self.tab[:, a:a + cols]


def bc(ap, axis, n):
    shape = list(ap.shape)
    return ap.unsqueeze(axis).broadcast_to(shape[:axis] + [n] + shape[axis:])


def refine(nc, o, r, v, tmp):
    o(nc.vector.tensor_tensor(tmp, r, r, ALU.mult))
    o(nc.vector.tensor_tensor(tmp, tmp, v, ALU.mult))
    o(nc.vector.tensor_scalar(tmp, tmp, -0.5, 1.5, ALU.mult, ALU.add))
    o(nc.vector.tensor_tensor(r, r, tmp, ALU.mult))


def stage_load(k):
    nc, i = k.nc, k.i
    k.tab = k.sb("tables", [P, KEPT_N])
    k.x = k.sb("x", [P, NJ, D])
    k.hT = k.sb("hT", [P, KC, T])
    k.pool = k.sb("pool", [P, POOL_N])
    k.store = k.sb("store", [P, STORE_N])
    k.s_small = k.sem("small_loaded")
    with nc.Block() as block:
        @block.sync
        def _(sp):
            sp.dma_start(k.x[:], i["x"].rearrange("a (j p) d -> p (a j) d", p=P)).then_inc(k.s_small, 16)
            sp.dma_start(k.tab[:], i["tables"][:, 0:KEPT_N]).then_inc(k.s_small, 16)
            sp.wait_ge(k.s_small, 32)


def stage_norm_t(k, tag, src, weight, hn, ahead=None):
    nc = k.nc
    s_w, s_ss, s_inv, s_rs, s_h, s_t = (k.sem(f"{n}_{tag}") for n in (
        "norm_weight_loaded", "sumsq_done", "inv_done", "rstd_done", "h_done", "turned"))
    scope = ExitStack()
    k.scope = scope
    ss = k.sb(f"ss_{tag}", [P, NJ])
    inv = k.sb(f"inv_{tag}", [P, NJ])
    rstd = k.sb(f"rstd_{tag}", [P, NJ])
    turned = k.ps(f"turned_ps_{tag}", [P, 4, W])
    rows = hn if weight is not None else src
    wrow = k.sb(f"norm_row_{tag}", [P, D]) if weight is not None else None
    with scope, nc.Block() as block:
        @block.sync
        def _(sp):
            if weight is not None:
                sp.dma_start(wrow[:], weight.broadcast_to([P, D])).then_inc(s_w, 16)
            if ahead is not None:
                ahead(sp)

        @block.scalar
        def _(act):
            if weight is None:
                if hn is not None:
                    nc.scalar.activation(hn[:], src[:], ACT.Copy)
                return
            for j in range(NJ):
                nc.scalar.activation(hn[:, j, :], src[:, j, :], ACT.Square,
                                     accum_out=ss[:, j:j + 1]).then_inc(s_ss, 1)
            act.wait_ge(s_inv, 1)
            nc.scalar.activation(rstd[:], inv[:], ACT.Sqrt).then_inc(s_rs, 1)

        @block.vector
        def _(dve):
            o = Order(dve, k.order["dve"])
            if weight is not None:
                dve.wait_ge(s_ss, NJ)
                o(nc.vector.tensor_scalar(ss[:], ss[:], 1.0 / D, EPS, ALU.mult, ALU.add))
                nc.vector.reciprocal(inv[:], ss[:]).then_inc(s_inv, 1)
                dve.wait_ge(s_rs, 1)
                refine(nc, o, rstd[:], ss[:], inv[:])
                dve.wait_ge(s_w, 16)
                for j in range(NJ):
                    nc.vector.scalar_tensor_tensor(out=hn[:, j, :], in0=src[:, j, :], scalar=rstd[:, j:j + 1],
                                                   in1=wrow[:], op0=ALU.mult, op1=ALU.mult).then_inc(s_h, 1)
            for b in range(4):
                j, c0 = b // 2, 4 * (b % 2)
                dve.wait_ge(s_t, b + 1)
                dst = k.hT[:, c0:c0 + 4, j * P:(j + 1) * P]
                got = turned[:, b, :].rearrange("p (c t) -> p c t", c=4)
                nc.vector.tensor_copy(dst, got)
            o.restart()

        @block.tensor
        def _(pe):
            for b in range(4):
                j, c0 = b // 2, 4 * (b % 2)
                if weight is not None:
                    pe.wait_ge(s_h, j + 1)
                for c in range(4):
                    last = nc.tensor.transpose(turned[:, b, c * P:(c + 1) * P],
                                               rows[:, j, c0 + c:D:KC], k.table("ident"))
                last.then_inc(s_t, 1)
    k.scope = k.ctx


POOL_N, STORE_N = 24576, KC * D
AT_CONV, AT_LA, AT_QK, AT_FREE = 0, 3 * GDN_H * T, 3 * GDN_H * T + 2 * NJ * W, 3 * GDN_H * T + 2 * NJ * W + 2 * GLA_H * T


def stage_project(k):
    nc, i = k.nc, k.i
    k.qkT = k.carve(k.pool, AT_QK, [P, 2, GLA_H, T])
    k.conv = k.carve(k.pool, AT_CONV, [P, 3 * GDN_H, T])
    k.la = k.carve(k.pool, AT_LA, [P, 2, NJ, W])
    k.nat = k.sb("nat", [P, 5, NJ, 2 * W])
    small = [P, 2, NJ, GDN_H]
    k.g, k.gcum, k.eg, k.et, k.beta, k.beg = (k.sb(n, small) for n in (
        "g", "g_cum", "exp_g_cum", "exp_g_tail", "beta", "beta_exp_g"))
    k.dec = k.sb("chunk_decay", [P, 2, 2, NJ, GDN_H])
    k.mixer_tab = k.sb("mixer_tables", [P, TABLE_N - KEPT_N])
    s_mt = k.sem("mixer_tables_loaded")
    PAD = TAPS // 2
    s_wf = [k.sem(f"w_in_loaded{b}") for b in range(2)]
    (s_ws, s_cw, s_ld, s_pad, s_prod, s_out, s_sm, s_smo, s_z, s_abs, s_log, s_mn, s_spz, s_spl, s_rate, s_be,
     s_g, s_sum, s_td, s_ge, s_conv, s_silu, s_sq, s_np, s_ni, s_ne) = (k.sem(n) for n in (
         "w_small_loaded", "conv_w_loaded", "gate_w_loaded", "pad_zeroed", "block_product", "block_out",
         "small_product", "small_out", "z_product", "z_abs", "z_log", "z_min", "softplus_z", "softplus_log",
         "rate_done", "beta_exp", "g_done", "g_sums", "tail_diff", "g_exps", "conv_done", "conv_silu",
         "squares_done", "norm_product", "norm_inv", "norm_done"))
    scope = ExitStack()
    k.scope = scope
    with scope:
        wbuf = [k.carve(k.pool, AT_FREE + b * KC * W, [P, KC, W]) for b in range(2)]
        wsm = k.sb("w_small", [P, KC, 64])
        cin = k.carve(k.store, 0, [P, 3 * GDN_H, T + 2 * PAD])
        at = AT_FREE + 2 * KC * W
        zabs = k.carve(k.pool, at, [P, 2, NJ, W])
        w2 = k.carve(k.pool, at + 4 * W, [P, 2, W])[0:RANK]
        gb = k.carve(k.store, 3 * GDN_H * (T + 2 * PAD), [P, 2, W])[0:1]
        rows = k.sb("gdn_rows", [P, 2, 2 * GDN_H])
        glrT = k.carve(k.pool, at + 6 * W, [P, 2, T])[0:RANK]
        dab = k.sb("dab", [P, NJ, 4 * GDN_H])
        sp = k.sb("sp", [P, 2] + small[1:])
        cw = k.sb("conv_w", [P, 3 * GDN_H, TAPS])
        sq = k.carve(k.pool, at + 7 * W, [P, 2, T])
        rn = k.carve(k.pool, at + 8 * W, [P, 2 * T])
        pp = k.ps("proj_ps", [P, 2, 2 * W])
        aux = k.ps("aux_ps", [P, 4, W])
        wsrc = i["w_in_blocks"].rearrange("b (p c) n -> b p c n", c=KC)
        nblk = NT_BLOCKS + NN_BLOCKS
        HC = 2 * GDN_H // 2
        with nc.Block() as block:
            @block.sync
            def _(sy):
                sy.dma_start(wsm[:], i["w_in_small"].rearrange("(p c) n -> p c n", c=KC)).then_inc(s_ws, 16)
                for b in range(2):
                    sy.dma_start(wbuf[b][:], wsrc[b]).then_inc(s_wf[b], 16)
                sy.dma_start(k.mixer_tab[:], i["tables"][:, KEPT_N:]).then_inc(s_mt, 16)
                for d, n in enumerate(("fwd", "bwd")):
                    sy.dma_start(w2[:, d, :], i[f"gla_gate_w2_{n}"][0]).then_inc(s_ld, 16)
                    sy.dma_start(gb[:, d, :], i[f"gla_gate_b_{n}"]).then_inc(s_ld, 16)
                    h = slice(d * GDN_H, (d + 1) * GDN_H)
                    sy.dma_start(rows[:, 0, h], i[f"gdn_a_log_{n}"].broadcast_to([P, GDN_H])).then_inc(s_ld, 16)
                    sy.dma_start(rows[:, 1, h], i[f"gdn_dt_bias_{n}"].broadcast_to([P, GDN_H])).then_inc(s_ld, 16)
                sy.dma_start(cw[:], i["conv_w"].rearrange("p (g t) -> p g t", t=TAPS)).then_inc(s_cw, 16)
                with nc.sync.Fori(1, nblk // 2) as it:
                    for b in range(2):
                        sy.wait_ge(s_prod, it * 2 + (b - 1))
                        sy.dma_start(wbuf[b][:], wsrc[it * 2 + b]).then_inc(s_wf[b], 16)

            def turned_block(b):
                for m in range(4):
                    for c in range(KC):
                        last = nc.tensor.matmul(pp[:, b, m * T:(m + 1) * T],
                                                wbuf[b][:, c, m * P:(m + 1) * P], k.hT[:, c, :],
                                                start=(c == 0), stop=(c == KC - 1))
                return last

            def straight_block(b):
                for j in range(NJ):
                    for c in range(KC):
                        last = nc.tensor.matmul(pp[:, b, j * W:(j + 1) * W],
                                                k.hT[:, c, j * P:(j + 1) * P], wbuf[b][:, c, :],
                                                start=(c == 0), stop=(c == KC - 1))
                return last

            @block.tensor
            def _(pe):
                pe.wait_ge(s_ws, 16)
                for d in range(2):
                    for c in range(KC):
                        nc.tensor.matmul(aux[0:RANK, d, 0:T], wsm[:, c, d * RANK:(d + 1) * RANK],
                                         k.hT[:, c, :], start=(c == 0), stop=(c == KC - 1))
                for j in range(NJ):
                    for c in range(KC):
                        last = nc.tensor.matmul(aux[:, 2, j * 32:(j + 1) * 32],
                                                k.hT[:, c, j * P:(j + 1) * P], wsm[:, c, 32:64],
                                                start=(c == 0), stop=(c == KC - 1))
                last.then_inc(s_sm, 1)
                pe.wait_ge(s_wf[0], 16)
                turned_block(0).then_inc(s_prod, 1)
                pe.wait_ge(s_ld, 128)
                pe.wait_ge(s_smo, 2)
                for d in range(2):
                    for j in range(NJ):
                        zb = aux[:, 2 * d + j, :]
                        nc.tensor.matmul(zb, glrT[:, d, j * P:(j + 1) * P], w2[:, d, :], start=True, stop=False)
                        last = nc.tensor.matmul(zb, k.table("ones")[0:1, :], gb[:, d, :], start=False, stop=True)
                last.then_inc(s_z, 1)
                pe.wait_ge(s_wf[1], 16)
                turned_block(1).then_inc(s_prod, 1)
                pe.wait_ge(s_g, 1)
                pe.wait_ge(s_mn, 1)
                pe.wait_ge(s_mt, 16)
                n = NJ * GDN_H
                for d in range(2):
                    nc.tensor.matmul(aux[:, 0, d * n:(d + 1) * n], k.table("cum", d), k.g[:, d], start=True, stop=True)
                nc.tensor.matmul(aux[:, 0, 2 * n:4 * n], k.table("blk"), k.g[:], start=True, stop=True)
                for c in range(2):
                    last = nc.tensor.matmul(aux[:, 0, (4 + 2 * c) * n:(6 + 2 * c) * n],
                                            k.table("half", c), k.g[:], start=True, stop=True)
                last.then_inc(s_sum, 1)
                with nc.tensor.Fori(1, NT_BLOCKS // 2) as it:
                    for b in range(2):
                        pe.wait_ge(s_wf[b], it * 16 + 16)
                        pe.wait_ge(s_out, it * 2 + (b - 1))
                        turned_block(b).then_inc(s_prod, 1)
                with nc.tensor.Fori(NT_BLOCKS // 2, nblk // 2) as it:
                    for b in range(2):
                        pe.wait_ge(s_wf[b], it * 16 + 16)
                        pe.wait_ge(s_out, it * 2 + (b - 1))
                        straight_block(b).then_inc(s_prod, 1)
                        pe.wait_ge(s_sq, it * 2 + (b + 1 - NT_BLOCKS))
                        nc.tensor.matmul(aux[:, 2, :], k.table("ones"), sq[:], start=True, stop=True).then_inc(s_np, 1)

            @block.scalar
            def _(act):
                act.wait_ge(s_sm, 1)
                nc.scalar.activation(glrT[:], aux[0:RANK, 0:2, 0:T], ACT.Copy).then_inc(s_smo, 1)
                nc.scalar.activation(dab[:], aux[:, 2, 0:64].rearrange("p (j n) -> p j n", j=NJ),
                                     ACT.Copy).then_inc(s_smo, 1)
                act.wait_ge(s_prod, 1)
                nc.scalar.activation(k.qkT[:, 0], pp[:, 0, :].rearrange("p (m t) -> p m t", m=4),
                                     ACT.Copy).then_inc(s_out, 1)
                act.wait_ge(s_z, 1)
                nc.scalar.activation(zabs[:], aux[:].rearrange("p (d j) n -> p d j n", d=2), ACT.Abs).then_inc(s_abs, 1)
                act.wait_ge(s_abs, 1)
                nc.scalar.activation(zabs[:], zabs[:], ACT.Exp, scale=-1.0).then_inc(s_abs, 1)
                act.wait_ge(s_spz, 2)
                nc.scalar.activation(sp[:, 1], sp[:, 1], ACT.Exp, scale=-1.0).then_inc(s_abs, 1)
                nc.scalar.activation(rows[:, 0, :], rows[:, 0, :], ACT.Exp).then_inc(s_rate, 1)
                act.wait_ge(s_smo, 2)
                nc.scalar.activation(k.beta[:], dab[:, :, 2 * GDN_H:].rearrange("p j (d h) -> p d j h", d=2),
                                     ACT.Exp, scale=-1.0).then_inc(s_be, 1)
                act.wait_ge(s_abs, 3)
                nc.scalar.activation(sp[:, 1], sp[:, 1], ACT.Ln, bias=1.0).then_inc(s_spl, 1)
                nc.scalar.activation(zabs[:], zabs[:], ACT.Ln, bias=1.0).then_inc(s_log, 1)
                act.wait_ge(s_prod, 2)
                nc.scalar.activation(k.qkT[:, 1], pp[:, 1, :].rearrange("p (m t) -> p m t", m=4),
                                     ACT.Copy).then_inc(s_out, 1)
                act.wait_ge(s_td, 1)
                nc.scalar.activation(k.eg[:], k.gcum[:], ACT.Exp).then_inc(s_ge, 1)
                nc.scalar.activation(k.et[:], k.et[:], ACT.Exp).then_inc(s_ge, 1)
                nc.scalar.activation(k.dec[:], k.dec[:], ACT.Exp).then_inc(s_ge, 1)
                act.wait_ge(s_pad, 2)
                with nc.scalar.Fori(1, NT_BLOCKS // 2) as it:
                    for b in range(2):
                        act.wait_ge(s_prod, it * 2 + (b + 1))
                        nc.scalar.activation(cin[:, bass.ds(it * 8 + (4 * b - 8), 4), PAD:PAD + T],
                                             pp[:, b, :].rearrange("p (m t) -> p m t", m=4),
                                             ACT.Copy).then_inc(s_out, 1)
                act.wait_ge(s_conv, 1)
                nc.scalar.activation(k.conv[:, 0:2 * GDN_H], k.conv[:, 0:2 * GDN_H], ACT.Silu).then_inc(s_silu, 1)
                with nc.scalar.Fori(NT_BLOCKS // 2, nblk // 2) as it:
                    for b in range(2):
                        act.wait_ge(s_prod, it * 2 + (b + 1))
                        nc.scalar.activation(k.nat[:, bass.ds(it - NT_BLOCKS // 2, 1), :, b * W:(b + 1) * W],
                                             pp[:, b, :].rearrange("p (o j n) -> p o j n", o=1, j=NJ),
                                             ACT.Copy).then_inc(s_out, 1)
                        act.wait_ge(s_ni, it * 2 + (b + 1 - NT_BLOCKS))
                        nc.scalar.activation(rn[:], rn[:], ACT.Sqrt).then_inc(s_ne, 1)
                act.wait_ge(s_conv, 2)
                nc.scalar.activation(k.conv[:, 2 * GDN_H:], k.conv[:, 2 * GDN_H:], ACT.Silu)

            @block.vector
            def _(dve):
                o = Order(dve, k.order["dve"])
                nc.vector.memset(cin[:, :, 0:PAD], 0.0).then_inc(s_pad, 1)
                nc.vector.memset(cin[:, :, PAD + T:], 0.0).then_inc(s_pad, 1)
                dve.wait_ge(s_ld, 128)
                dve.wait_ge(s_smo, 2)
                z = dab[:, :, 0:2 * GDN_H].rearrange("p j (d h) -> p d j h", d=2)
                for d in range(2):
                    o(nc.vector.tensor_tensor(sp[:, 0, d], z[:, d],
                                              bc(rows[:, 1, d * GDN_H:(d + 1) * GDN_H], 1, NJ), ALU.add))
                o(nc.vector.tensor_scalar(sp[:, 1], sp[:, 0], -1.0, None, ALU.mult))
                nc.vector.tensor_tensor(sp[:, 1], sp[:, 1], sp[:, 0], ALU.max).then_inc(s_spz, 1)
                dve.wait_ge(s_spz, 1)
                nc.vector.tensor_scalar(sp[:, 0], sp[:, 0], 0.0, None, ALU.max).then_inc(s_spz, 1)
                dve.wait_ge(s_abs, 1)
                nc.vector.tensor_scalar(k.la[:], aux[:].rearrange("p (d j) n -> p d j n", d=2), 0.0, None,
                                        ALU.min).then_inc(s_mn, 1)
                dve.wait_ge(s_spl, 1)
                dve.wait_ge(s_spz, 2)
                o(nc.vector.tensor_tensor(sp[:, 0], sp[:, 0], sp[:, 1], ALU.add))
                dve.wait_ge(s_rate, 1)
                for d in range(2):
                    o(nc.vector.tensor_tensor(k.g[:, d], sp[:, 0, d],
                                              bc(rows[:, 0, d * GDN_H:(d + 1) * GDN_H], 1, NJ), ALU.mult))
                nc.vector.tensor_scalar(k.g[:], k.g[:], -1.0, None, ALU.mult).then_inc(s_g, 1)
                dve.wait_ge(s_be, 1)
                o(nc.vector.tensor_scalar(k.beta[:], k.beta[:], 1.0, None, ALU.add))
                o(nc.vector.reciprocal(k.beta[:], k.beta[:]))
                dve.wait_ge(s_log, 1)
                dve.wait_ge(s_mn, 1)
                o(nc.vector.tensor_tensor(k.la[:], k.la[:], zabs[:], ALU.subtract))
                n = 2 * NJ * GDN_H
                dve.wait_ge(s_sum, 1)
                flat = "p d j h -> p (d j h)"
                o(nc.vector.tensor_copy(k.gcum[:].rearrange(flat), aux[:, 0, 0:n]))
                o(nc.vector.tensor_copy(k.dec[:].rearrange("p c d j h -> p (c d j h)"), aux[:, 0, 2 * n:4 * n]))
                nc.vector.tensor_tensor(k.et[:].rearrange(flat), aux[:, 0, n:2 * n], k.gcum[:].rearrange(flat),
                                        ALU.subtract).then_inc(s_td, 1)
                dve.wait_ge(s_ge, 3)
                o(nc.vector.tensor_tensor(k.beg[:], k.beta[:], k.eg[:], ALU.mult))
                dve.wait_ge(s_pad, 2)
                dve.wait_ge(s_cw, 16)

                def convolve(it):
                    for b in range(2):
                        dve.wait_ge(s_out, it * 2 + (b + 1))
                        for t in range(TAPS):
                            for m in range(4):
                                g = it * 8 + (4 * b - 8 + m)
                                acc = k.conv[:, bass.ds(g, 1), :]
                                seen = cin[:, bass.ds(g, 1), t:t + T]
                                tap = cw[:, bass.ds(g, 1), t]
                                if t == 0:
                                    ins = nc.vector.tensor_scalar(acc, seen, tap, None, ALU.mult)
                                else:
                                    ins = nc.vector.scalar_tensor_tensor(
                                        out=acc, in0=seen, scalar=tap, in1=acc, op0=ALU.mult, op1=ALU.add)
                                o(ins)

                with nc.vector.Fori(1, NT_BLOCKS // 2) as it:
                    o.restart()
                    convolve(it)
                o.restart()
                dve.sem_inc(s_conv, 2)
                dve.wait_ge(s_silu, 1)
                with nc.vector.Fori(0, HC // 2) as it:
                    o.restart()
                    for b in range(2):
                        heads = k.conv[:, bass.ds(it * 4 + 2 * b, 2), :]
                        nc.vector.tensor_tensor(sq[:], heads, heads, ALU.mult).then_inc(s_sq, 1)
                        dve.wait_ge(s_np, it * 2 + (b + 1))
                        o(nc.vector.tensor_scalar(rn[:], aux[:, 2, :], EPS, None, ALU.add))
                        nc.vector.reciprocal(rn[:], rn[:]).then_inc(s_ni, 1)
                        dve.wait_ge(s_ne, it * 2 + (b + 1))
                        o(nc.vector.tensor_tensor(heads, heads, rn[:].rearrange("p (a t) -> p a t", a=2), ALU.mult))
                o.restart()
                dve.sem_inc(s_sq, 2)
                for n in range(2):
                    dve.wait_ge(s_ne, HC + n)
                    dve.sem_inc(s_ni, 1)
    k.scope = k.ctx


def stage_gla(k):
    nc = k.nc
    HP = 2
    NI = GLA_H // HP
    U = 4
    k.oa = k.carve(k.pool, POOL_N - NJ * D, [P, NJ, D])
    k.ob = k.carve(k.pool, POOL_N - 2 * NJ * D, [P, NJ, D])
    A = range(HP)
    mk = lambda n: [k.sem(f"gla_{n}{a}") for a in A]
    (s_stg, s_cum, s_tot, s_exp, s_te, s_dk, s_sc, s_kt, s_at, s_ktn, s_kv, s_st, s_o, s_hd, s_zero, s_v) = (
        mk(n) for n in ("staged", "cum_product", "total_out", "exps_done", "tail_exp", "decayed", "scores",
                        "tail_turned", "scores_masked", "tail_natural", "chunk_kv", "state_done",
                        "out_product", "head_done", "zeroed", "v_staged"))
    s_nw, s_gact = k.sem("attn_norms_loaded"), k.sem("gates_active")
    assert NI == NJ
    scope = ExitStack()
    k.scope = scope
    with scope:
        used = [AT_FREE]
        wa = k.sb("gla_norm", [P, GLA_DV])
        wb = k.sb("gdn_norm", [P, GDN_D])

        def sb(n, sh):
            views = []
            for a in A:
                views.append(k.carve(k.pool, used[0], sh))
                used[0] += int(np.prod(sh[1:]))
            return views

        q, kk = sb("q", [P, T]), sb("k", [P, T])
        la, v = sb("la", [P, U, P]), sb("v", [P, NJ, GLA_DV])
        tot, dec = sb("tot", [P, U, 2]), sb("dec", [P, U, 2])
        ep, en, et = sb("ep", [P, U, P]), sb("en", [P, U, P]), sb("et", [P, U, P])
        at, ktn = sb("at", [P, U, P]), sb("ktn", [P, U, P])
        st = sb("st", [P, 3, 2, GLA_DV])
        B0 = [k.ps(f"gla_cum_ps{a}", [P, U, P]) for a in A]
        B1 = [k.ps(f"gla_sc_ps{a}", [P, U, P]) for a in A]
        BO = [k.ps(f"gla_out_ps{a}", [P, NJ, W]) for a in A]

        def rows(d, n):
            m = n if d == 0 else 3 - n
            return m // 2, m % 2

        with nc.Block() as block:
            @block.sync
            def _(sp):
                sp.dma_start(wa[:], k.i["gla_norm_w"].broadcast_to([P, GLA_DV])).then_inc(s_nw, 16)
                sp.dma_start(wb[:], k.i["gdn_norm_w"].broadcast_to([P, GDN_D])).then_inc(s_nw, 16)

            @block.gpsimd
            def _(pool):
                o = Order(pool, k.order["pool"])
                pool.wait_ge(s_nw, 32)
                with nc.gpsimd.Fori(0, NI) as it:
                    o.restart()
                    tile = bass.ds(it, 1)
                    pool.wait_ge(s_gact, it * 2 + 2)
                    for n, w, hh in ((0, wa, GLA_H), (1, wb, GDN_H)):
                        r = k.nat[:, 1 + n, tile]
                        by_head = r.rearrange("p o (h d) -> p (o h) d", h=hh)
                        o(nc.gpsimd.tensor_tensor(by_head, by_head, bc(w[:], 1, hh), ALU.mult))
                        o(nc.gpsimd.tensor_tensor(r, r, k.nat[:, 3 + n, tile], ALU.mult))
                o.restart()

            @block.scalar
            def _(act):
                with nc.scalar.Fori(0, NI) as it:
                    for a in A:
                        h = it * HP + a
                        nc.scalar.activation(la[a][:], k.la[:, :, :, bass.ds(h * P, P)].rearrange("p d j n -> p (d j) n"),
                                             ACT.Copy, scale=1.0 / TAU).then_inc(s_stg[a], 1)
                        nc.scalar.activation(q[a][:], k.qkT[:, 0, bass.ds(h, 1), :].rearrange("p o t -> p (o t)"), ACT.Copy,
                                             scale=float(GLA_DK) ** -0.5).then_inc(s_stg[a], 1)
                        nc.scalar.activation(kk[a][:], k.qkT[:, 1, bass.ds(h, 1), :].rearrange("p o t -> p (o t)"), ACT.Copy).then_inc(s_stg[a], 1)
                        nc.scalar.activation(v[a][:], k.nat[:, 0, :, bass.ds(h * GLA_DV, GLA_DV)],
                                             ACT.Copy).then_inc(s_v[a], 1)
                    for a in A:
                        act.wait_ge(s_cum[a], it + 1)
                        act.wait_ge(s_tot[a], it * 2 + 2)
                        nc.scalar.activation(ep[a][:], B0[a][:], ACT.Exp).then_inc(s_exp[a], 1)
                        nc.scalar.activation(en[a][:], B0[a][:], ACT.Exp, scale=-1.0).then_inc(s_exp[a], 1)
                        nc.scalar.activation(et[a][:], et[a][:], ACT.Exp).then_inc(s_exp[a], 1)
                        nc.scalar.activation(dec[a][:], tot[a][:], ACT.Exp).then_inc(s_exp[a], 1)
                    for a in A:
                        act.wait_ge(s_kt[a], it + 1)
                        nc.scalar.activation(ktn[a][:], B0[a][:], ACT.Copy).then_inc(s_ktn[a], 1)
                    rz, ab = (k.nat[:, n:n + 2, bass.ds(it, 1)] for n in (1, 3))
                    nc.scalar.activation(rz, rz, ACT.Silu).then_inc(s_gact, 1)
                    nc.scalar.activation(ab, ab, ACT.Sigmoid).then_inc(s_gact, 1)
                    for a in A:
                        act.wait_ge(s_hd[a], it + 1)

            @block.vector
            def _(dve):
                o = Order(dve, k.order["dve"])
                for a in A:
                    nc.vector.memset(at[a][:], 0.0).then_inc(s_zero[a], 1)
                with nc.vector.Fori(0, NI) as it:
                    o.restart()
                    for a in A:
                        dve.wait_ge(s_cum[a], it + 1)
                        o(nc.vector.tensor_copy(tot[a][:, 0:2], B0[a][:, 0:2, CH - 1::CH]))
                        o(nc.vector.tensor_copy(tot[a][:, 2:4], B0[a][:, 2:4, 0::CH]))
                        for d in range(2):
                            nc.vector.tensor_tensor(
                                et[a][:, 2 * d:2 * d + 2].rearrange("p j (c t) -> p (j c) t", c=2),
                                bc(tot[a][:, 2 * d:2 * d + 2].rearrange("p j c -> p (j c)"), 2, CH),
                                B0[a][:, 2 * d:2 * d + 2].rearrange("p j (c t) -> p (j c) t", c=2),
                                ALU.subtract).then_inc(s_tot[a], 1)
                    for a in A:
                        dve.wait_ge(s_exp[a], it * 4 + 4)
                        dve.wait_ge(s_stg[a], it * 3 + 3)
                        for e, x in ((ep, q), (en, kk), (et, kk)):
                            e4 = e[a][:].rearrange("p (d j) t -> p d (j t)", d=2)
                            nc.vector.tensor_tensor(e4, e4, bc(x[a][:], 1, 2), ALU.mult).then_inc(s_dk[a], 1)
                    for a in A:
                        dve.wait_ge(s_zero[a], 1)
                        dve.wait_ge(s_sc[a], it + 1)
                        for d in range(2):
                            nc.vector.copy_predicated(at[a][:, 2 * d:2 * d + 2], bc(k.table("incl", d).bitcast(I32), 1, NJ),
                                                      B1[a][:, 2 * d:2 * d + 2]).then_inc(s_at[a], 1)
                    for n in range(3):
                        for a in A:
                            dve.wait_ge(s_kv[a], it * 3 + (n + 1))
                            kv = B1[a][:].rearrange("p u t -> p (u t)")
                            for d in range(2):
                                j, c = rows(d, n)
                                got = kv[:, d * GLA_DV:(d + 1) * GLA_DV]
                                if n == 0:
                                    ins = nc.vector.tensor_copy(st[a][:, 0, d], got)
                                else:
                                    ins = nc.vector.scalar_tensor_tensor(
                                        out=st[a][:, n, d], in0=st[a][:, n - 1, d],
                                        scalar=dec[a][:, 2 * d + j, c:c + 1], in1=got, op0=ALU.mult, op1=ALU.add)
                                ins.then_inc(s_st[a], 1)
                            dve.wait_ge(s_st[a], it * 6 + (2 * n + 2))
                    for a in A:
                        dve.wait_ge(s_o[a], it + 1)
                        h = it * HP + a
                        nc.vector.tensor_copy(k.oa[:, :, bass.ds(h * GLA_DV, GLA_DV)],
                                              BO[a][:, :, 0:GLA_DV]).then_inc(s_hd[a], 1)
                    for a in A:
                        dve.wait_ge(s_hd[a], it + 1)
                o.restart()

            @block.tensor
            def _(pe):
                po = Order(pe, k.order["pe"])
                with nc.tensor.Fori(0, NI) as it:
                    po.restart()
                    for a in A:
                        pe.wait_ge(s_stg[a], it * 3 + 3)
                        for u in range(U):
                            last = nc.tensor.matmul(B0[a][:, u], la[a][:, u], k.table("cum", u // 2),
                                                    start=True, stop=True)
                        last.then_inc(s_cum[a], 1)
                    for a in A:
                        pe.wait_ge(s_dk[a], it * 3 + 3)
                        for u in range(U):
                            last = nc.tensor.matmul(B1[a][:, u], en[a][:, u], ep[a][:, u], start=True, stop=True)
                        last.then_inc(s_sc[a], 1)
                        for u in range(U):
                            last = nc.tensor.transpose(B0[a][:, u], et[a][:, u], k.table("ident"))
                        last.then_inc(s_kt[a], 1)
                    for a in A:
                        pe.wait_ge(s_v[a], it + 1)
                        pe.wait_ge(s_at[a], it * 2 + 2)
                        for j in range(NJ):
                            for d in range(2):
                                nc.tensor.matmul(BO[a][:, j, 0:GLA_DV], at[a][:, 2 * d + j], v[a][:, j],
                                                 start=(d == 0), stop=True, skip_group_check=True)
                    for n in range(4):
                        for a in A:
                            if n < 3:
                                pe.wait_ge(s_ktn[a], it + 1)
                                if n:
                                    pe.wait_ge(s_st[a], it * 6 + 2 * n)
                                kv = B1[a][:].rearrange("p u t -> p (u t)")
                                for d in range(2):
                                    j, c = rows(d, n)
                                    r = slice(c * CH, (c + 1) * CH)
                                    last = nc.tensor.matmul(kv[:, d * GLA_DV:(d + 1) * GLA_DV],
                                                            ktn[a][r, 2 * d + j], v[a][r, j],
                                                            start=True, stop=True)
                                    if d == 0:
                                        po(last)
                                last.then_inc(s_kv[a], 1)
                            if n:
                                pe.wait_ge(s_st[a], it * 6 + 2 * n)
                                for d in range(2):
                                    j, c = rows(d, n)
                                    r = slice(c * CH, (c + 1) * CH)
                                    last = nc.tensor.matmul(BO[a][r, j, 0:GLA_DV], ep[a][:, 2 * d + j, r],
                                                            st[a][:, n - 1, d], start=False, stop=True,
                                                            skip_group_check=True)
                                if n == 3:
                                    last.then_inc(s_o[a], 1)
                    for a in A:
                        pe.wait_ge(s_hd[a], it + 1)
    k.scope = k.ctx


def stage_gdn(k, ahead=None):
    nc = k.nc
    HP = 2
    NI = GDN_H // HP
    U = 4
    A = range(HP)
    mk = lambda n: [k.sem(f"gdn_{n}{a}") for a in A]
    (s_qk, s_vg, s_p1, s_diff, s_ex, s_sc, s_nb, s_lt, s_lv, s_vs, s_vp, s_zz, s_x, s_uw, s_uws, s_ws, s_vn,
     s_kv, s_s, s_hd, s_xt, s_xs) = (
        mk(n) for n in ("qk_staged", "v_g_staged", "first_products", "diffs_done", "exps_done", "masked",
                        "natural_done", "L_turned", "L_done", "level_masked", "level_product", "update_product",
                        "inverse_done", "uw_product", "uw_out", "ws_product", "v_new_done", "kv_product",
                        "state_done", "head_done", "inverse_turned", "inverse_out"))
    scope = ExitStack()
    k.scope = scope
    with scope:
        used = [AT_LA]

        def sb(n, sh):
            views = []
            for a in A:
                views.append(k.carve(k.pool, used[0], sh))
                used[0] += int(np.prod(sh[1:]))
            return views

        q, kk, v = sb("q", [P, T]), sb("k", [P, T]), sb("v", [P, T])
        gB = sb("gB", [P, 2, NJ, P])
        kbg, ktl, vb = (sb(n, [P, 2, NJ, P]) for n in ("kbg", "ktl", "vb"))
        mx, mn = sb("mx", [P, 2, NJ, P]), sb("mn", [P, 2, NJ, P])
        nL, aT = sb("nL", [P, 2, NJ, P]), sb("aT", [P, 2, NJ, P])
        X, XT, V = (sb(n, [P, 2, NJ, P]) for n in ("X", "XT", "V"))
        us, wT, vn = gB, mx, mn
        S = sb("S", [P, 2, P])
        B = [[k.ps(f"gdn_ps{a}_{b}", [P, 2, NJ, P]) for b in range(4)] for a in A]

        def rows(d, n):
            m = n if d == 0 else 3 - n
            return m // 2, m % 2

        def col(small, h):
            return small[:, :, :, bass.ds(h, 1)].broadcast_to([P, 2, NJ, P])

        def mask(name, n=0):
            return k.table(name, 2 * n, 2 * P).rearrange("p (d t) -> p d t", d=2)

        def masked(eng, out, in0, name, n=0):
            ins = []
            for d in range(2):
                ins.append(eng.tensor_tensor(out[:, d], in0[:, d], bc(mask(name, n)[:, d], 1, NJ), ALU.mult))
            return ins

        with nc.Block() as block:
            @block.sync
            def _(sp):
                if ahead is not None:
                    ahead(sp)

            @block.gpsimd
            def _(pool):
                o = Order(pool, k.order["pool"])
                with nc.gpsimd.Fori(0, NI) as it:
                    o.restart()
                    for a in A:
                        h = it * HP + a
                        flat = lambda x: x.rearrange("p o t -> p (o t)")
                        nc.gpsimd.tensor_copy(kk[a][:], flat(k.conv[:, bass.ds(h + GDN_H, 1), :])).then_inc(s_qk[a], 1)
                        o(nc.gpsimd.tensor_copy(q[a][:], flat(k.conv[:, bass.ds(h, 1), :])))
                        nc.gpsimd.tensor_scalar(q[a][:], q[a][:], float(GDN_D) ** -0.5, None, ALU.mult).then_inc(s_qk[a], 1)
                    for a in A:
                        h = it * HP + a
                        pool.wait_ge(s_ex[a], it * 2 + 2)
                        for ins in masked(nc.gpsimd, mx[a], mx[a], "strictn"):
                            o(ins)
                        nc.gpsimd.tensor_tensor(mx[a][:], mx[a][:], col(k.beta, h), ALU.mult).then_inc(s_sc[a], 1)
                        for ins in masked(nc.gpsimd, mn[a], mn[a], "incl"):
                            ins.then_inc(s_sc[a], 1)
                    for a in A:
                        pool.wait_ge(s_lv[a], it * 2 + 1)
                        for ins in masked(nc.gpsimd, X[a], nL[a], "lev0"):
                            o(ins)
                        nc.gpsimd.tensor_tensor(X[a][:].rearrange("p d j t -> p (d j) t"),
                                                X[a][:].rearrange("p d j t -> p (d j) t"),
                                                bc(k.table("ident"), 1, U), ALU.add).then_inc(s_x[a], 1)
                    for a in A:
                        pool.wait_ge(s_hd[a], it + 1)
                o.restart()

            @block.scalar
            def _(act):
                with nc.scalar.Fori(0, NI) as it:
                    for a in A:
                        h = it * HP + a
                        nc.scalar.activation(v[a][:], k.conv[:, bass.ds(h + 2 * GDN_H, 1), :].rearrange("p o t -> p (o t)"),
                                             ACT.Copy).then_inc(s_vg[a], 1)
                        nc.scalar.activation(gB[a][:], col(k.g, h), ACT.Copy).then_inc(s_vg[a], 1)
                    for a in A:
                        act.wait_ge(s_diff[a], it * 2 + 2)
                        nc.scalar.activation(mx[a][:], mx[a][:], ACT.Exp, scale=-1.0).then_inc(s_ex[a], 1)
                        nc.scalar.activation(mn[a][:], mn[a][:], ACT.Exp).then_inc(s_ex[a], 1)
                    for l in range(2, LEVELS):
                        for a in A:
                            act.wait_ge(s_xt[a], it * (LEVELS - 2) + (l - 1))
                            act.wait_ge(s_zz[a], it * (LEVELS - 1) + (l - 1))
                            nc.scalar.activation(X[a][:], B[a][1][:], ACT.Copy).then_inc(s_xs[a], 1)
                    for a in A:
                        act.wait_ge(s_uw[a], it + 1)
                        nc.scalar.activation(us[a][:], B[a][1][:], ACT.Copy).then_inc(s_uws[a], 1)
                        nc.scalar.activation(wT[a][:], B[a][2][:], ACT.Copy).then_inc(s_uws[a], 1)
                    for a in A:
                        act.wait_ge(s_hd[a], it + 1)

            @block.vector
            def _(dve):
                o = Order(dve, k.order["dve"])
                with nc.vector.Fori(0, NI) as it:
                    o.restart()
                    for a in A:
                        h = it * HP + a
                        dve.wait_ge(s_p1[a], it * 3 + 3)
                        o(nc.vector.tensor_tensor(mx[a][:], B[a][2][:], col(k.gcum, h), ALU.subtract))
                        nc.vector.tensor_scalar(mn[a][:], mx[a][:], 0.0, None, ALU.min).then_inc(s_diff[a], 1)
                        nc.vector.tensor_scalar(mx[a][:], mx[a][:], 0.0, None, ALU.max).then_inc(s_diff[a], 1)
                        tk = B[a][0][:, 0]
                        tv = B[a][0][:, 1]
                        for dst, src, f in ((kbg, tk, k.beg), (ktl, tk, k.et), (vb, tv, k.beta)):
                            nc.vector.tensor_tensor(dst[a][:], bc(src, 1, 2), col(f, h), ALU.mult).then_inc(s_nb[a], 1)
                    for a in A:
                        dve.wait_ge(s_sc[a], it * 3 + 3)
                        nc.vector.tensor_tensor(nL[a][:], bc(B[a][1][:, 0], 1, 2), mx[a][:], ALU.mult).then_inc(s_lv[a], 1)
                        nc.vector.tensor_tensor(aT[a][:], bc(B[a][1][:, 1], 1, 2), mn[a][:], ALU.mult).then_inc(s_lv[a], 1)
                    for a in A:
                        dve.wait_ge(s_lt[a], it + 1)
                        for ins in masked(nc.vector, XT[a], B[a][0], "lev"):
                            o(ins)
                        nc.vector.tensor_tensor(XT[a][:].rearrange("p d j t -> p (d j) t"),
                                                XT[a][:].rearrange("p d j t -> p (d j) t"),
                                                bc(k.table("ident"), 1, U), ALU.add).then_inc(s_x[a], 1)
                    for l in range(1, LEVELS):
                        for a in A:
                            dve.wait_ge(s_vp[a], it * (LEVELS - 1) + l)
                            for ins in masked(nc.vector, V[a], B[a][0], "lev", l):
                                ins.then_inc(s_vs[a], 1)
                        for a in A:
                            dve.wait_ge(s_zz[a], it * (LEVELS - 1) + l)
                            nc.vector.tensor_tensor(XT[a][:], XT[a][:], B[a][2][:], ALU.add).then_inc(s_x[a], 1)
                    for a in A:
                        o(nc.vector.memset(S[a][:], 0.0))
                        dve.sem_inc(s_s[a], 1)
                    for n in range(4):
                        for a in A:
                            if n:
                                dve.wait_ge(s_ws[a], it * 3 + n)
                                for d in range(2):
                                    j, c = rows(d, n)
                                    r = slice(c * CH, (c + 1) * CH)
                                    nc.vector.tensor_tensor(vn[a][r, d, j], us[a][r, d, j], B[a][3][r, 0, d],
                                                            ALU.subtract).then_inc(s_vn[a], 1)
                        for a in A:
                            if n < 3:
                                h = it * HP + a
                                dve.wait_ge(s_kv[a], it * 4 + (n + 1))
                                for d in range(2):
                                    j, c = rows(d, n)
                                    nc.vector.scalar_tensor_tensor(
                                        out=S[a][:, d], in0=S[a][:, d], scalar=k.dec[:, c, d, j, bass.ds(h, 1)],
                                        in1=B[a][3][:, 1, d], op0=ALU.mult, op1=ALU.add).then_inc(s_s[a], 1)
                    for a in A:
                        h = it * HP + a
                        dve.wait_ge(s_kv[a], it * 4 + 4)
                        o(nc.vector.tensor_tensor(V[a][:], B[a][0][:], col(k.eg, h), ALU.mult))
                        o(nc.vector.tensor_tensor(V[a][:], V[a][:], B[a][1][:], ALU.add))
                        nc.vector.tensor_tensor(k.ob[:, :, bass.ds(h * GDN_D, GDN_D)], V[a][:, 0], V[a][:, 1],
                                                ALU.add).then_inc(s_hd[a], 1)
                    for a in A:
                        dve.wait_ge(s_hd[a], it + 1)
                o.restart()

            @block.tensor
            def _(pe):
                def each(a, fn):
                    for d in range(2):
                        for j in range(NJ):
                            last = fn(a, d, j)
                    return last

                mm = nc.tensor.matmul
                po = Order(pe, k.order["pe"])
                with nc.tensor.Fori(0, NI) as it:
                    po.restart()
                    for a in A:
                        pe.wait_ge(s_vg[a], it * 2 + 2)
                        each(a, lambda a, d, j: mm(B[a][2][:, d, j], gB[a][:, d, j], k.table("cum", d),
                                                   start=True, stop=True)).then_inc(s_p1[a], 1)
                        pe.wait_ge(s_qk[a], it * 2 + 2)
                        for x, half in ((kk, 0), (v, 1)):
                            for j in range(NJ):
                                last = nc.tensor.transpose(B[a][0][:, half, j], x[a][:, j * P:(j + 1) * P], k.table("ident"))
                        last.then_inc(s_p1[a], 1)
                        for x, half in ((kk, 0), (q, 1)):
                            for j in range(NJ):
                                t = slice(j * P, (j + 1) * P)
                                last = mm(B[a][1][:, half, j], kk[a][:, t], x[a][:, t], start=True, stop=True)
                        last.then_inc(s_p1[a], 1)
                    for a in A:
                        pe.wait_ge(s_nb[a], it * 3 + 3)
                        pe.wait_ge(s_lv[a], it * 2 + 2)
                        each(a, lambda a, d, j: nc.tensor.transpose(B[a][0][:, d, j], nL[a][:, d, j],
                                                                    k.table("ident"))).then_inc(s_lt[a], 1)
                    per = LEVELS + 1
                    for l in range(1, LEVELS):
                        for a in A:
                            pe.wait_ge(s_x[a], it * per + (l + 1))
                            each(a, lambda a, d, j: mm(B[a][0][:, d, j], nL[a][:, d, j], XT[a][:, d, j],
                                                       start=True, stop=True)).then_inc(s_vp[a], 1)
                            if l > 1:
                                each(a, lambda a, d, j: nc.tensor.transpose(B[a][1][:, d, j], XT[a][:, d, j],
                                                                            k.table("ident"))).then_inc(s_xt[a], 1)
                        for a in A:
                            pe.wait_ge(s_vs[a], it * 2 * (LEVELS - 1) + 2 * l)
                            if l > 1:
                                pe.wait_ge(s_xs[a], it * (LEVELS - 2) + (l - 1))
                            each(a, lambda a, d, j: mm(B[a][2][:, d, j], X[a][:, d, j], V[a][:, d, j],
                                                       start=True, stop=True)).then_inc(s_zz[a], 1)
                    for a in A:
                        pe.wait_ge(s_x[a], it * per + per)
                        each(a, lambda a, d, j: mm(B[a][1][:, d, j], XT[a][:, d, j], vb[a][:, d, j],
                                                   start=True, stop=True))
                        each(a, lambda a, d, j: mm(B[a][2][:, d, j], kbg[a][:, d, j], XT[a][:, d, j],
                                                   start=True, stop=True)).then_inc(s_uw[a], 1)
                    for n in range(4):
                        for a in A:
                            if n == 0:
                                pe.wait_ge(s_uws[a], it * 2 + 2)
                            pe.wait_ge(s_s[a], it * 7 + (2 * n + 1))
                            if n:
                                for d in range(2):
                                    j, c = rows(d, n)
                                    r = slice(c * CH, (c + 1) * CH)
                                    last = mm(B[a][3][r, 0, d], wT[a][:, d, j, r], S[a][:, d], start=True, stop=True)
                                last.then_inc(s_ws[a], 1)
                            for d in range(2):
                                j, c = rows(d, n)
                                r = slice(c * CH, (c + 1) * CH)
                                mm(B[a][0][r, d, j], q[a][:, j * P + c * CH:j * P + (c + 1) * CH], S[a][:, d],
                                   start=True, stop=True)
                        for a in A:
                            new = us[a] if n == 0 else vn[a]
                            if n:
                                pe.wait_ge(s_vn[a], it * 6 + 2 * n)
                            for d in range(2):
                                j, c = rows(d, n)
                                r = slice(c * CH, (c + 1) * CH)
                                mm(B[a][3][:, 1, d], ktl[a][r, d, j], new[r, d, j], start=True, stop=True)
                                last = mm(B[a][1][r, d, j], aT[a][r, d, j, r], new[r, d, j], start=True, stop=True)
                                if d == 0:
                                    po(last)
                            last.then_inc(s_kv[a], 1)
                    for a in A:
                        pe.wait_ge(s_hd[a], it + 1)
    k.scope = k.ctx


def stage_combine(k, ahead=None):
    nc = k.nc
    s_inv, s_rs, s_gate, s_sq = (k.sem(f"comb_{n}") for n in ("inv_done", "rstd_done", "gated", "squares"))
    scope = ExitStack()
    k.scope = scope
    with scope:
        tmp = k.carve(k.pool, POOL_N // 2, [P, 2, NJ, D])
        v = k.sb("comb_var", [P, NJ, GLA_H + GDN_H])
        inv = k.sb("comb_inv", [P, NJ, GLA_H + GDN_H])
        rs = k.sb("comb_rstd", [P, NJ, GLA_H + GDN_H])
        heads = lambda x, n: x.rearrange("p j (h d) -> p j h d", h=n)
        cols = (slice(0, GLA_H), slice(GLA_H, GLA_H + GDN_H))
        with nc.Block() as block:
            @block.sync
            def _(sp):
                if ahead is not None:
                    ahead(sp)

            @block.scalar
            def _(act):
                for j in range(NJ):
                    nc.scalar.activation(tmp[:, 0, j], k.oa[:, j], ACT.Square).then_inc(s_sq, 1)
                for j in range(NJ):
                    nc.scalar.activation(tmp[:, 1, j], k.ob[:, j], ACT.Square).then_inc(s_sq, 1)
                act.wait_ge(s_inv, 1)
                nc.scalar.activation(rs[:], inv[:], ACT.Sqrt).then_inc(s_rs, 1)

            @block.gpsimd
            def _(pool):
                pool.wait_ge(s_sq, NJ)
                nc.gpsimd.tensor_tensor(k.oa[:], k.oa[:], k.nat[:, 1], ALU.mult).then_inc(s_gate, 1)
                pool.wait_ge(s_sq, 2 * NJ)
                nc.gpsimd.tensor_tensor(k.ob[:], k.ob[:], k.nat[:, 2], ALU.mult).then_inc(s_gate, 1)

            @block.vector
            def _(dve):
                o = Order(dve, k.order["dve"])
                for n, hh in ((0, GLA_H), (1, GDN_H)):
                    for j in range(NJ):
                        dve.wait_ge(s_sq, n * NJ + j + 1)
                        o(nc.vector.tensor_reduce(v[:, j, cols[n]], tmp[:, n, j].rearrange("p (h d) -> p h d", h=hh),
                                                  AX.X, ALU.add))
                    o(nc.vector.tensor_scalar(v[:, :, cols[n]], v[:, :, cols[n]], hh / D, EPS, ALU.mult, ALU.add))
                nc.vector.reciprocal(inv[:], v[:]).then_inc(s_inv, 1)
                dve.wait_ge(s_rs, 1)
                refine(nc, o, rs[:], v[:], inv[:])
                for n, x, hh in ((0, k.oa, GLA_H), (1, k.ob, GDN_H)):
                    dve.wait_ge(s_gate, n + 1)
                    o(nc.vector.tensor_tensor(heads(x[:], hh), heads(x[:], hh), bc(rs[:, :, cols[n]], 3, D // hh), ALU.mult))
                o(nc.vector.tensor_tensor(k.oa[:], k.oa[:], k.ob[:], ALU.add))
                o.restart()
    k.scope = k.ctx


def load_out(k, sp, weight):
    w = k.carve(k.store, 0, [P, KC, D])
    for c in range(0, KC, 2):
        sp.dma_start(w[:, c:c + 2, :], weight[:, c:c + 2, :]).then_inc(k.s_out_w, 16)
    k.out_loads += 16 * (KC // 2)


def stage_out(k, tag, alpha):
    nc = k.nc
    s_p = k.sem(f"out_product_{tag}")
    scope = ExitStack()
    k.scope = scope
    with scope:
        w = k.carve(k.store, 0, [P, KC, D])
        y = k.ps(f"out_ps_{tag}", [P, NJ, 2, W])
        with nc.Block() as block:
            @block.tensor
            def _(pe):
                pe.wait_ge(k.s_out_w, k.out_loads)
                for j in range(NJ):
                    for n in range(2):
                        for c in range(KC):
                            last = nc.tensor.matmul(y[:, j, n, :], k.hT[:, c, j * P:(j + 1) * P],
                                                    w[:, c, n * W:(n + 1) * W], start=(c == 0), stop=(c == KC - 1))
                        last.then_inc(s_p, 1)

            @block.vector
            def _(dve):
                for j in range(NJ):
                    for n in range(2):
                        dve.wait_ge(s_p, 2 * j + n + 1)
                        xs = k.x[:, j, n * W:(n + 1) * W]
                        nc.vector.scalar_tensor_tensor(out=xs, in0=xs, scalar=alpha, in1=y[:, j, n, :],
                                                       op0=ALU.mult, op1=ALU.add)
    k.scope = k.ctx


def stage_norm(k, tag, gain, bias=None, ahead=None):
    nc = k.nc
    eps = EPS if bias is None else LN_EPS
    s_ld, s_ss, s_inv, s_rs, s_c, s_sc = (k.sem(f"{n}_{tag}") for n in
                                          ("norm_w_loaded", "sumsq", "inv", "rstd", "centred", "scaled"))
    scope = ExitStack()
    k.scope = scope
    with scope:
        g = k.sb(f"gain_{tag}", [P, D])
        b = k.sb(f"bias_{tag}", [P, D])
        sq = k.hT[:].rearrange("p (j c) t -> p j (c t)", j=NJ)
        mu, v, inv, rs = (k.sb(f"{n}_{tag}", [P, NJ]) for n in ("mu", "var", "inv", "rstd"))
        with nc.Block() as block:
            @block.sync
            def _(sp):
                sp.dma_start(g[:], gain.broadcast_to([P, D])).then_inc(s_ld, 16)
                if bias is not None:
                    sp.dma_start(b[:], bias.broadcast_to([P, D])).then_inc(s_ld, 16)
                if ahead is not None:
                    ahead(sp)

            @block.scalar
            def _(act):
                for j in range(NJ):
                    if bias is not None:
                        act.wait_ge(s_c, j + 1)
                    nc.scalar.activation(sq[:, j], k.x[:, j], ACT.Square, accum_out=v[:, j:j + 1]).then_inc(s_ss, 1)
                act.wait_ge(s_inv, 1)
                nc.scalar.activation(rs[:], inv[:], ACT.Sqrt).then_inc(s_rs, 1)

            @block.gpsimd
            def _(pool):
                if bias is not None:
                    pool.wait_ge(s_sc, 1)
                    nc.gpsimd.tensor_tensor(k.x[:, 0], k.x[:, 0], b[:], ALU.add)

            @block.vector
            def _(dve):
                o = Order(dve, k.order["dve"])
                if bias is not None:
                    for j in range(NJ):
                        o(nc.vector.tensor_reduce(mu[:, j:j + 1], k.x[:, j], AX.X, ALU.add))
                        o(nc.vector.tensor_scalar(mu[:, j:j + 1], mu[:, j:j + 1], 1.0 / D, None, ALU.mult))
                        nc.vector.tensor_scalar(k.x[:, j], k.x[:, j], mu[:, j:j + 1], None,
                                                ALU.subtract).then_inc(s_c, 1)
                dve.wait_ge(s_ss, NJ)
                o(nc.vector.tensor_scalar(v[:], v[:], 1.0 / D, eps, ALU.mult, ALU.add))
                nc.vector.reciprocal(inv[:], v[:]).then_inc(s_inv, 1)
                dve.wait_ge(s_rs, 1)
                refine(nc, o, rs[:], v[:], inv[:])
                dve.wait_ge(s_ld, 16 if bias is None else 32)
                for j in range(NJ):
                    nc.vector.scalar_tensor_tensor(out=k.x[:, j], in0=k.x[:, j], scalar=rs[:, j:j + 1],
                                                   in1=g[:], op0=ALU.mult, op1=ALU.mult).then_inc(s_sc, 1)
                if bias is not None:
                    dve.wait_ge(s_sc, NJ)
                    nc.vector.tensor_tensor(k.x[:, 1], k.x[:, 1], b[:], ALU.add)
                o.restart()
    k.scope = k.ctx


def stage_router(k, tag, w_group, w_fine, b_group=None, b_fine=None, ahead=None):
    nc = k.nc
    NL = NG + NE
    s_ld, s_b, s_p, s_d, s_e, s_sel, s_pos = (k.sem(f"{n}_{tag}") for n in (
        "router_loaded", "router_b_loaded", "logits", "logit_diffs", "logit_exps", "selected", "places"))
    scope = ExitStack()
    k.scope = scope
    with scope:
        w = k.sb(f"router_w_{tag}", [P, KC, NL])
        b = k.sb(f"router_b_{tag}", [P, NL])
        lg = k.sb(f"logits_{tag}", [P, NJ, NL])
        eq = k.sb(f"eq_{tag}", [P, NJ, NL])
        s1 = k.sb(f"sel1_{tag}", [P, NJ, NE])
        m = k.sb(f"max_{tag}", [P, 8, NJ])
        ge = k.sb(f"gexp_{tag}", [P, NJ, NG])
        sel = k.sb(f"sel_{tag}", [P, NJ, NE])
        cnt = k.sb(f"count_{tag}", [P, 2])
        lp = k.ps(f"logit_ps_{tag}", [P, NJ, NL])
        pp = k.ps(f"place_ps_{tag}", [P, NJ + 1, NE])
        rank = k.tab[:, OFF["rank"]:OFF["rank"] + NL]
        with nc.Block() as block:
            @block.sync
            def _(sp):
                sp.dma_start(w[:, :, 0:NG], w_group.rearrange("(p c) n -> p c n", c=KC)).then_inc(s_ld, 16)
                sp.dma_start(w[:, :, NG:], w_fine.rearrange("(p c) n -> p c n", c=KC)).then_inc(s_ld, 16)
                if b_group is not None:
                    sp.dma_start(b[:, 0:NG], b_group.broadcast_to([P, NG])).then_inc(s_b, 16)
                    sp.dma_start(b[:, NG:], b_fine.broadcast_to([P, NE])).then_inc(s_b, 16)
                if ahead is not None:
                    ahead(sp)

            @block.tensor
            def _(pe):
                pe.wait_ge(s_ld, 32)
                for j in range(NJ):
                    for c in range(KC):
                        last = nc.tensor.matmul(lp[:, j, :], k.hT[:, c, j * P:(j + 1) * P], w[:, c, :],
                                                start=(c == 0), stop=(c == KC - 1))
                last.then_inc(s_p, 1)
                pe.wait_ge(s_sel, 1)
                for j in range(NJ + 1):
                    for i in range(min(j + 1, NJ)):
                        t = k.table("before" if i == j else "ones")
                        last = nc.tensor.matmul(pp[:, j], t, sel[:, i], start=(i == 0), stop=(i == min(j, NJ - 1)))
                last.then_inc(s_pos, 1)

            @block.scalar
            def _(act):
                act.wait_ge(s_d, 1)
                nc.scalar.activation(ge[:], ge[:], ACT.Exp).then_inc(s_e, 1)
                act.wait_ge(s_d, 2)
                nc.scalar.activation(m[:, 3], m[:, 3], ACT.Exp).then_inc(s_e, 1)

            @block.vector
            def _(dve):
                o = Order(dve, k.order["dve"])
                tt, ts = nc.vector.tensor_tensor, nc.vector.tensor_scalar

                def first_max(x, n, r, top, sel):
                    o(nc.vector.tensor_reduce(top, x, AX.X, ALU.max))
                    o(tt(sel, x, bc(top, 2, n), ALU.is_equal))
                    o(tt(sel, sel, bc(r, 1, NJ), ALU.mult))
                    o(nc.vector.tensor_reduce(m[:, 7], sel, AX.X, ALU.max))
                    o(tt(sel, sel, bc(m[:, 7], 2, n), ALU.is_equal))

                dve.wait_ge(s_p, 1)
                if b_group is not None:
                    dve.wait_ge(s_b, 32)
                    o(tt(lg[:], lp[:], bc(b[:], 1, NJ), ALU.add))
                else:
                    o(nc.vector.tensor_copy(lg[:], lp[:]))
                grp, fine = lg[:, :, 0:NG], lg[:, :, NG:]
                gs, s2 = eq[:, :, 0:NG], eq[:, :, NG:]
                first_max(grp, NG, rank[:, 0:NG], m[:, 0], gs)
                tt(ge[:], grp, bc(m[:, 0], 2, NG), ALU.subtract).then_inc(s_d, 1)
                o(ts(gs, gs, -1.0, BIG, ALU.add, ALU.mult))
                for j in range(NJ):
                    f = fine[:, j].rearrange("p (g e) -> p g e", g=NG)
                    o(tt(f, f, bc(gs[:, j], 2, EPG), ALU.add))
                first_max(fine, NE, rank[:, NG:], m[:, 1], s1[:])
                o(ts(s2, s1[:], -BIG, None, ALU.mult))
                o(tt(fine, fine, s2, ALU.add))
                first_max(fine, NE, rank[:, NG:], m[:, 2], s2)
                tt(m[:, 3], m[:, 2], m[:, 1], ALU.subtract).then_inc(s_d, 1)
                tt(sel[:], s1[:], s2, ALU.add).then_inc(s_sel, 1)
                o(nc.vector.memset(k.gates[:, :, NE:], 0.0))
                o(nc.vector.memset(k.place[:, :, NE:], -1.0))
                dve.wait_ge(s_e, 1)
                o(nc.vector.tensor_reduce(m[:, 4], ge[:], AX.X, ALU.add))
                dve.wait_ge(s_e, 2)
                o(ts(m[:, 5], m[:, 3], 1.0, None, ALU.add))
                o(tt(m[:, 5], m[:, 5], m[:, 4], ALU.mult))
                o(nc.vector.reciprocal(m[:, 5], m[:, 5]))
                o(tt(m[:, 6], m[:, 5], m[:, 3], ALU.mult))
                o(tt(s1[:], s1[:], bc(m[:, 5], 2, NE), ALU.mult))
                o(tt(s2, s2, bc(m[:, 6], 2, NE), ALU.mult))
                g, pl = k.gates[:, :, 0:NE], k.place[:, :, 0:NE]
                o(tt(g, s1[:], s2, ALU.add))
                dve.wait_ge(s_pos, 1)
                dve.wait_ge(s_sel, 1)
                o(nc.vector.scalar_tensor_tensor(out=pl, in0=pp[:, 0:NJ], scalar=1.0, in1=sel[:],
                                                 op0=ALU.add, op1=ALU.mult))
                o(ts(pl, pl, -1.0, None, ALU.add))
                o(ts(sel[:], pl, float(CAP), None, ALU.is_ge))
                o(tt(k.over[:], sel[:], g, ALU.mult))
                o(nc.vector.tensor_reduce(cnt[:, 0:1], pp[:, NJ], AX.X, ALU.max))
                o(ts(cnt[:, 1:2], cnt[:, 0:1], float(CAP), None, ALU.is_gt))
                o(nc.vector.tensor_copy(k.over_flag[:], cnt[0:1, 1:2]))
                o.restart()
    k.scope = k.ctx


class Experts:

    def __init__(self, k, tag, H, w_gate, w_up, w_down):
        HT = H // P
        self.tag, self.H, self.dram = tag, H, (w_gate, w_up, w_down)
        n = 2 * KC * H
        self.wg = [k.carve(k.pool, 0, [P, 2, KC, H]), None]
        self.wu = [k.carve(k.pool, n, [P, 2, KC, H]), None]
        self.wd = k.carve(k.pool, 2 * n, [P, 2, HT, D])
        self.views = (w_gate.rearrange("e (p c) n -> e p c n", c=KC), w_up.rearrange("e (p c) n -> e p c n", c=KC),
                      w_down.rearrange("e (c p) n -> e p c n", p=P))
        live, k.live = k.live, None
        self.s_lg, self.s_lu = ([k.sem(f"{n}_{tag}{b}") for b in range(2)] for n in ("w_gate_loaded", "w_up_loaded"))
        self.s_ld = k.sem(f"w_down_loaded_{tag}")
        self.s_last = [k.sem(f"last_w_down_loaded_{tag}{n}") for n in range(2)]
        k.live = live

    def load_gate(self, sp, b, expert):
        for e in range(2):
            sp.dma_start(self.wg[b][:, e], self.views[0][expert(e)]).then_inc(self.s_lg[b], 16)

    def load_up(self, sp, b, expert):
        for e in range(2):
            sp.dma_start(self.wu[b][:, e], self.views[1][expert(e)]).then_inc(self.s_lu[b], 16)

    def load_down(self, sp, expert):
        for e in range(2):
            sp.dma_start(self.wd[:, e], self.views[2][expert(e)]).then_inc(self.s_ld, 16)

    def place_last(self):
        flat = lambda x: x.rearrange("p e c n -> p (e c n)")
        rows = lambda x, c: flat(x).rearrange("p (e c n) -> p e c n", e=2, c=c)
        self.wd_last = [rows(self.wg[1], self.H // P), rows(self.wg[0], self.H // P)]
        self.wg_last = rows(self.wd, KC)

    def load_last_down(self, sp, n):
        for e in range(2):
            sp.dma_start(self.wd_last[n][:, e], self.views[2][NE - 4 + 2 * n + e]).then_inc(self.s_last[n], 16)

    def load_last_gate(self, sp):
        for e in range(2):
            sp.dma_start(self.wg_last[:, e], self.views[0][NE - 2 + e]).then_inc(self.s_lg[1], 16)

    def first(self, sp):
        self.load_gate(sp, 0, lambda e: e)
        self.load_up(sp, 0, lambda e: e)
        self.load_down(sp, lambda e: e)

    def second_gate(self, k, sp, region, at):
        self.wg[1] = k.carve(region, at, [P, 2, KC, self.H])
        self.load_gate(sp, 1, lambda e: 2 + e)

    def second_up(self, k, sp, region, at):
        self.wu[1] = k.carve(region, at, [P, 2, KC, self.H])
        self.load_up(sp, 1, lambda e: 2 + e)


def stage_experts(k, ex, alpha, ahead=None):
    stage_packed(k, ex, alpha, ahead)
    full = k.nc.values_load(k.over_flag[0:1, 0:1], min_val=0, max_val=1)
    with k.nc.If(full > 0):
        stage_general(k, ex.tag + "g", ex.H, *ex.dram)
    with k.nc.Else():
        k.nc.all_engine_barrier()


def stage_packed(k, ex, alpha, ahead):
    nc = k.nc
    tag, H = ex.tag, ex.H
    HT = H // P
    NI = NE // 2
    rows = k.h_rows
    s_lg, s_lu, s_ld = ex.s_lg, ex.s_lu, ex.s_ld
    ex.place_last()
    (s_pm, s_gx, s_xg, s_g, s_u, s_sg, s_hid, s_pg, s_pt, s_pgs, s_ht, s_hts, s_y, s_ys,
     s_sc, s_add, s_x, s_yh, s_slot) = (k.sem(f"{n}_{tag}") for n in (
         "onehot_done", "rows_gathered", "gathered_out",
         "gate_product", "up_product", "silu_done", "hidden_done", "gated_onehot_done", "onehot_turned",
         "turned_onehot_out", "hidden_turned", "turned_hidden_out", "y_product", "y_out", "y_scattered",
         "y_added", "x_scaled", "y_high_done",
         "slot_gates_done"))
    scope = ExitStack()
    k.scope = scope
    with scope:
        one = k.sb(f"onehot_{tag}", [P, NJ, 2, CAP])
        gone = k.sb(f"gated_onehot_{tag}", [P, NJ, 2, CAP])
        oneT = k.sb(f"onehot_T_{tag}", [P, T], F32R)
        slot_gate = k.sb(f"slot_gate_{tag}", [P, 1])
        xgT = k.sb(f"gathered_T_{tag}", [P, KC, P])
        hid = k.sb(f"hidden_{tag}", [P, H])
        hidT = k.carve(hid, 0, [P, HT, P])
        yh, yl = (k.sb(f"y_{n}_{tag}", [P, 2, W], F32R) for n in ("high", "low"))
        XG = k.ps(f"gather_ps_{tag}", [P, 2, W])
        SC = k.ps(f"scatter_ps_{tag}", [P, W])
        G = k.ps(f"gate_ps_{tag}", [P, W])
        Up = k.ps(f"up_ps_{tag}", [P, W])
        TP = k.ps(f"turn_ps_{tag}", [P, W])
        Y = k.ps(f"y_ps_{tag}", [P, 2, W])
        scatter_bank = [XG[:, 0], XG[:, 1], SC[:], XG[:, 0]]

        def count(it, b, per, more):
            return it * (2 * per) + (b * per + more)

        with nc.Block() as block:
            @block.sync
            def _(sp):
                with nc.sync.Fori(0, NI // 2 - 2) as it:
                    for b in range(2):
                        sp.wait_ge(s_g, count(it, b, 1, 1))
                        ex.load_gate(sp, b, lambda e: it * 4 + (2 * b + 4 + e))
                        sp.wait_ge(s_u, count(it, b, 1, 1))
                        ex.load_up(sp, b, lambda e: it * 4 + (2 * b + 4 + e))
                        sp.wait_ge(s_y, count(it, b, 2, 2))
                        ex.load_down(sp, lambda e: it * 4 + (2 * b + 2 + e))
                n = NI - 1
                sp.wait_ge(s_g, n - 2)
                ex.load_gate(sp, 0, lambda e: 2 * (n - 1) + e)
                sp.wait_ge(s_u, n - 2)
                ex.load_up(sp, 0, lambda e: 2 * (n - 1) + e)
                sp.wait_ge(s_y, 2 * (n - 2))
                ex.load_down(sp, lambda e: 2 * (n - 2) + e)
                sp.wait_ge(s_g, n - 1)
                ex.load_last_down(sp, 0)
                sp.wait_ge(s_y, 2 * (n - 1))
                ex.load_last_gate(sp)
                sp.wait_ge(s_u, n - 1)
                ex.load_up(sp, 1, lambda e: 2 * n + e)
                sp.wait_ge(s_g, n)
                ex.load_last_down(sp, 1)
                if ahead is not None:
                    sp.wait_ge(s_u, NI)
                    ahead(sp)

            @block.tensor
            def _(pe):
                mm = nc.tensor.matmul

                def gather():
                    for n in range(2):
                        for c in range(4):
                            for j in range(NJ):
                                last = mm(XG[:, n, c * P:(c + 1) * P], rows[:, j, 4 * n + c:D:KC],
                                          one[:, j], start=(j == 0), stop=(j == NJ - 1))
                        last.then_inc(s_gx, 1)

                def both_experts(out, stationary, w, s_done):
                    for c in range(len(w[0])):
                        for e in range(2):
                            last = mm(out[e * CAP:(e + 1) * CAP, 0:w[e][c].shape[-1]],
                                      stationary(c)[:, e * CAP:(e + 1) * CAP], w[e][c],
                                      start=(c == 0), stop=(c == len(w[0]) - 1))
                    last.then_inc(s_done, 1)

                def scatter(first_added):
                    for o in range(4):
                        if o == 3:
                            pe.wait_ge(s_add, first_added)
                        to_tile = oneT[:, (o // 2) * P:(o // 2 + 1) * P]
                        mm(scatter_bank[o], to_tile, yh[:, o % 2], start=True, stop=False)
                        mm(scatter_bank[o], to_tile, yl[:, o % 2], start=False, stop=True).then_inc(s_sc, 1)

                def pair(it, b, gate, down, s_loaded, loads):
                    pe.wait_ge(s_xg, count(it, b, 2, 2))
                    pe.wait_ge(s_lg[b], it * 32 + 32)
                    both_experts(G, lambda c: xgT[:, c], [[gate[:, e, c] for c in range(KC)] for e in range(2)], s_g)
                    pe.wait_ge(s_lu[b], it * 32 + 32)
                    both_experts(Up, lambda c: xgT[:, c], [[ex.wu[b][:, e, c] for c in range(KC)] for e in range(2)], s_u)
                    pe.wait_ge(s_ys, count(it, b, 2, 2))
                    pe.wait_ge(s_pgs, count(it, b, 1, 1))
                    scatter(count(it, b, 4, 1))
                    pe.wait_ge(s_pg, count(it, b, 1, 1))
                    for j in range(NJ):
                        last = nc.tensor.transpose(TP[:, j * P:(j + 1) * P],
                                                   gone[:, j].rearrange("p e s -> p (e s)"), k.table("ident"))
                    last.then_inc(s_pt, 1)
                    pe.wait_ge(s_hid, count(it, b, 1, 1))
                    for m in range(HT):
                        last = nc.tensor.transpose(G[:, m * P:(m + 1) * P], hid[:, m * P:(m + 1) * P],
                                                   k.table("ident"))
                    last.then_inc(s_ht, 1)
                    pe.wait_ge(s_pm, count(it, b, 1, 2))
                    pe.wait_ge(s_add, count(it, b, 4, 4))
                    gather()
                    pe.wait_ge(s_hts, count(it, b, 1, 1))
                    pe.wait_ge(s_loaded, loads)
                    for n in range(2):
                        both_experts(Y[:, n], lambda c: hidT[:, c],
                                     [[down[:, e, c, n * W:(n + 1) * W] for c in range(HT)] for e in range(2)], s_y)

                pe.wait_ge(s_pm, 1)
                gather()
                with nc.tensor.Fori(0, NI // 2 - 1) as it:
                    for b in range(2):
                        pair(it, b, ex.wg[b], ex.wd, s_ld, count(it, b, 32, 32))
                pair(NI // 2 - 1, 0, ex.wg[0], ex.wd_last[0], ex.s_last[0], 32)
                pair(NI // 2 - 1, 1, ex.wg_last, ex.wd_last[1], ex.s_last[1], 32)
                pe.wait_ge(s_ys, 2 * NI + 2)
                pe.wait_ge(s_xg, 2 * NI + 2)
                scatter(4 * NI + 1)

            @block.scalar
            def _(act):
                def gathered(counts):
                    for n in range(2):
                        act.wait_ge(s_gx, counts[n])
                        nc.scalar.activation(xgT[:, 4 * n:4 * n + 4].rearrange("p c s -> p (c s)"), XG[:, n],
                                             ACT.Copy).then_inc(s_xg, 1)

                gathered((1, 2))
                with nc.scalar.Fori(0, NI // 2) as it:
                    for b in range(2):
                        act.wait_ge(s_g, count(it, b, 1, 1))
                        nc.scalar.activation(hid[:], G[:, 0:H], ACT.Silu).then_inc(s_sg, 1)
                        act.wait_ge(s_ht, count(it, b, 1, 1))
                        nc.scalar.activation(hidT[:].rearrange("p c s -> p (c s)"), G[:, 0:HT * P],
                                             ACT.Copy).then_inc(s_hts, 1)
                        gathered([count(it, b, 2, 3 + n) for n in range(2)])
                        act.wait_ge(s_pgs, count(it, b, 1, 2))
                        for n in range(2):
                            act.wait_ge(s_y, count(it, b, 2, n + 1))
                            nc.scalar.activation(yh[:, n], Y[:, n], ACT.Copy, scale=slot_gate[:, 0:1]).then_inc(s_yh, 1)

            @block.vector
            def _(dve):
                slots = bc(bc(k.tab[:, OFF["slot"]:OFF["slot"] + CAP], 1, 2), 1, NJ)

                def add(counts):
                    for o in range(4):
                        dve.wait_ge(s_sc, counts[o])
                        xs = k.x[:, o // 2, (o % 2) * W:(o % 2 + 1) * W]
                        nc.vector.tensor_tensor(xs, xs, scatter_bank[o], ALU.add).then_inc(s_add, 1)

                nc.vector.tensor_tensor(one[:], slots, bc(k.place[:, :, 0:2], 3, CAP), ALU.is_equal).then_inc(s_pm, 1)
                for part in (yh, yl):
                    nc.vector.memset(part[:].bitcast(F32), 0.0).then_inc(s_ys, 1)
                nc.vector.memset(oneT[:].bitcast(F32), 0.0).then_inc(s_pgs, 1)
                dve.wait_ge(s_ys, 2)
                dve.wait_ge(s_pgs, 1)
                nc.vector.tensor_scalar(k.x[:], k.x[:], alpha, None, ALU.mult).then_inc(s_x, 1)
                dve.wait_ge(s_x, 1)
                dve.wait_ge(s_pm, 1)
                nc.vector.tensor_tensor(gone[:], one[:], bc(k.gates[:, :, 0:2], 3, CAP), ALU.mult).then_inc(s_pg, 1)
                with nc.vector.Fori(0, NI // 2) as it:
                    for b in range(2):
                        following = bass.ds(it * 4 + (2 * b + 2), 2)
                        dve.wait_ge(s_gx, count(it, b, 2, 2))
                        dve.wait_ge(s_pg, count(it, b, 1, 1))
                        nc.vector.tensor_tensor(one[:], slots, bc(k.place[:, :, following], 3, CAP),
                                                ALU.is_equal).then_inc(s_pm, 1)
                        dve.wait_ge(s_u, count(it, b, 1, 1))
                        dve.wait_ge(s_sg, count(it, b, 1, 1))
                        nc.vector.tensor_tensor(hid[:], hid[:], Up[:, 0:H], ALU.mult).then_inc(s_hid, 1)
                        add([count(it, b, 4, o + 1) for o in range(4)])
                        dve.wait_ge(s_pt, count(it, b, 1, 1))
                        dve.wait_ge(s_add, count(it, b, 4, 4))
                        nc.vector.tensor_reduce(slot_gate[:], TP[:, 0:T], AX.X, ALU.add).then_inc(s_slot, 1)
                        nc.vector.tensor_scalar(oneT[:], TP[:, 0:T], 0.0, None, ALU.not_equal).then_inc(s_pgs, 1)
                        dve.wait_ge(s_pm, count(it, b, 1, 2))
                        nc.vector.tensor_tensor(gone[:], one[:], bc(k.gates[:, :, following], 3, CAP),
                                                ALU.mult).then_inc(s_pg, 1)
                        dve.wait_ge(s_slot, count(it, b, 1, 1))
                        for n in range(2):
                            dve.wait_ge(s_yh, count(it, b, 2, n + 1))
                            nc.vector.scalar_tensor_tensor(
                                out=yl[:, n], in0=Y[:, n], scalar=slot_gate[:, 0:1], in1=yh[:, n].bitcast(F32),
                                op0=ALU.mult, op1=ALU.subtract).then_inc(s_ys, 1)
                add([4 * NI + o + 1 for o in range(4)])
    k.scope = k.ctx


def stage_general(k, tag, H, w_gate, w_up, w_down):
    nc = k.nc
    HT = H // P
    NP2 = HT // 2
    NI = NE // 2
    s_lg, s_lu, s_ld = ([k.sem(f"{n}_{tag}{b}") for b in range(2)] for n in
                        ("w_gate_loaded", "w_up_loaded", "w_down_loaded"))
    s_g, s_u, s_sg, s_hid, s_dn, s_yp, s_y, s_used = (k.sem(f"{n}_{tag}") for n in (
        "gate_product", "up_product", "silu_done", "hidden_done", "down_used", "down_product", "y_added",
        "up_used"))
    scope = ExitStack()
    k.scope = scope
    with scope:
        wg = [k.carve(k.pool, b * KC * H, [P, KC, H]) for b in range(2)]
        wu = [k.carve(k.pool, (2 + b) * KC * H, [P, KC, H]) for b in range(2)]
        wd = [k.carve(k.pool, (4 + b) * KC * H, [P, HT, D]) for b in range(2)]
        sg = k.sb(f"silu_{tag}", [P, NP2, 2 * T])
        hid = [k.sb(f"hid_{tag}{b}", [P, NP2, 2 * T]) for b in range(2)]
        pg = k.ps(f"gate_ps_{tag}", [P, NP2, 2 * T])
        pu = k.ps(f"up_ps_{tag}", [P, NP2, 2 * T])
        py = k.ps(f"y_ps_{tag}", [P, NJ, 2, W])
        vg = w_gate.rearrange("e (p c) n -> e p c n", c=KC)
        vu = w_up.rearrange("e (p c) n -> e p c n", c=KC)
        vd = w_down.rearrange("e (c p) n -> e p c n", p=P)
        with nc.Block() as block:
            @block.sync
            def _(sp):
                def load(b, e):
                    sp.dma_start(wg[b][:], vg[e]).then_inc(s_lg[b], 16)
                    sp.dma_start(wu[b][:], vu[e]).then_inc(s_lu[b], 16)

                for b in range(2):
                    load(b, b)
                    sp.dma_start(wd[b][:], vd[b]).then_inc(s_ld[b], 16)
                with nc.sync.Fori(1, NI) as it:
                    for b in range(2):
                        sp.wait_ge(s_used, it * 2 + (b - 1))
                        load(b, it * 2 + b)
                        sp.wait_ge(s_dn, it * 2 + (b + 1))
                        sp.dma_start(wd[b][:], vd[it * 2 + b]).then_inc(s_ld[b], 16)

            @block.tensor
            def _(pe):
                pe.sem_inc(s_dn, 2)
                with nc.tensor.Fori(0, NI) as it:
                    for b in range(2):
                        for pr in range(NP2):
                            pe.wait_ge(s_hid, it * (2 * NP2) + (b * NP2 + pr + 1))
                            for w, ps, s_l, s_p in ((wg, pg, s_lg, s_g), (wu, pu, s_lu, s_u)):
                                if pr == 0:
                                    pe.wait_ge(s_l[b], it * 16 + 16)
                                for m in range(2):
                                    for c in range(KC):
                                        n0 = (2 * pr + m) * P
                                        last = nc.tensor.matmul(ps[:, pr, m * T:(m + 1) * T],
                                                                w[b][:, c, n0:n0 + P], k.hT[:, c, :],
                                                                start=(c == 0), stop=(c == KC - 1))
                                last.then_inc(s_p, 1)
                        pe.wait_ge(s_u, it * (2 * NP2) + (b + 1) * NP2)
                        pe.sem_inc(s_used, 1)
                        pe.wait_ge(s_ld[b], it * 16 + 16)
                        pe.wait_ge(s_hid, it * (2 * NP2) + (b + 2) * NP2)
                        for j in range(NJ):
                            for n in range(2):
                                g = 2 * j + n
                                pe.wait_ge(s_y, it * 8 + (4 * b + g + 1))
                                for m in range(HT):
                                    hm = hid[b][:, m // 2, (m % 2) * T + j * P:(m % 2) * T + (j + 1) * P]
                                    last = nc.tensor.matmul(py[:, j, n, :], hm, wd[b][:, m, n * W:(n + 1) * W],
                                                            start=(m == 0), stop=(m == HT - 1))
                                last.then_inc(s_yp, 1)
                        pe.wait_ge(s_yp, it * 8 + (4 * b + 4))
                        pe.sem_inc(s_dn, 1)

            @block.scalar
            def _(act):
                with nc.scalar.Fori(0, NI) as it:
                    for b in range(2):
                        for pr in range(NP2):
                            n = it * (2 * NP2) + (b * NP2 + pr + 1)
                            act.wait_ge(s_hid, n)
                            act.wait_ge(s_g, n)
                            nc.scalar.activation(sg[:, pr], pg[:, pr], ACT.Silu).then_inc(s_sg, 1)

            @block.vector
            def _(dve):
                dve.sem_inc(s_hid, NP2)
                dve.sem_inc(s_y, 4)
                with nc.vector.Fori(0, NI) as it:
                    for b in range(2):
                        dve.wait_ge(s_dn, it * 2 + (b + 1))
                        for pr in range(NP2):
                            n = it * (2 * NP2) + (b * NP2 + pr + 1)
                            dve.wait_ge(s_u, n)
                            dve.wait_ge(s_sg, n)
                            nc.vector.tensor_tensor(hid[b][:, pr], sg[:, pr], pu[:, pr], ALU.mult).then_inc(s_hid, 1)
                        for j in range(NJ):
                            for h in range(2):
                                n = it * 8 + (4 * b + 2 * j + h + 1)
                                dve.wait_ge(s_y, n)
                                dve.wait_ge(s_yp, n)
                                xs = k.x[:, j, h * W:(h + 1) * W]
                                nc.vector.scalar_tensor_tensor(
                                    out=xs, in0=py[:, j, h, :], scalar=k.over[:, j, bass.ds(it * 2 + b, 1)],
                                    in1=xs, op0=ALU.mult, op1=ALU.add).then_inc(s_y, 1)
                dve.wait_ge(s_y, 4 * NE + 4)
    k.scope = k.ctx


def load_even(k, sp):
    sp.dma_start(k.w_even0[:], k.i["w_in_even"].rearrange("(p c) n -> p c n", c=KC)[:, :, 0:W]).then_inc(
        k.s_even0, 16)


def stage_even_project(k):
    nc, i = k.nc, k.i
    N = i["w_in_even"].shape[1]
    k.en = k.sb("even_nat", [P, NJ, N])
    s_w = [k.s_even0] + [k.sem(f"w_even_loaded{b}") for b in (1, 2)]
    s_p, s_o = k.sem("even_product"), k.sem("even_out")
    scope = ExitStack()
    k.scope = scope
    src = i["w_in_even"].rearrange("(p c) n -> p c n", c=KC)
    cuts = [(n, min(W, N - n)) for n in range(0, N, W)]
    with scope:
        w = [k.w_even0] + [k.carve(k.pool, b * KC * W, [P, KC, W]) for b in range(2)]
        ps = k.ps("even_ps", [P, 2, NJ, W])
        with nc.Block() as block:
            @block.sync
            def _(sp):
                for n, (a, width) in enumerate(cuts):
                    if n == 0:
                        continue
                    if n >= 3:
                        sp.wait_ge(s_p, n - 2)
                    sp.dma_start(w[n % 3][:, :, 0:width], src[:, :, a:a + width]).then_inc(s_w[n % 3], 16)

            @block.tensor
            def _(pe):
                for n, (a, width) in enumerate(cuts):
                    pe.wait_ge(s_w[n % 3], 16 * (n // 3 + 1))
                    if n >= 2:
                        pe.wait_ge(s_o, n - 1)
                    for j in range(NJ):
                        for c in range(KC):
                            last = nc.tensor.matmul(ps[:, n % 2, j, 0:width], k.hT[:, c, j * P:(j + 1) * P],
                                                    w[n % 3][:, c, 0:width], start=(c == 0), stop=(c == KC - 1))
                    last.then_inc(s_p, 1)

            @block.scalar
            def _(act):
                for n, (a, width) in enumerate(cuts):
                    act.wait_ge(s_p, n + 1)
                    nc.scalar.activation(k.en[:, :, a:a + width], ps[:, n % 2, :, 0:width], ACT.Copy).then_inc(s_o, 1)
    k.scope = k.ctx


def stage_even_mix(k):
    nc, i = k.nc, k.i
    RD = 128
    k.mix = k.h_rows
    names = ("tables", "rot_a", "rot_b", "rot_c", "rot_d", "rotated", "turned", "turned_out", "lg_abs", "lg_exp",
             "lg_ln", "dist", "dist_exp", "ret_scores", "ret_weighted", "ret_product", "win_scores", "win_masked",
             "win_diff", "win_exp", "p_turned", "p_out", "win_product", "sink_diff", "ret_out", "gn_sq", "gn_inv",
             "gn_rstd", "silu")
    s = {n: k.sem(f"even_{n}") for n in names}
    scope = ExitStack()
    k.scope = scope
    with scope:
        at = [0]

        def room(shape):
            at[0] += int(np.prod(shape[1:]))
            return k.carve(k.pool, at[0] - int(np.prod(shape[1:])), shape)

        lgt = k.sb("ret_logit", [P, 2 * RET_H])
        lga = k.sb("ret_logit_abs", [P, 2 * RET_H])
        sink = k.sb("sink", [P, WIN_H])
        gn = k.sb("ret_gain", [P, W])
        tb = room([P, ROPE_N + 6 * T])
        rot = room([P, NJ, W * 2 + 640])
        ta = room([P, NJ, 8, 64])
        tc_ = room([P, NJ, 8, 64])
        rT = room([P, 8, T])
        wT = room([P, 5, T])
        dm = room([P, RET_H, NJ * T])
        st = room([P, RET_H, NJ, T])
        sc = room([P, WIN_H, NJ, T])
        pT = room([P, WIN_H, NJ, T])
        ya = room([P, NJ, RET_H, RD])
        sq = ta[:].rearrange("p j (h a) d -> p j h (a d)", a=2)
        sm = k.sb("even_small", [P, 10, NJ, WIN_H])
        pb = [k.ps(f"even_ps{b}", [P, W]) for b in range(8)]
        o64 = 2 * 64 * NJ
        cos = {64: tb[:, 0:64 * NJ], 32: tb[:, o64:o64 + 32 * NJ]}
        sin = {64: tb[:, 64 * NJ:o64], 32: tb[:, o64 + 32 * NJ:ROPE_N]}
        ahead, behind = tb[:, ROPE_N:ROPE_N + 2 * T], tb[:, ROPE_N + 2 * T:ROPE_N + 4 * T]
        wmask = tb[:, ROPE_N + 4 * T:]
        groups = [(0, 8, 64, 0, 128), (4 * W, 4, 32, 2 * W, 128), (4 * W + 256, 4, 32, 2 * W + 64, 128),
                  (5 * W, 2, 32, 2 * W + 512, 64)]

        def halves(x, a, n, half, j, step):
            if step == 2 * half:
                v = x[:, j, a:a + n * step].rearrange("p (h s d) -> p h s d", h=n, s=2)
                return v[:, :, 0], v[:, :, 1]
            at = 2 * W + (a - 2 * W) % step
            v = x[:, j, 2 * W:2 * W + n * step].rearrange("p (h s) -> p h s", h=n)
            return v[:, :, at - 2 * W:at - 2 * W + half], v[:, :, at - 2 * W + half:at - 2 * W + 2 * half]

        def angle(t, half, j, n):
            return bc(t[half][:, j * half:(j + 1) * half], 1, n)

        def turn_list():
            out = []
            for h in range(8):
                out.append((h // 2, (h % 2) * 2, lambda j, h=h: rot[:, j, h * RD:(h + 1) * RD]))
            for m in range(4):
                out.append((4 + m // 2, (m % 2) * 2,
                            lambda j, m=m: rot[:, j, 2 * W + m * P:2 * W + (m + 1) * P]))
            out.append((6, 0, lambda j: rot[:, j, 2 * W + 512:2 * W + 640]))
            return out

        with nc.Block() as block:
            @block.sync
            def _(sp):
                sp.dma_start(tb[:], i["even_tables"]).then_inc(s["tables"], 16)
                sp.dma_start(lgt[:], i["ret_decay_logit"].broadcast_to([P, 2 * RET_H])).then_inc(s["tables"], 16)
                sp.dma_start(gn[:], i["ret_gn_gain"].broadcast_to([P, W])).then_inc(s["tables"], 16)
                sp.dma_start(sink[:], i["sink_logit"].broadcast_to([P, WIN_H])).then_inc(s["tables"], 16)

            @block.gpsimd
            def _(pool):
                o = Order(pool, k.order["pool"])
                pool.wait_ge(s["tables"], 64)
                tt = nc.gpsimd.tensor_tensor
                for a, n, half, b, step in groups:
                    for j in range(NJ):
                        x1, x2 = halves(k.en, a, n, half, j, 2 * half)
                        _, y2 = halves(rot, b, n, half, j, step)
                        t1 = tc_[:, j, 0:n, 0:half]
                        o(tt(t1, x1, angle(sin, half, j, n), ALU.mult))
                        o(tt(y2, x2, angle(cos, half, j, n), ALU.mult))
                        o(tt(y2, y2, t1, ALU.add))
                pool.sem_inc(s["rotated"], 1)
                o.restart()

            @block.vector
            def _(dve):
                o = Order(dve, k.order["dve"])
                tt, ts, stt = nc.vector.tensor_tensor, nc.vector.tensor_scalar, nc.vector.scalar_tensor_tensor
                red = nc.vector.tensor_reduce
                dve.wait_ge(s["tables"], 64)
                o(ts(lga[:], lgt[:], -1.0, None, ALU.mult))
                tt(lga[:], lga[:], lgt[:], ALU.max).then_inc(s["lg_abs"], 1)
                for a, n, half, b, step in groups:
                    for j in range(NJ):
                        x1, x2 = halves(k.en, a, n, half, j, 2 * half)
                        y1, _ = halves(rot, b, n, half, j, step)
                        t1 = ta[:, j, 0:n, 0:half]
                        o(tt(t1, x2, angle(sin, half, j, n), ALU.mult))
                        o(tt(y1, x1, angle(cos, half, j, n), ALU.mult))
                        o(tt(y1, y1, t1, ALU.subtract))
                dve.sem_inc(s["rotated"], 1)
                dve.wait_ge(s["lg_ln"], 1)
                o(ts(lgt[:], lgt[:], 0.0, None, ALU.min))
                o(tt(lgt[:], lgt[:], lga[:], ALU.subtract))
                for h in range(RET_H):
                    o(ts(dm[:, h], ahead, lgt[:, h:h + 1], None, ALU.mult))
                    stt(out=dm[:, h], in0=behind, scalar=lgt[:, RET_H + h:RET_H + h + 1], in1=dm[:, h],
                        op0=ALU.mult, op1=ALU.add).then_inc(s["dist"], 1)
                for h in range(RET_H):
                    dve.wait_ge(s["ret_scores"], h + 1)
                    dve.wait_ge(s["dist_exp"], h + 1)
                    tt(st[:, h].rearrange("p a t -> p (a t)"), pb[h][:], dm[:, h], ALU.mult).then_inc(s["ret_weighted"], 1)
                for h in range(WIN_H):
                    dve.wait_ge(s["win_scores"], h + 1)
                    tt(sc[:, h].rearrange("p a t -> p (a t)"), pb[4 + h % 4][:], wmask, ALU.add).then_inc(s["win_masked"], 1)
                dve.wait_ge(s["win_masked"], WIN_H)
                hj = "p a h -> p h a"
                o(red(sm[:, 0].rearrange(hj), sc[:], AX.X, ALU.max))
                o(tt(sm[:, 0], sm[:, 0], bc(sink[:], 1, NJ), ALU.max))
                o(tt(sm[:, 1], bc(sink[:], 1, NJ), sm[:, 0], ALU.subtract))
                for j in range(NJ):
                    tt(sc[:, :, j], sc[:, :, j], bc(sm[:, 0, j], 2, T), ALU.subtract).then_inc(s["win_diff"], 1)
                dve.wait_ge(s["ret_product"], 1)
                yp = pb[0][:].rearrange("p (h d) -> p h d", h=RET_H), pb[1][:].rearrange("p (h d) -> p h d", h=RET_H)
                for j in range(NJ):
                    o(nc.vector.tensor_copy(ya[:, j], yp[j]))
                o(red(sm[:, 2, :, 0:RET_H], ya[:], AX.X, ALU.add))
                o(ts(sm[:, 2, :, 0:RET_H], sm[:, 2, :, 0:RET_H], 1.0 / RD, None, ALU.mult))
                o(tt(ya[:], ya[:], bc(sm[:, 2, :, 0:RET_H], 3, RD), ALU.subtract))
                o(tt(sq[:], ya[:], ya[:], ALU.mult))
                o(red(sm[:, 3, :, 0:RET_H], sq[:], AX.X, ALU.add))
                o(ts(sm[:, 3, :, 0:RET_H], sm[:, 3, :, 0:RET_H], 1.0 / RD, GN_EPS, ALU.mult, ALU.add))
                nc.vector.reciprocal(sm[:, 4, :, 0:RET_H], sm[:, 3, :, 0:RET_H]).then_inc(s["gn_inv"], 1)
                dve.wait_ge(s["gn_rstd"], 1)
                refine(nc, o, sm[:, 5, :, 0:RET_H], sm[:, 3, :, 0:RET_H], sm[:, 4, :, 0:RET_H])
                o(tt(ya[:], ya[:], bc(sm[:, 5, :, 0:RET_H], 3, RD), ALU.mult))
                ma = k.mix[:, :, 0:W]
                o(tt(ma, ya[:].rearrange("p j h d -> p j (h d)"), bc(gn[:], 1, NJ), ALU.mult))
                dve.wait_ge(s["silu"], 1)
                o(tt(ma, ma, k.en[:, :, 3 * W:4 * W], ALU.mult))
                dve.wait_ge(s["win_exp"], 3)
                o(red(sm[:, 6].rearrange(hj), sc[:], AX.X, ALU.add))
                o(tt(sm[:, 6], sm[:, 6], sm[:, 7], ALU.add))
                o(nc.vector.reciprocal(sm[:, 8], sm[:, 6]))
                for h in range(WIN_H):
                    if h % 2:
                        dve.wait_ge(s["p_turned"], h + 1)
                        nc.vector.tensor_copy(pT[:, h].rearrange("p a t -> p (a t)"), pb[h][:]).then_inc(s["p_out"], 1)
                dve.wait_ge(s["win_product"], 1)
                for j in range(NJ):
                    o(tt(k.mix[:, j, W:].rearrange("p (h d) -> p h d", h=WIN_H),
                         pb[6 + j][:].rearrange("p (h d) -> p h d", h=WIN_H), bc(sm[:, 8, j], 2, WIN_D), ALU.mult))
                o.restart()

            @block.scalar
            def _(act):
                act.wait_ge(s["lg_abs"], 1)
                nc.scalar.activation(lga[:], lga[:], ACT.Exp, scale=-1.0).then_inc(s["lg_exp"], 1)
                act.wait_ge(s["lg_exp"], 1)
                nc.scalar.activation(lga[:], lga[:], ACT.Ln, bias=1.0).then_inc(s["lg_ln"], 1)
                for b in range(7):
                    act.wait_ge(s["turned"], b + 1)
                    got = pb[b][:].rearrange("p (h t) -> p h t", h=2)
                    if b < 4:
                        dst, scale = rT[:, 2 * b:2 * b + 2], (1.0 if b < 2 else RD ** -0.5)
                    elif b < 6:
                        dst, scale = wT[:, 2 * (b - 4):2 * (b - 4) + 2], WIN_D ** -0.5
                    else:
                        dst, scale, got = wT[:, 4:5], 1.0, got[:, 0:1]
                    nc.scalar.activation(dst, got, ACT.Copy, scale=scale).then_inc(s["turned_out"], 1)
                for h in range(RET_H):
                    act.wait_ge(s["dist"], h + 1)
                    nc.scalar.activation(dm[:, h], dm[:, h], ACT.Exp).then_inc(s["dist_exp"], 1)
                act.wait_ge(s["win_diff"], 2)
                nc.scalar.activation(sc[:], sc[:], ACT.Exp).then_inc(s["win_exp"], 2)
                nc.scalar.activation(sm[:, 7], sm[:, 1], ACT.Exp).then_inc(s["win_exp"], 1)
                act.wait_ge(s["gn_inv"], 1)
                nc.scalar.activation(sm[:, 5, :, 0:RET_H], sm[:, 4, :, 0:RET_H], ACT.Sqrt).then_inc(s["gn_rstd"], 1)
                nc.scalar.activation(k.en[:, :, 3 * W:4 * W], k.en[:, :, 3 * W:4 * W], ACT.Silu).then_inc(s["silu"], 1)
                for h in range(0, WIN_H, 2):
                    act.wait_ge(s["p_turned"], h + 1)
                    nc.scalar.activation(pT[:, h].rearrange("p a t -> p (a t)"), pb[h][:], ACT.Copy).then_inc(s["p_out"], 1)

            @block.tensor
            def _(pe):
                mm = nc.tensor.matmul
                pe.wait_ge(s["rotated"], 2)
                turns = turn_list()
                for n, (b, place, cols) in enumerate(turns):
                    for j in range(NJ):
                        last = nc.tensor.transpose(pb[b][:, (place + j) * P:(place + j + 1) * P], cols(j), k.table("ident"))
                    if n == len(turns) - 1 or turns[n + 1][0] != b:
                        last.then_inc(s["turned"], 1)
                pe.wait_ge(s["turned_out"], 7)
                for h in range(RET_H):
                    for sj in range(NJ):
                        last = mm(pb[h][:, sj * T:(sj + 1) * T], rT[:, RET_H + h, sj * P:(sj + 1) * P], rT[:, h, :],
                                  start=True, stop=True)
                    last.then_inc(s["ret_scores"], 1)
                for h in range(WIN_H):
                    m, r = h % 4, slice(64 * (h // 4), 64 * (h // 4) + 64)
                    if h >= 4:
                        pe.wait_ge(s["win_masked"], h - 3)
                    for j in range(NJ):
                        last = mm(pb[4 + h % 4][:, j * T:(j + 1) * T], wT[r, m, j * P:(j + 1) * P], wT[r, 4, :],
                                  start=True, stop=True)
                    last.then_inc(s["win_scores"], 1)
                pe.wait_ge(s["ret_weighted"], RET_H)
                for j in range(NJ):
                    for h in range(RET_H):
                        for sj in range(NJ):
                            last = mm(pb[j][:, h * RD:(h + 1) * RD], st[:, h, sj, j * P:(j + 1) * P],
                                      k.en[:, sj, 2 * W + h * RD:2 * W + (h + 1) * RD],
                                      start=(sj == 0), stop=(sj == NJ - 1))
                last.then_inc(s["ret_product"], 1)
                pe.wait_ge(s["win_exp"], 3)
                pe.wait_ge(s["gn_inv"], 1)
                for h in range(WIN_H):
                    for sj in range(NJ):
                        for j in range(NJ):
                            last = nc.tensor.transpose(pb[h][:, sj * T + j * P:sj * T + (j + 1) * P],
                                                       sc[:, h, j, sj * P:(sj + 1) * P], k.table("ident"))
                    last.then_inc(s["p_turned"], 1)
                pe.wait_ge(s["p_out"], WIN_H)
                for j in range(NJ):
                    for h in range(WIN_H):
                        kv = h // 4
                        for sj in range(NJ):
                            last = mm(pb[6 + j][:, h * WIN_D:(h + 1) * WIN_D], pT[:, h, sj, j * P:(j + 1) * P],
                                      k.en[:, sj, 5 * W + 128 + kv * WIN_D:5 * W + 128 + (kv + 1) * WIN_D],
                                      start=(sj == 0), stop=(sj == NJ - 1))
                last.then_inc(s["win_product"], 1)
    k.scope = k.ctx


def stage_fourier(k, ahead):
    nc = k.nc
    s_a, s_ao, s_b = (k.sem(f"dft_{n}") for n in ("rows_product", "rows_out", "columns_product"))
    scope = ExitStack()
    k.scope = scope
    with scope:
        a = k.sb("dft_rows", [P, KC, 2, T])
        ps = [k.ps(f"dft_ps{b}", [P, 2, T]) for b in range(8)]
        with nc.Block() as block:
            @block.sync
            def _(sp):
                ahead(sp)

            @block.tensor
            def _(pe):
                pe.wait_ge(k.s_dft, 16)
                for c in range(KC):
                    for j in range(NJ):
                        last = nc.tensor.matmul(ps[c][:], k.x[:, j, c * P:(c + 1) * P], k.dft[:, j],
                                                start=(j == 0), stop=(j == NJ - 1))
                    last.then_inc(s_a, 1)
                for g in range(KC // 2):
                    pe.wait_ge(s_ao, 4 * (g + 1))
                    for o in range(2):
                        n = 0
                        for f in range(2):
                            for q in range(2):
                                last = nc.tensor.matmul(ps[2 * g + o][:, 0, :], k.dft[:, q, f, o * P:(o + 1) * P],
                                                        a[:, 2 * g + q, f, :], start=(n == 0), stop=(n == 3))
                                n += 1
                        last.then_inc(s_b, 1)

            @block.scalar
            def _(act):
                for c in range(KC):
                    act.wait_ge(s_a, c + 1)
                    nc.scalar.activation(a[:, c, 0], ps[c][:, 0], ACT.Copy).then_inc(s_ao, 1)
                    nc.scalar.activation(a[:, c, 1], ps[c][:, 1], ACT.Copy, scale=-1.0).then_inc(s_ao, 1)
                for c in range(KC):
                    act.wait_ge(s_b, c + 1)
                    nc.scalar.activation(k.hT[:, c, :], ps[c][:, 0], ACT.Copy, scale=1.0 / T)
    k.scope = k.ctx


def stage_store(k):
    s_o = k.sem("stored")
    with k.nc.Block() as block:
        @block.sync
        def _(sp):
            sp.dma_start(k.out.rearrange("a (j p) d -> p (a j) d", p=P), k.x[:]).then_inc(s_o, 16)
            sp.wait_ge(s_o, 16)


def build(nc, ins, out):
    with ExitStack() as ctx:
        k = Core(nc, ins, out, ctx)
        i = ins
        k.s_out_w, k.s_even0, k.s_dft, k.out_loads = (
            k.sem("out_weights_loaded"), k.sem("w_even0_loaded"), k.sem("dft_table_loaded"), 0)
        stage_load(k)
        k.live = []
        k.gates = k.sb("gates", [P, NJ, NE + 2])
        k.place = k.sb("place", [P, NJ, NE + 2])
        k.over = k.sb("over", [P, NJ, NE])
        k.over_flag = k.sb("over_flag", [1, 1], I32)
        ex = [Experts(k, "one", H1, i["moe_w_gate"][0], i["moe_w_up"][0], i["moe_w_down"][0])]
        ex += [Experts(k, f"l{n}", H2, i["expert_w_gate"][n], i["expert_w_up"][n], i["expert_w_down"][n])
               for n in range(2)]
        rows_pc, rows_cp = "(p c) n -> p c n", "(c p) n -> p c n"
        with ExitStack() as mixer:
            outer, k.ctx = k.ctx, mixer
            k.scope = mixer
            stage_norm_t(k, "n1", k.x, i["norm1_w"], k.carve(k.pool, 0, [P, NJ, D]))
            stage_project(k)
            stage_gla(k)
            stage_gdn(k, lambda sp: load_out(k, sp, i["w_out"][0].rearrange(rows_pc, c=KC)))
            stage_combine(k, ex[0].first)
            def second(sp):
                ex[0].second_gate(k, sp, k.pool, POOL_N // 2)
                ex[0].second_up(k, sp, k.pool, POOL_N // 2 + 2 * KC * H1)
            stage_norm_t(k, "mix1", k.oa, None, None, second)
            k.ctx = k.scope = outer
        k.retire()
        stage_out(k, "one", 1.0)
        k.h_rows = k.sb("h_rows", [P, NJ, D])
        stage_norm_t(k, "n2", k.x, i["norm2_w"], k.h_rows)
        stage_router(k, "one", i["moe_w_group"][0], i["moe_w_router"][0],
                     ahead=lambda sp: load_out(k, sp, i["w_out_even"].rearrange(rows_pc, c=KC)))
        with ExitStack() as even:
            outer, k.ctx = k.ctx, even
            k.scope = even
            k.w_even0 = k.sb("w_even0", [P, KC, W])
            stage_experts(k, ex[0], 1.0, lambda sp: load_even(k, sp))
            stage_norm(k, "f", i["norm_f_w"])
            k.retire()
            stage_norm_t(k, "e", k.x, None, None)
            stage_even_project(k)
            stage_even_mix(k)
            stage_norm_t(k, "mix2", k.mix, None, None, ex[1].first)
            k.ctx = k.scope = outer
        k.dft = k.sb("dft_tab", [P, NJ, 2, T])

        def load_fourier(sp):
            sp.dma_start(k.dft[:], i["dft"]).then_inc(k.s_dft, 16)
            load_out(k, sp, i["w_out_fourier"].rearrange(rows_cp, p=P))

        k.gate_room = k.sb("gate_room", [P, 2 * KC * H2])
        for n in range(2):
            if n == 0:
                stage_out(k, "even", ALPHA)
            else:
                k.retire()
                stage_fourier(k, lambda sp: ex[2].second_gate(k, sp, k.gate_room, 0))
                stage_out(k, "fourier", ALPHA)
            stage_norm(k, f"a{n}", i["ln1_gain"][n:n + 1], i["ln1_bias"][n:n + 1],
                       None if n else lambda sp: ex[1].second_gate(k, sp, k.gate_room, 0))
            stage_norm_t(k, f"moe{n}", k.x, None, k.h_rows)
            stage_router(k, f"l{n}", i["router_coarse_w"][n], i["router_fine_w"][n],
                         i["router_coarse_b"][n:n + 1], i["router_fine_b"][n:n + 1],
                         lambda sp: ex[1 + n].second_up(k, sp, k.store, 0))
            stage_experts(k, ex[1 + n], ALPHA, None if n else load_fourier)
            stage_norm(k, f"b{n}", i["ln2_gain"][n:n + 1], i["ln2_bias"][n:n + 1], None if n else ex[2].first)
        stage_store(k)


def lay_out(inputs):
    a = {n: np.ascontiguousarray(v) for n, v in inputs.items()}
    w = a["w_in"][0]
    starts = ([0, 512]
              + [3104 + W * n for n in range(6)]
              + [1024, 1536, 2048, 2560]
              + [6176, 6688] + [7232, 7744, 8256, 8768])
    g = 3 * GDN_H
    return {
        "x": a["x"], "norm1_w": a["norm1_w"], "norm2_w": a["norm2_w"], "tables": tables(),
        "w_in_blocks": np.ascontiguousarray(np.stack([w[:, s:s + W] for s in starts])),
        "w_in_small": np.ascontiguousarray(np.concatenate([w[:, 3072:3104], w[:, 7200:7232]], 1)),
        "conv_w": np.ascontiguousarray(
            a["gdn_conv_w"][0].T.reshape(g, P, TAPS).transpose(1, 0, 2).reshape(P, g * TAPS)),
        **{n: a[n] for n in ("gla_gate_w2_fwd", "gla_gate_w2_bwd", "gla_gate_b_fwd", "gla_gate_b_bwd",
                             "gdn_a_log_fwd", "gdn_a_log_bwd", "gdn_dt_bias_fwd", "gdn_dt_bias_bwd",
                             "gla_norm_w", "gdn_norm_w", "w_out", "moe_w_group", "moe_w_router",
                             "moe_w_gate", "moe_w_up", "moe_w_down")},
        "norm_f_w": a["norm_f_w"].reshape(1, D),
        "w_in_even": a["w_in_even_2"][0], "w_out_even": a["w_out_even_2"][0],
        "w_out_fourier": a["w_out_fourier_2"][0],
        "even_tables": even_tables(), "dft": dft_table(),
        "ret_decay_logit": a["ret_decay_logit_2"].reshape(1, 2 * RET_H),
        "ret_gn_gain": a["ret_gn_gain_2"], "sink_logit": a["sink_logit_2"],
        "router_coarse_w": a["router_coarse_w_2"], "router_coarse_b": a["router_coarse_b_2"],
        "router_fine_w": a["router_fine_w_2"], "router_fine_b": a["router_fine_b_2"],
        "expert_w_gate": a["expert_w_gate_2"], "expert_w_up": a["expert_w_up_2"],
        "expert_w_down": a["expert_w_down_2"],
        "ln1_gain": a["ln1_gain_2"], "ln1_bias": a["ln1_bias_2"],
        "ln2_gain": a["ln2_gain_2"], "ln2_bias": a["ln2_bias_2"],
    }


def kernel(**inputs):
    import concourse.bacc as bacc
    from concourse.bass_utils import run_bass_kernel_spmd

    nc = bacc.Bacc("TRN2", target_bir_lowering=False, num_devices=1)
    arrays, args = {}, {}
    for name, a in lay_out(inputs).items():
        arrays[f"in_{name}"] = a
        args[name] = nc.dram_tensor(f"in_{name}", a.shape, F32, kind="ExternalInput").ap()
    out = nc.dram_tensor("out", (1, T, D), F32, kind="ExternalOutput").ap()
    build(nc, args, out)
    r = run_bass_kernel_spmd(nc, [arrays], core_ids=[0])
    return r.results[0]["out"]
```
